# Optimizing a Trainium2 kernel written in Bass

```python
import math
import jax, jax.numpy as jnp
from jax import lax
import numpy as np

D_MODEL = 1024
BATCH = 1
SEQ = 1024
DEPTH = 1
DEC_BATCH = 8
DEC_SEQ = 16
PAST_LEN = 256

CHUNK = 64
W_A = D_MODEL // 2
DK = 128
DV = 128
H_A = W_A // DK
W_B = D_MODEL // 2
N_BLK_B = 8
BLK_W_B = W_B // N_BLK_B
CONV_W = 4
RG_C = 8.0
MIX_W = W_A + W_B
IN_COLS = 4 * W_A + 2 * W_B
PEER_HEADS = 8
N_SUBKEYS = 128
N_EXPERTS = N_SUBKEYS * N_SUBKEYS
PEER_TOPK = 16
PEER_DQ = 256
PEER_DHALF = PEER_DQ // 2
PEER_BLOCK = 256
PLE_DIM = 256
EPS = 1e-6

kernel_name = "hgrn2_rglru_peer_streaming_step"

def rmsnorm(x, g):
    x32 = x.astype(jnp.float32)
    y = x32 * lax.rsqrt(jnp.mean(x32 * x32, axis=-1, keepdims=True) + EPS)
    return (y * g.astype(jnp.float32)).astype(x.dtype)

def hgrn2_mixer(zq, zf, zi, lb, S0):
    B_, L = zq.shape[0], zq.shape[1]
    C = min(CHUNK, L)
    nC = L // C
    f = lb + (1.0 - lb) * jax.nn.sigmoid(zf.astype(jnp.float32))
    k = 1.0 - f
    logf = jnp.log(f)
    q = jax.nn.silu(zq.astype(jnp.float32))
    v = zi.astype(jnp.float32)

    def to_chunks(a):
        return a.reshape(B_, nC, C, a.shape[2], a.shape[3]).transpose(1, 0, 3, 2, 4)

    mask = jnp.tril(jnp.ones((C, C), dtype=bool))

    def step(S, inp):
        qc, kc, vc, gc = inp
        cum = jnp.cumsum(gc, axis=2)
        qd = qc * jnp.exp(cum)
        kd = kc * jnp.exp(-cum)
        att = jnp.where(mask, jnp.einsum('bhtd,bhsd->bhts', qd, kd), 0.0)
        o = jnp.einsum('bhts,bhsv->bhtv', att, vc) + jnp.einsum('bhtd,bhdv->bhtv', qd, S)
        last = cum[:, :, -1:, :]
        kdec = kc * jnp.exp(last - cum)
        S = jnp.exp(last[:, :, 0, :])[..., None] * S + jnp.einsum('bhsd,bhsv->bhdv', kdec, vc)
        return S, o

    S, o = lax.scan(step, S0.astype(jnp.float32), (to_chunks(q), to_chunks(k), to_chunks(v), to_chunks(logf)))
    o = o.transpose(1, 0, 3, 2, 4).reshape(B_, L, H_A, DV)
    return o, S

def rglru_mixer(xb, gate, conv_buf, h0, conv_w, conv_b, w_a, b_a, w_x, b_x, lam):
    B_, L = xb.shape[0], xb.shape[1]
    xp = jnp.concatenate([conv_buf.astype(xb.dtype), xb], axis=1)
    xc = conv_b + sum(xp[:, j:j + L] * conv_w[j] for j in range(CONV_W))
    new_buf = xp[:, -(CONV_W - 1):]
    xh = xc.reshape(B_, L, N_BLK_B, BLK_W_B)
    r = jax.nn.sigmoid(jnp.einsum('blnc,ncd->blnd', xh, w_a).reshape(B_, L, W_B) + b_a)
    i = jax.nn.sigmoid(jnp.einsum('blnc,ncd->blnd', xh, w_x).reshape(B_, L, W_B) + b_x)
    log_a = -RG_C * r.astype(jnp.float32) * jax.nn.softplus(-lam.astype(jnp.float32))
    a = jnp.exp(log_a)
    b = jnp.sqrt(-jnp.expm1(2.0 * log_a)) * (i * xc).astype(jnp.float32)
    b = b.at[:, 0].add(a[:, 0] * h0.astype(jnp.float32))

    def combine(lhs, rhs):
        a_l, b_l = lhs
        a_r, b_r = rhs
        return a_l * a_r, a_r * b_l + b_r

    _, h = lax.associative_scan(combine, (a, b), axis=1)
    out = h.astype(xb.dtype) * jax.nn.gelu(gate)
    return out, h[:, -1], new_buf

def peer(x, w_q, keys, U, V):
    B_, L, D = x.shape
    T = B_ * L
    blk = min(PEER_BLOCK, T)
    nblk = -(-T // blk)
    pad = nblk * blk - T
    xt = jnp.pad(x.reshape(T, D), ((0, pad), (0, 0))).reshape(nblk, blk, D)
    keys32 = keys.astype(jnp.float32)

    def one(xb):
        q = (xb @ w_q).reshape(blk, PEER_HEADS, 2, PEER_DHALF).astype(jnp.float32)
        s = jnp.einsum('thpc,hpnc->thpn', q, keys32)
        sv, si = lax.top_k(s, PEER_TOPK)
        cand = (sv[:, :, 0, :, None] + sv[:, :, 1, None, :]).reshape(blk, PEER_HEADS, PEER_TOPK * PEER_TOPK)
        cidx = (si[:, :, 0, :, None] * N_SUBKEYS + si[:, :, 1, None, :]).reshape(blk, PEER_HEADS, PEER_TOPK * PEER_TOPK)
        cs, ci = lax.top_k(cand, PEER_TOPK)
        eidx = jnp.take_along_axis(cidx, ci, axis=-1)
        g = jax.nn.softmax(cs, axis=-1)
        u = U[eidx]
        act = jax.nn.gelu(jnp.einsum('thkd,td->thk', u, xb).astype(jnp.float32))
        wgt = (g * act).astype(xb.dtype)
        return jnp.einsum('thk,thkd->td', wgt, V[eidx])

    out = lax.map(one, xt).reshape(nblk * blk, D)[:T]
    return out.reshape(B_, L, D)

def run_layer(h, p_l, S0, h0, buf0, lb, lp):
    B_, L = h.shape[0], h.shape[1]
    u = rmsnorm(h, lp['g_mix'])
    z = u @ lp['w_in']
    zq, zf, zi, zg, zx, zy = jnp.split(z, [W_A, 2 * W_A, 3 * W_A, 4 * W_A, 4 * W_A + W_B], axis=-1)
    oA, S_new = hgrn2_mixer(zq.reshape(B_, L, H_A, DK), zf.reshape(B_, L, H_A, DK),
                            zi.reshape(B_, L, H_A, DV), lb, S0)
    oA = rmsnorm(oA, lp['g_hgrn_norm'].reshape(H_A, DV)).reshape(B_, L, W_A).astype(h.dtype) * jax.nn.silu(zg)
    oB, h_new, buf_new = rglru_mixer(zx, zy, buf0, h0, lp['conv_w'], lp['conv_b'], lp['w_rg_a'], lp['b_rg_a'],
                                     lp['w_rg_x'], lp['b_rg_x'], lp['lambda_rg'])
    h = h + jnp.concatenate([oA, oB], axis=-1) @ lp['w_out']
    h = h + peer(rmsnorm(h, lp['g_ffn']), lp['w_peer_q'], lp['peer_keys'], lp['peer_u'], lp['peer_v'])
    h = h + (p_l @ lp['w_ple']) * jax.nn.sigmoid(rmsnorm(h, lp['g_ple']) @ lp['w_ple_gate'])
    return h, S_new, h_new, buf_new

def setup_inputs(seed: int = 0) -> dict:
    key = jax.random.key(seed)
    ks = jax.random.split(key, 32)

    def nrm(k, shape, s):
        return jax.random.normal(k, shape, jnp.float32) * s

    a0 = jax.random.uniform(ks[13], (DEPTH, W_B), jnp.float32, minval=0.9, maxval=0.999)
    s0 = a0 ** (1.0 / RG_C)
    lam = jnp.log(s0) - jnp.log1p(-s0)
    return {
        "x_prompt": nrm(ks[0], (BATCH, SEQ, D_MODEL), 1.0),
        "x_sample": nrm(ks[1], (DEC_BATCH, DEC_SEQ, D_MODEL), 1.0),
        "state_hgrn": nrm(ks[2], (DEPTH, DEC_BATCH, H_A, DK, DV), 0.5),
        "state_rglru": nrm(ks[3], (DEPTH, DEC_BATCH, W_B), 0.5),
        "state_conv": nrm(ks[4], (DEPTH, DEC_BATCH, CONV_W - 1, W_B), 1.0),
        "p_prompt": nrm(ks[5], (DEPTH, BATCH, SEQ, PLE_DIM), 1.0),
        "p_sample": nrm(ks[6], (DEPTH, DEC_BATCH, DEC_SEQ, PLE_DIM), 1.0),
        "g_mix": 1.0 + nrm(ks[7], (DEPTH, D_MODEL), 0.02),
        "w_in": nrm(ks[8], (DEPTH, D_MODEL, IN_COLS), D_MODEL ** -0.5),
        "lower_bounds": nrm(ks[9], (DEPTH + 1, W_A), 0.1),
        "g_hgrn_norm": 1.0 + nrm(ks[10], (DEPTH, W_A), 0.02),
        "conv_w": nrm(ks[11], (DEPTH, CONV_W, W_B), CONV_W ** -0.5),
        "conv_b": nrm(ks[12], (DEPTH, W_B), 0.01),
        "w_rg_a": nrm(ks[14], (DEPTH, N_BLK_B, BLK_W_B, BLK_W_B), BLK_W_B ** -0.5),
        "b_rg_a": nrm(ks[15], (DEPTH, W_B), 0.01),
        "w_rg_x": nrm(ks[16], (DEPTH, N_BLK_B, BLK_W_B, BLK_W_B), BLK_W_B ** -0.5),
        "b_rg_x": nrm(ks[17], (DEPTH, W_B), 0.01),
        "lambda_rg": lam,
        "w_out": nrm(ks[18], (DEPTH, MIX_W, D_MODEL), MIX_W ** -0.5),
        "g_ffn": 1.0 + nrm(ks[19], (DEPTH, D_MODEL), 0.02),
        "w_peer_q": nrm(ks[20], (DEPTH, D_MODEL, PEER_HEADS * PEER_DQ), D_MODEL ** -0.5),
        "peer_keys": nrm(ks[21], (DEPTH, PEER_HEADS, 2, N_SUBKEYS, PEER_DHALF), PEER_DHALF ** -0.5),
        "peer_u": nrm(ks[22], (DEPTH, N_EXPERTS, D_MODEL), D_MODEL ** -0.5),
        "peer_v": nrm(ks[23], (DEPTH, N_EXPERTS, D_MODEL), PEER_HEADS ** -0.5),
        "g_ple": 1.0 + nrm(ks[24], (DEPTH, D_MODEL), 0.02),
        "w_ple_gate": nrm(ks[25], (DEPTH, D_MODEL, D_MODEL), D_MODEL ** -0.5),
        "w_ple": nrm(ks[26], (DEPTH, PLE_DIM, D_MODEL), PLE_DIM ** -0.5),
        "g_final": 1.0 + nrm(ks[27], (D_MODEL,), 0.02),
    }

def reference(x_prompt, x_sample, state_hgrn, state_rglru, state_conv, p_prompt, p_sample,
              g_mix, w_in, lower_bounds, g_hgrn_norm, conv_w, conv_b, w_rg_a, b_rg_a, w_rg_x, b_rg_x,
              lambda_rg, w_out, g_ffn, w_peer_q, peer_keys, peer_u, peer_v, g_ple, w_ple_gate, w_ple, g_final):
    lb_all = jnp.cumsum(jax.nn.softmax(lower_bounds.astype(jnp.float32), axis=0), axis=0)

    h_p = x_prompt
    h_s = x_sample
    hg_p, rg_p, cv_p, hg_s, rg_s, cv_s = [], [], [], [], [], []
    for l in range(DEPTH):
        lp = dict(g_mix=g_mix[l], w_in=w_in[l], g_hgrn_norm=g_hgrn_norm[l], conv_w=conv_w[l], conv_b=conv_b[l],
                  w_rg_a=w_rg_a[l], b_rg_a=b_rg_a[l], w_rg_x=w_rg_x[l], b_rg_x=b_rg_x[l], lambda_rg=lambda_rg[l],
                  w_out=w_out[l], g_ffn=g_ffn[l], w_peer_q=w_peer_q[l], peer_keys=peer_keys[l],
                  peer_u=peer_u[l], peer_v=peer_v[l], g_ple=g_ple[l], w_ple_gate=w_ple_gate[l], w_ple=w_ple[l])
        lb = lb_all[l].reshape(H_A, DK)
        Bp = h_p.shape[0]
        h_p, S1, r1, c1 = run_layer(h_p, p_prompt[l], jnp.zeros((Bp, H_A, DK, DV), jnp.float32),
                                    jnp.zeros((Bp, W_B), jnp.float32),
                                    jnp.zeros((Bp, CONV_W - 1, W_B), h_p.dtype), lb, lp)
        h_s, S2, r2, c2 = run_layer(h_s, p_sample[l], state_hgrn[l], state_rglru[l], state_conv[l], lb, lp)
        hg_p.append(S1); rg_p.append(r1); cv_p.append(c1)
        hg_s.append(S2); rg_s.append(r2); cv_s.append(c2)

    y_prompt = rmsnorm(h_p, g_final)
    y_sample = rmsnorm(h_s, g_final)
    new_hgrn_prompt = jnp.stack(hg_p, axis=0)
    new_rglru_prompt = jnp.stack(rg_p, axis=0)
    new_conv_prompt = jnp.stack(cv_p, axis=0)
    new_hgrn_sample = jnp.stack(hg_s, axis=0)
    new_rglru_sample = jnp.stack(rg_s, axis=0)
    new_conv_sample = jnp.stack(cv_s, axis=0)
    return (y_prompt, y_sample, new_hgrn_prompt, new_rglru_prompt, new_conv_prompt,
            new_hgrn_sample, new_rglru_sample, new_conv_sample)


_drawn_inputs = setup_inputs


def setup_inputs(seed=0):
    import zlib

    import numpy as np

    out = dict(_drawn_inputs(seed))
    spreads = {}
    factors = {'g_hgrn_norm': 3.636,
     'b_rg_a': 22.591,
     'b_rg_x': 8.0,
     'g_ple': 200.0,
     'g_final': 30.2,
     'g_ffn': 3.744}
    for name, (base, spread) in spreads.items():
        noise = np.random.default_rng([zlib.crc32(name.encode()), seed]).standard_normal(out[name].shape)
        drawn = base * np.exp(spread * noise) if base else spread * noise
        out[name] = __import__('jax').numpy.asarray(drawn.astype(out[name].dtype))
    for name, factor in factors.items():
        out[name] = (out[name] * factor).astype(out[name].dtype)
    return out
```

```python
import numpy as np
from contextlib import ExitStack

import concourse.bass as bass
from concourse import mybir

F32 = mybir.dt.float32
F32R = mybir.dt.float32r
U32 = mybir.dt.uint32
I32 = mybir.dt.int32
ALU = mybir.AluOpType
ACT = mybir.ActivationFunctionType
AX = mybir.AxisListType

D = 1024
KC = D // 128
SEQ, DB, DS = 1024, 8, 16
T = SEQ + DB * DS
NT = T // 128
NPT = SEQ // 128
CH = 64
NCH = SEQ // CH
HA = 4
HP = 16
PH = 8
K = 16
NK = 128
NN, NW = 3, T // 3
EPS = 1e-6
LOWEST = -3.0e38


class Order:

    def __init__(self, eng, sem, per=None, i=0):
        self.eng, self.sem, self.per, self.i, self.n = eng, sem, per, i, 0

    def did(self, ins):
        ins.then_inc(self.sem, 1)
        self.n += 1
        return self.value()

    def value(self):
        return self.n if self.per is None else self.i * self.per + self.n

    def settle(self):
        self.eng.wait_ge(self.sem, self.value())

    def close(self):
        assert self.per is None or self.n == self.per, (self.n, self.per)


class Program:

    def __init__(self, nc, a, out, ctx):
        self.nc, self.a, self.out, self.ctx = nc, a, out, ctx
        self.h = ctx.enter_context(nc.sbuf_tensor("h", [128, NT, D], F32))
        self.ident = ctx.enter_context(nc.sbuf_tensor("ident", [128, 128], F32))
        self.apart = None


def wait_apart(e, P, sem, value):
    e.wait_ge(sem, value)
    e.sem_inc(P.apart, 1)


def token_rows(x_prompt, x_sample):
    return x_prompt[0].rearrange("(t p) d -> p t d", p=128), x_sample.rearrange("b s d -> (b s) d")


def column(vec, first, n=128):
    return vec[first:first + n].rearrange("(p a) -> p a", a=1)


def load_and_constants(P):
    nc, a = P.nc, P.a
    loaded, zeroed, made = (P.ctx.enter_context(nc.semaphore(x)) for x in ("h_loaded", "ident_zeroed", "ident_made"))
    P.apart = P.ctx.enter_context(nc.semaphore("apart"))
    with nc.Block() as block:
        @block.sync
        def _(e):
            rows_p, rows_s = token_rows(a["x_prompt"], a["x_sample"])
            e.dma_start(P.h[:, 0:NPT, :], rows_p).then_inc(loaded, 16)
            e.dma_start(P.h[:, NPT, :], rows_s).then_inc(loaded, 16)
            e.wait_ge(loaded, 32)

        @block.gpsimd
        def _(e):
            nc.gpsimd.memset(P.ident[:], 0.0).then_inc(zeroed, 1)
            e.wait_ge(zeroed, 1)
            nc.gpsimd.affine_select(out=P.ident[:], in_=P.ident[:], compare_op=ALU.not_equal, fill=1.0,
                                    base=0, pattern=[[-1, 128]], channel_multiplier=1).then_inc(made, 1)


def norm_transpose(P, name, gain, xhi, xlo):
    nc = P.nc
    with ExitStack() as ctx:
        sb = lambda n, s, d=F32: ctx.enter_context(nc.sbuf_tensor(f"{name}_{n}", s, d))
        gbc = sb("gain", [128, D])
        junk = sb("squares", [128, 2, D])
        stat = sb("stat", [128, NT])
        rstd = sb("rstd", [128, NT])
        un = sb("normed", [128, 3, D])
        pt = ctx.enter_context(nc.psum_tensor(f"{name}_pt", [128, 3, KC, 128], F32))
        s = lambda n: ctx.enter_context(nc.semaphore(f"{name}_{n}"))
        gain_in, squared, mean_ready, rooted, rstd_ready = map(s, ("gain_in", "squared", "mean", "rooted", "rstd"))
        normed, transposed, hi_done, lo_done = map(s, ("normed", "transposed", "hi", "lo"))
        with nc.Block() as block:
            @block.sync
            def _(e):
                e.dma_start(gbc[:], gain.rearrange("(a n) -> a n", a=1).broadcast_to([128, D])).then_inc(gain_in, 16)

            @block.scalar
            def _(e):
                for t in range(NT):
                    if t >= 2:
                        e.wait_ge(squared, t - 1)
                    nc.scalar.activation(junk[:, t % 2], P.h[:, t], ACT.Square,
                                         accum_out=stat[:, t:t + 1]).then_inc(squared, 1)
                e.wait_ge(mean_ready, 1)
                nc.scalar.activation(rstd[:], stat[:], ACT.Sqrt).then_inc(rooted, 1)
                with e.Fori(0, NT // 3) as i:
                    for u in range(3):
                        e.wait_ge(transposed, i * 3 + u + 1)
                        nc.scalar.activation(xhi[:, :, bass.ds((i * 3 + u) * 128, 128)], pt[:, u],
                                             ACT.Copy).then_inc(hi_done, 1)

            @block.vector
            def _(e):
                e.wait_ge(squared, NT)
                nc.vector.tensor_scalar(stat[:], stat[:], 1.0 / D, EPS, ALU.mult, ALU.add).then_inc(mean_ready, 1)
                e.wait_ge(rooted, 1)
                nc.vector.reciprocal(rstd[:], rstd[:]).then_inc(rstd_ready, 1)
                e.wait_ge(rstd_ready, 1)
                e.wait_ge(gain_in, 16)
                nc.vector.sem_inc(lo_done, 3)
                with e.Fori(0, NT // 3) as i:
                    for u in range(3):
                        e.wait_ge(lo_done, i * 3 + u + 1)
                        nc.vector.scalar_tensor_tensor(
                            out=un[:, u], in0=P.h[:, bass.ds(i * 3 + u, 1), :].rearrange("p a d -> p (a d)"),
                            scalar=rstd[:, bass.ds(i * 3 + u, 1)], in1=gbc[:],
                            op0=ALU.mult, op1=ALU.mult).then_inc(normed, 1)
                    for u in range(3):
                        e.wait_ge(hi_done, i * 3 + u + 1)
                        cols = bass.ds((i * 3 + u) * 128, 128)
                        nc.vector.tensor_tensor(xlo[:, :, cols], pt[:, u], xhi[:, :, cols].bitcast(F32),
                                                ALU.subtract).then_inc(lo_done, 1)

            @block.tensor
            def _(e):
                with e.Fori(0, NT // 3) as i:
                    for u in range(3):
                        e.wait_ge(normed, i * 3 + u + 1)
                        e.wait_ge(lo_done, i * 3 + u + 1)
                        for k in range(KC):
                            last = nc.tensor.transpose(pt[:, u, k], un[:, u, k * 128:(k + 1) * 128], P.ident[:])
                        last.then_inc(transposed, 1)


def three_passes(nc, out, w, x, first, last):
    nc.tensor.matmul(out, w[0], x[0], start=first, stop=False)
    nc.tensor.matmul(out, w[0], x[1], start=False, stop=False)
    return nc.tensor.matmul(out, w[1], x[0], start=False, stop=last)


def project_inputs(P, xhi, xlo, z_dram):
    nc = P.nc
    NB = P.a["w_in"].shape[2] // 128
    w_v = P.a["w_in"][0].rearrange("(k p) c -> p k c", p=128)
    with ExitStack() as ctx:
        raw = ctx.enter_context(nc.sbuf_tensor("win_raw", [128, 2, KC, 128], F32))
        whi = ctx.enter_context(nc.sbuf_tensor("win_hi", [128, 2, KC, 128], F32R))
        wlo = ctx.enter_context(nc.sbuf_tensor("win_lo", [128, 2, KC, 128], F32R))
        zst = ctx.enter_context(nc.sbuf_tensor("z_stage", [128, 2, T], F32))
        pz = ctx.enter_context(nc.psum_tensor("pz", [128, NN, 512], F32))
        s = lambda n: ctx.enter_context(nc.semaphore(n))
        w_in = [s(f"win_in{u}") for u in range(2)]
        z_out = [s(f"z_out{u}") for u in range(2)]
        hi_done, lo_done, mm_done, z_ready = map(s, ("win_hi_done", "win_lo_done", "z_summed", "z_ready"))
        with nc.Block() as block:
            @block.sync
            def _(e):
                nc.sync.sem_inc(z_out[0], 16)
                nc.sync.sem_inc(z_out[1], 16)

                def load(i, u):
                    e.wait_ge(lo_done, i * 2 + u + 1)
                    e.dma_start(raw[:, u], w_v[:, :, bass.ds((i * 2 + u) * 128, 128)]).then_inc(w_in[u], 16)

                def store(i, u):
                    e.wait_ge(z_ready, (i * 2 + u + 2) * NN)
                    e.dma_start(z_dram[bass.ds(i * 2 + u, 1)].rearrange("a p t -> p (a t)"),
                                zst[:, u]).then_inc(z_out[u], 16)

                load(0, 0)
                load(0, 1)
                with e.Fori(0, NB // 2 - 1) as i:
                    load(i + 1, 0)
                    store(i, 0)
                    load(i + 1, 1)
                    store(i, 1)
                store(NB // 2 - 1, 0)
                store(NB // 2 - 1, 1)
                e.wait_ge(z_out[0], (NB // 2 + 1) * 16)
                e.wait_ge(z_out[1], (NB // 2 + 1) * 16)

            @block.scalar
            def _(e):
                nc.scalar.sem_inc(z_ready, NN)

                def hi(i, u):
                    e.wait_ge(w_in[u], (i + 1) * 16)
                    e.wait_ge(mm_done, (i * 2 + u + 1) * NN)
                    nc.scalar.activation(whi[:, u], raw[:, u], ACT.Copy).then_inc(hi_done, 1)

                def evacuate(i, u):
                    e.wait_ge(z_out[u], (i + 1) * 16)
                    for n in range(NN):
                        e.wait_ge(mm_done, (i * 2 + u + 2) * NN + n + 1)
                        nc.scalar.activation(zst[:, u, n * NW:(n + 1) * NW], pz[:, n, 0:NW],
                                             ACT.Copy).then_inc(z_ready, 1)

                hi(0, 0)
                with e.Fori(0, NB // 2 - 1) as i:
                    hi(i, 1)
                    evacuate(i, 0)
                    hi(i + 1, 0)
                    evacuate(i, 1)
                last = NB // 2 - 1
                hi(last, 1)
                evacuate(last, 0)
                evacuate(last, 1)

            @block.vector
            def _(e):
                nc.vector.sem_inc(lo_done, 2)
                with e.Fori(0, NB // 2) as i:
                    for u in range(2):
                        e.wait_ge(hi_done, i * 2 + u + 1)
                        nc.vector.tensor_tensor(wlo[:, u], raw[:, u], whi[:, u].bitcast(F32),
                                                ALU.subtract).then_inc(lo_done, 1)

            @block.tensor
            def _(e):
                nc.tensor.sem_inc(mm_done, 2 * NN)
                with e.Fori(0, NB // 2) as i:
                    for u in range(2):
                        e.wait_ge(lo_done, i * 2 + u + 3)
                        for n in range(NN):
                            e.wait_ge(z_ready, (i * 2 + u) * NN + n + 1)
                            for k in range(KC):
                                mm = three_passes(nc, pz[:, n, 0:NW], (whi[:, u, k], wlo[:, u, k]),
                                                  (xhi[:, k, n * NW:(n + 1) * NW], xlo[:, k, n * NW:(n + 1) * NW]),
                                                  k == 0, k == KC - 1)
                            mm.then_inc(mm_done, 1)


def mixers(P, z_dram, cat):
    nc, a, out = P.nc, P.a, P.out
    with ExitStack() as ctx:
        def sb(n, shape, d=F32):
            return ctx.enter_context(nc.sbuf_tensor(f"mx_{n}", shape, d))
        used = []

        def s(n):
            used.append(nc.alloc_semaphore(f"mx_{n}"))
            return used[-1]


        zq, zf, zv, zg, zy = (sb(n, [128, T]) for n in ("zq", "zf", "zv", "zg", "zy"))
        xp = sb("xp", [128, SEQ + 3])
        xs = sb("xs", [128, DB, DS + 3])
        sf, sq, cum, e1, e2, e3, xc, r, ig = (sb(n, [128, T]) for n in (
            "sf", "sq", "cum", "e1", "e2", "e3", "xc", "r", "ig"))
        scan_mask = sb("scan_mask", [128, T])
        vtok, kdtok, att, on = (sb(n, [128, NT, 128]) for n in ("vtok", "kdtok", "att", "on"))
        states = sb("states", [128, NCH + 1, 128])
        s0 = sb("s0", [128, DB, 128])
        snew = sb("snew", [128, DB, 128])
        vmask = sb("vmask", [128, DB, 128])
        qdz = sb("qdz", [128, DB * (128 + DS)])
        wg = sb("wg", [128, 2, 128])
        rows_in = sb("rows_in", [128, 128])
        cols_out = sb("cols_out", [128, 128])
        rows_out = sb("rows_out", [36, 128])
        mask_p = sb("mask_p", [128, 128])
        mask_s = sb("mask_s", [128, 128])
        bmask = sb("bmask", [128, DB])
        rs = sb("rs", [128, NT])
        NPAR = 12
        LB, LB1, GN, CB, BA, BX, SP8, NSP8 = range(8)
        CW = 8
        par = sb("par", [128, 4, NPAR])
        cur = sb("cur", [128, NPAR])
        lbraw = sb("lbraw", [128, 2, 4])
        tmp = sb("tmp", [128, 6, 4])
        gps = ctx.enter_context(nc.psum_tensor("mx_ps", [128, 8, 512], F32))
        flat = gps[:].rearrange("p b n -> p (b n)")
        ps_v = flat[:, 0:T].rearrange("p (t c) -> p t c", c=128)
        ps_kd = flat[:, 1536:1536 + T].rearrange("p (t c) -> p t c", c=128)
        ps_ds = flat[:, 0:2048].rearrange("p (c n) -> p c n", n=128)
        ds_of = lambda c: ps_ds[:, (c % 2) * (NCH // 2) + c // 2]
        ps_dss = flat[:, 2048:3072].rearrange("p (c n) -> p c n", n=128)
        ps_att, ps_o, ps_ont = ps_v, ps_kd, ps_v
        ps_state = gps[:, 6, 0:128]
        ps_rows = gps[:, 6, 128:256]

        consts, par_in, par_ready = s("consts"), s("par_in"), s("par_ready")
        act_par, dve_par = s("act_par"), s("dve_par")
        with nc.Block() as block:
            @block.sync
            def _(e):
                with nc.allow_non_contiguous_dma(reason="small per-channel vectors"):
                    for j, v in ((GN, a["g_hgrn_norm"]), (CB, a["conv_b"]), (BA, a["b_rg_a"]), (BX, a["b_rg_x"]),
                                 (SP8, a["lambda_rg"])):
                        e.dma_start(par[:, :, j], v[0].rearrange("(i p) -> p i", p=128)).then_inc(par_in, 16)
                    for j in range(4):
                        e.dma_start(par[:, :, CW + j], a["conv_w"][0, j].rearrange("(i p) -> p i", p=128)
                                    ).then_inc(par_in, 16)
                    for j in range(2):
                        e.dma_start(lbraw[:, j], a["lower_bounds"][j].rearrange("(i p) -> p i", p=128)
                                    ).then_inc(par_in, 16)
                    e.wait_ge(par_in, 11 * 16)

            @block.gpsimd
            def _(e):
                o = Order(e, consts)
                for m, value in ((mask_p, 1.0), (mask_s, 1.0), (bmask, 1.0), (scan_mask, 1.0), (att, 0.0), (qdz, 0.0),
                                 (wg, 0.0), (rows_in, 0.0), (cols_out, 0.0)):
                    o.did(nc.gpsimd.memset(m[:], value))
                o.did(nc.gpsimd.memset(states[:, 0], 0.0))
                o.did(nc.gpsimd.memset(xp[:, 0:3], 0.0))
                o.settle()
                for m in (mask_p, mask_s):
                    o.did(nc.gpsimd.affine_select(out=m[:], in_=m[:], compare_op=ALU.is_ge, fill=0.0, base=0,
                                                  pattern=[[1, 128]], channel_multiplier=-1))
                for m, pat in ((bmask[:], [[-DS, DB]]),):
                    o.did(nc.gpsimd.affine_select(out=m, in_=m, compare_op=ALU.is_ge, fill=0.0, base=0,
                                                  pattern=pat, channel_multiplier=1))
                o.did(nc.gpsimd.memset(scan_mask[:, 0:SEQ].rearrange("p (c n) -> p c n", n=CH)[:, :, 0:1], 0.0))
                o.did(nc.gpsimd.memset(scan_mask[:, SEQ:T].rearrange("p (c n) -> p c n", n=DS)[:, :, 0:1], 0.0))
                o.settle()
                o.did(nc.gpsimd.memset(mask_p[0:CH, CH:128], 0.0))
                o.did(nc.gpsimd.affine_select(out=mask_s[:].rearrange("p (b r) -> p b r", r=DS),
                                              in_=mask_s[:].rearrange("p (b r) -> p b r", r=DS),
                                              compare_op=ALU.is_ge, fill=0.0, base=0,
                                              pattern=[[-DS, DB], [0, DS]], channel_multiplier=1))
                o.did(nc.gpsimd.affine_select(out=bmask[:], in_=bmask[:], compare_op=ALU.is_ge, fill=0.0,
                                              base=DS - 1, pattern=[[DS, DB]], channel_multiplier=-1))
                o.settle()

            @block.scalar
            def _(e):
                e.wait_ge(dve_par, 1)
                nc.scalar.activation(tmp[:, 0:2], tmp[:, 0:2], ACT.Exp).then_inc(act_par, 1)
                nc.scalar.activation(tmp[:, 3], tmp[:, 3], ACT.Exp, scale=-1.0).then_inc(act_par, 1)
                e.wait_ge(dve_par, 2)
                nc.scalar.activation(tmp[:, 5], tmp[:, 4], ACT.Ln).then_inc(act_par, 1)

            @block.vector
            def _(e):
                v = nc.vector
                o = Order(e, par_ready)

                def link(ins):
                    o.did(ins)
                    o.settle()

                e.wait_ge(par_in, 11 * 16)
                link(v.tensor_tensor(tmp[:, 2], lbraw[:, 0], lbraw[:, 1], ALU.max))
                link(v.tensor_tensor(tmp[:, 0], lbraw[:, 0], tmp[:, 2], ALU.subtract))
                link(v.tensor_tensor(tmp[:, 1], lbraw[:, 1], tmp[:, 2], ALU.subtract))
                link(v.tensor_scalar(tmp[:, 3], par[:, :, SP8], -1.0, None, ALU.mult))
                v.tensor_tensor(tmp[:, 3], tmp[:, 3], par[:, :, SP8], ALU.max).then_inc(dve_par, 1)
                e.wait_ge(act_par, 2)
                link(v.tensor_tensor(tmp[:, 2], tmp[:, 0], tmp[:, 1], ALU.add))
                link(v.reciprocal(tmp[:, 2], tmp[:, 2]))
                link(v.tensor_tensor(par[:, :, LB], tmp[:, 0], tmp[:, 2], ALU.mult))
                link(v.tensor_scalar(par[:, :, LB1], par[:, :, LB], -1.0, 1.0, ALU.mult, ALU.add))
                v.tensor_scalar(tmp[:, 4], tmp[:, 3], 1.0, None, ALU.add).then_inc(dve_par, 1)
                e.wait_ge(act_par, 3)
                link(v.tensor_scalar(tmp[:, 0], tmp[:, 4], 1.0, None, ALU.is_equal))
                link(v.scalar_tensor_tensor(out=tmp[:, 1], in0=tmp[:, 4], scalar=-1.0, in1=tmp[:, 0],
                                            op0=ALU.add, op1=ALU.add))
                link(v.reciprocal(tmp[:, 1], tmp[:, 1]))
                link(v.tensor_tensor(tmp[:, 5], tmp[:, 5], tmp[:, 0], ALU.add))
                link(v.tensor_tensor(tmp[:, 5], tmp[:, 5], tmp[:, 1], ALU.mult))
                link(v.tensor_tensor(tmp[:, 5], tmp[:, 5], tmp[:, 3], ALU.mult))
                link(v.tensor_scalar(tmp[:, 2], par[:, :, SP8], -1.0, 0.0, ALU.mult, ALU.max))
                link(v.tensor_tensor(tmp[:, 2], tmp[:, 2], tmp[:, 5], ALU.add))
                link(v.tensor_scalar(par[:, :, SP8], tmp[:, 2], 8.0, None, ALU.mult))
                link(v.tensor_scalar(par[:, :, NSP8], tmp[:, 2], -8.0, None, ALU.mult))

        (loaded, stored, cur_ready, all_used, sig_f, sig_q, sig_g, sig_r, sig_i, f_ready, ln_f, cum_ready, dl_ready,
         exp_cum, exp_dl, exp_a, qk_ready, kdec_ready, v_t, kdec_t, v_tok, kdec_tok, vmask_ready, ds_ready, dss_ready,
         st_ready, sn_ready, att_sum, att_ready, qdz_ready, o_sum, o_sq, ms_ready, rms_root, on_ready, on_t,
         state_t, xc_ready, gates, va_ready, sqrt_b, gelu_y, oc_ready, oc_t, rows_ready, self_ok) = (s(n) for n in (
             "loaded", "stored", "cur", "used", "sig_f", "sig_q", "sig_g", "sig_r", "sig_i", "f", "ln_f", "cum", "dl",
             "exp_cum", "exp_dl", "exp_a", "qk", "kdec", "v_t", "kdec_t", "v_tok", "kdec_tok", "vmask", "ds", "dss",
             "st", "sn", "att_sum", "att", "qdz", "o_sum", "o_sq", "ms", "rms_root", "on", "on_t",
             "state_t", "xc", "gates", "va", "sqrt_b", "gelu_y", "oc", "oc_t", "rows", "self"))
        NLOAD, NSTORE = 14, 6
        PROMPT, SAMPLE = slice(0, SEQ), slice(SEQ, T)

        def by(x, n):
            return x.rearrange("p (c n) -> p c n", n=n)

        with nc.Block() as block:
            @block.sync
            def _(e):
                nc.sync.sem_inc(stored, NSTORE * 16)
                with e.Fori(0, 4) as i:
                    e.wait_ge(all_used, i + 1)
                    zsrc = lambda c: z_dram[bass.ds(i + 4 * c, 1)].rearrange("a p t -> p (a t)")
                    for dst, c in ((zf, 1), (zq, 0), (zv, 2), (zg, 3), (zy, 5)):
                        e.dma_start(dst[:], zsrc(c)).then_inc(loaded, 16)
                    e.dma_start(xp[:, 3:], zsrc(4)[:, PROMPT]).then_inc(loaded, 16)
                    e.dma_start(xs[:, :, 3:], by(zsrc(4)[:, SAMPLE], DS)).then_inc(loaded, 16)
                    cols = bass.ds(i * 128, 128)
                    for w, src in ((0, a["w_rg_a"]), (1, a["w_rg_x"])):
                        for q in range(2):
                            e.dma_start(wg[64 * q:64 * q + 64, w, 64 * q:64 * q + 64],
                                        src[0, bass.ds(i * 2 + q, 1)].rearrange("a c d -> c (a d)")
                                        ).then_inc(loaded, 16)
                    e.dma_start(s0[:], a["state_hgrn"][0, :, bass.ds(i, 1)].rearrange("b a d v -> d (b a) v")
                                ).then_inc(loaded, 16)
                    e.dma_start(rows_in[0:24, :], a["state_conv"][0, :, :, cols].rearrange("b j c -> (b j) c")
                                ).then_inc(loaded, 16)
                    e.dma_start(rows_in[24:32, :], a["state_rglru"][0, :, cols]).then_inc(loaded, 16)
                    e.wait_ge(st_ready, i + 1)
                    e.dma_start(out["hgrn_p"][0, 0, bass.ds(i, 1)].rearrange("a d v -> d (a v)"),
                                states[:, NCH]).then_inc(stored, 16)
                    e.wait_ge(sn_ready, i + 1)
                    e.dma_start(out["hgrn_s"][0, :, bass.ds(i, 1)].rearrange("b a d v -> d (b a) v"),
                                snew[:]).then_inc(stored, 16)
                    e.wait_ge(rows_ready, i + 1)
                    e.dma_start(out["conv_p"][0, 0, :, cols], rows_out[0:3, :]).then_inc(stored, 16)
                    e.dma_start(out["conv_s"][0, :, :, cols].rearrange("b j c -> (b j) c"),
                                rows_out[3:27, :]).then_inc(stored, 16)
                    e.dma_start(out["rglru_p"][0, :, cols], rows_out[27:28, :]).then_inc(stored, 16)
                    e.dma_start(out["rglru_s"][0, :, cols], rows_out[28:36, :]).then_inc(stored, 16)
                e.wait_ge(stored, 5 * NSTORE * 16)

            @block.scalar
            def _(e):
                f = nc.scalar.activation
                with e.Fori(0, 4) as i:
                    e.wait_ge(loaded, (i + 1) * NLOAD * 16)
                    e.wait_ge(cur_ready, i + 1)
                    f(sf[:], zf[:], ACT.Sigmoid).then_inc(sig_f, 1)
                    f(sq[:], zq[:], ACT.Sigmoid).then_inc(sig_q, 1)
                    f(e3[:], zg[:], ACT.Sigmoid).then_inc(sig_g, 1)
                    e.wait_ge(gates, i + 1)
                    for dst, at, bias, done in ((r, 0, BA, sig_r), (ig, 3, BX, sig_i)):
                        f(dst[:].rearrange("p (n w) -> p n w", w=NW), gps[:, at:at + 3, 0:NW], ACT.Sigmoid,
                          bias=cur[:, bias:bias + 1]).then_inc(done, 1)
                    e.wait_ge(v_t, i + 1)
                    f(vtok[:], ps_v, ACT.Copy).then_inc(v_tok, 1)
                    e.wait_ge(f_ready, i + 1)
                    f(cum[:], sf[:], ACT.Ln).then_inc(ln_f, 1)
                    e.wait_ge(cum_ready, i + 1)
                    f(e1[:], sf[:], ACT.Exp).then_inc(exp_cum, 1)
                    f(e2[:], sf[:], ACT.Exp, scale=-1.0).then_inc(exp_cum, 1)
                    e.wait_ge(dl_ready, i + 1)
                    f(e3[:], cum[:], ACT.Exp).then_inc(exp_dl, 1)
                    e.wait_ge(sig_r, i + 1)
                    e.wait_ge(exp_cum, i * 2 + 2)
                    f(sf[:], r[:], ACT.Tanh, scale=cur[:, SP8:SP8 + 1]).then_inc(exp_a, 1)
                    e.wait_ge(exp_a, i * 2 + 1)
                    f(r[:], r[:], ACT.Exp, scale=cur[:, NSP8:NSP8 + 1]).then_inc(exp_a, 1)
                    e.wait_ge(va_ready, i + 1)
                    f(sf[:], sf[:], ACT.Sqrt).then_inc(sqrt_b, 1)
                    e.wait_ge(o_sum, i + 1)
                    f(cum[:].rearrange("p (t c) -> p t c", c=128), ps_o, ACT.Square).then_inc(o_sq, 1)
                    e.wait_ge(ms_ready, i + 1)
                    f(rs[:], rs[:], ACT.Sqrt).then_inc(rms_root, 1)
                    f(zy[:], zy[:], ACT.Gelu_apprx_tanh).then_inc(gelu_y, 1)

            @block.vector
            def _(e):
                v = nc.vector
                nc.vector.sem_inc(all_used, 1)
                PER = 41
                with e.Fori(0, 4) as i:
                    o = Order(e, self_ok, PER, i)

                    def link(ins):
                        o.did(ins)
                        o.settle()

                    e.wait_ge(all_used, i + 1)
                    v.tensor_copy(cur[:], par[:, bass.ds(i, 1)].rearrange("p a n -> p (a n)")).then_inc(cur_ready, 1)
                    e.wait_ge(cur_ready, i + 1)
                    e.wait_ge(state_t, i + 1)
                    link(v.tensor_copy(xs[:, :, 0:3], ps_state[:, 0:24].rearrange("p (b j) -> p b j", j=3)))
                    link(v.tensor_scalar(xc[:, PROMPT], xp[:, 0:SEQ], cur[:, CW:CW + 1], cur[:, CB:CB + 1],
                                         ALU.mult, ALU.add))
                    link(v.tensor_scalar(by(xc[:, SAMPLE], DS), xs[:, :, 0:DS], cur[:, CW:CW + 1],
                                         cur[:, CB:CB + 1], ALU.mult, ALU.add))
                    for j in range(1, 4):
                        tap = cur[:, CW + j:CW + j + 1]
                        link(v.scalar_tensor_tensor(out=xc[:, PROMPT], in0=xp[:, j:j + SEQ], scalar=tap,
                                                    in1=xc[:, PROMPT], op0=ALU.mult, op1=ALU.add))
                        ins = v.scalar_tensor_tensor(out=by(xc[:, SAMPLE], DS), in0=xs[:, :, j:j + DS], scalar=tap,
                                                     in1=by(xc[:, SAMPLE], DS), op0=ALU.mult, op1=ALU.add)
                        if j < 3:
                            link(ins)
                        else:
                            ins.then_inc(xc_ready, 1)
                    e.wait_ge(xc_ready, i + 1)
                    e.wait_ge(sig_f, i + 1)
                    v.tensor_scalar(sf[:], sf[:], cur[:, LB1:LB1 + 1], cur[:, LB:LB + 1],
                                    ALU.mult, ALU.add).then_inc(f_ready, 1)
                    e.wait_ge(f_ready, i + 1)
                    link(v.tensor_scalar(zf[:], sf[:], -1.0, 1.0, ALU.mult, ALU.add))
                    e.wait_ge(sig_q, i + 1)
                    link(v.tensor_tensor(zq[:], zq[:], sq[:], ALU.mult))
                    e.wait_ge(sig_g, i + 1)
                    link(v.tensor_tensor(zg[:], zg[:], e3[:], ALU.mult))
                    e.wait_ge(ln_f, i + 1)
                    v.tensor_tensor_scan(sf[:], scan_mask[:], cum[:], 0.0, ALU.mult, ALU.add).then_inc(cum_ready, 1)
                    e.wait_ge(cum_ready, i + 1)
                    for cols, n in ((PROMPT, CH), (SAMPLE, DS)):
                        c = by(sf[:, cols], n)
                        ins = v.tensor_tensor(by(cum[:, cols], n), c[:, :, n - 1:n].broadcast_to(list(c.shape)), c,
                                              ALU.subtract)
                        if n == DS:
                            ins.then_inc(dl_ready, 1)
                        else:
                            o.did(ins)
                    e.wait_ge(exp_cum, i * 2 + 2)
                    o.did(v.tensor_tensor(zq[:], zq[:], e1[:], ALU.mult))
                    v.tensor_tensor(e2[:], zf[:], e2[:], ALU.mult).then_inc(qk_ready, 1)
                    e.wait_ge(exp_dl, i + 1)
                    v.tensor_tensor(e3[:], zf[:], e3[:], ALU.mult).then_inc(kdec_ready, 1)
                    o.settle()
                    v.tensor_copy(by(qdz[:], 128 + DS)[:, :, 0:DS], by(zq[:, SAMPLE], DS)).then_inc(qdz_ready, 1)
                    e.wait_ge(v_tok, i + 1)
                    for b in range(DB):
                        ins = v.tensor_scalar(vmask[:, b], vtok[:, NPT], bmask[:, b:b + 1], None, ALU.mult)
                    ins.then_inc(vmask_ready, 1)
                    e.wait_ge(kdec_t, i + 1)
                    v.tensor_copy(kdtok[:], ps_kd).then_inc(kdec_tok, 1)
                    e.wait_ge(ds_ready, i + 1)
                    e.wait_ge(stored, (i + 1) * NSTORE * 16)
                    for c in range(NCH):
                        at = (c + 1) * CH - 1
                        ins = v.scalar_tensor_tensor(out=states[:, c + 1], in0=states[:, c], scalar=e1[:, at:at + 1],
                                                     in1=ds_of(c), op0=ALU.mult, op1=ALU.add)
                        if c < NCH - 1:
                            link(ins)
                        else:
                            ins.then_inc(st_ready, 1)
                    e.wait_ge(dss_ready, i + 1)
                    for b in range(DB):
                        at = SEQ + (b + 1) * DS - 1
                        ins = v.scalar_tensor_tensor(out=snew[:, b], in0=s0[:, b], scalar=e1[:, at:at + 1],
                                                     in1=ps_dss[:, b], op0=ALU.mult, op1=ALU.add)
                    ins.then_inc(sn_ready, 1)
                    wait_apart(e, P, att_sum, i + 1)
                    v.copy_predicated(att[:, 0:NPT], mask_p[:].bitcast(I32).rearrange("p (a n) -> p a n", a=1)
                                      .broadcast_to([128, NPT, 128]), ps_att[:, 0:NPT])
                    v.copy_predicated(att[:, NPT], mask_s[:].bitcast(I32), ps_att[:, NPT]).then_inc(att_ready, 1)
                    e.wait_ge(exp_a, i * 2 + 2)
                    link(v.tensor_tensor(cum[:], r[:], r[:], ALU.mult))
                    v.scalar_tensor_tensor(out=sf[:], in0=cum[:], scalar=1.0, in1=sf[:],
                                           op0=ALU.add, op1=ALU.mult).then_inc(va_ready, 1)
                    e.wait_ge(sig_i, i + 1)
                    link(v.tensor_tensor(ig[:], ig[:], xc[:], ALU.mult))
                    e.wait_ge(sqrt_b, i + 1)
                    link(v.tensor_tensor(ig[:], ig[:], sf[:], ALU.mult))
                    first_a, first_b = by(r[:, SAMPLE], DS)[:, :, 0], by(ig[:, SAMPLE], DS)[:, :, 0]
                    link(v.tensor_tensor(e3[:, 0:DB], first_a, ps_state[:, 24:32], ALU.mult))
                    link(v.tensor_tensor(first_b, first_b, e3[:, 0:DB], ALU.add))
                    link(v.memset(first_a, 0.0))
                    link(v.tensor_tensor_scan(xc[:], r[:], ig[:], 0.0, ALU.mult, ALU.add))
                    o.did(v.tensor_copy(cols_out[:, 0:3], xp[:, SEQ:SEQ + 3]))
                    o.did(v.tensor_copy(cols_out[:, 3:27].rearrange("p (b j) -> p b j", j=3), xs[:, :, DS:DS + 3]))
                    o.did(v.tensor_copy(cols_out[:, 27:28], xc[:, SEQ - 1:SEQ]))
                    v.tensor_copy(cols_out[:, 28:36], by(xc[:, SAMPLE], DS)[:, :, DS - 1]).then_inc(oc_ready, 1)
                    e.wait_ge(o_sq, i + 1)
                    link(v.tensor_reduce(rs[:], cum[:].rearrange("p (t c) -> p t c", c=128), AX.X, ALU.add))
                    v.tensor_scalar(rs[:], rs[:], 1.0 / 128, EPS, ALU.mult, ALU.add).then_inc(ms_ready, 1)
                    e.wait_ge(rms_root, i + 1)
                    link(v.reciprocal(rs[:], rs[:]))
                    v.tensor_tensor(on[:], ps_o, rs[:].rearrange("p (t a) -> p t a", a=1).broadcast_to([128, NT, 128]),
                                    ALU.mult).then_inc(on_ready, 1)
                    e.wait_ge(gelu_y, i + 1)
                    link(v.tensor_tensor(cat[:, bass.ds(i + 4, 1)].rearrange("p a t -> p (a t)"), xc[:], zy[:],
                                         ALU.mult))
                    e.wait_ge(oc_t, i + 1)
                    v.tensor_copy(rows_out[:], ps_rows[0:36]).then_inc(rows_ready, 1)
                    e.wait_ge(on_t, i + 1)
                    e.wait_ge(stored, (i + 1) * NSTORE * 16)
                    v.scalar_tensor_tensor(out=cat[:, bass.ds(i, 1)].rearrange("p a t -> p (a t)"),
                                           in0=flat[:, 0:T], scalar=cur[:, GN:GN + 1], in1=zg[:],
                                           op0=ALU.mult, op1=ALU.mult).then_inc(all_used, 1)
                    o.close()

            @block.tensor
            def _(e):
                mm, tr = nc.tensor.matmul, nc.tensor.transpose
                with e.Fori(0, 4) as i:
                    e.wait_ge(loaded, (i + 1) * NLOAD * 16)
                    tr(ps_state, rows_in[:], P.ident[:]).then_inc(state_t, 1)
                    e.wait_ge(xc_ready, i + 1)
                    e.wait_ge(all_used, i + 1)
                    for n in range(NN):
                        for w in range(2):
                            last = mm(gps[:, 3 * w + n, 0:NW], wg[:, w], xc[:, n * NW:(n + 1) * NW],
                                      start=True, stop=True)
                    last.then_inc(gates, 1)
                    e.wait_ge(sig_r, i + 1)
                    for t in range(NT):
                        last = tr(ps_v[:, t], zv[:, t * 128:(t + 1) * 128], P.ident[:])
                    last.then_inc(v_t, 1)
                    e.wait_ge(sig_i, i + 1)
                    e.wait_ge(kdec_ready, i + 1)
                    for t in range(NT):
                        last = tr(ps_kd[:, t], e3[:, t * 128:(t + 1) * 128], P.ident[:])
                    last.then_inc(kdec_t, 1)
                    e.wait_ge(v_tok, i + 1)
                    e.wait_ge(kdec_tok, i + 1)
                    for c in range(NCH):
                        t, half = c // 2, slice(CH * (c % 2), CH * (c % 2) + CH)
                        last = mm(ds_of(c), kdtok[half, t], vtok[half, t], start=True, stop=True)
                    last.then_inc(ds_ready, 1)
                    e.wait_ge(vmask_ready, i + 1)
                    for q in range(2):
                        last = mm(ps_dss[:, 4 * q:4 * q + 4].rearrange("p b n -> p (b n)"), kdtok[:, NPT],
                                  vmask[:, 4 * q:4 * q + 4].rearrange("p b n -> p (b n)"), start=True, stop=True)
                    last.then_inc(dss_ready, 1)
                    e.wait_ge(qk_ready, i + 1)
                    e.wait_ge(st_ready, i + 1)
                    for t in range(NT):
                        cols = slice(t * 128, (t + 1) * 128)
                        last = mm(ps_att[:, t], e2[:, cols], zq[:, cols], start=True, stop=True)
                    last.then_inc(att_sum, 1)
                    e.wait_ge(att_ready, i + 1)
                    e.wait_ge(sn_ready, i + 1)
                    e.wait_ge(qdz_ready, i + 1)
                    for t in range(NPT):
                        mm(ps_o[:, t], att[:, t], vtok[:, t], start=True, stop=False, skip_group_check=True)
                        for q in range(2):
                            half = slice(CH * q, CH * q + CH)
                            mm(ps_o[half, t], zq[:, t * 128 + CH * q:t * 128 + CH * q + CH], states[:, 2 * t + q],
                               start=False, stop=True, skip_group_check=True)
                    mm(ps_o[:, NPT], att[:, NPT], vtok[:, NPT], start=True, stop=False, skip_group_check=True)
                    for b in range(DB):
                        last = mm(ps_o[:, NPT], qdz[:, b * 128:(b + 1) * 128], s0[:, b], start=False,
                                  stop=b == DB - 1, skip_group_check=True)
                    last.then_inc(o_sum, 1)
                    e.wait_ge(oc_ready, i + 1)
                    tr(ps_rows, cols_out[:], P.ident[:]).then_inc(oc_t, 1)
                    e.wait_ge(on_ready, i + 1)
                    for t in range(NT):
                        last = tr(ps_ont[:, t], on[:, t], P.ident[:])
                    last.then_inc(on_t, 1)
        nc.clear_and_free_semaphores(used)
        nc.all_engine_barrier()


def output_projection(P, cat):
    nc = P.nc
    w_v = P.a["w_out"][0].rearrange("(k p) c -> p k c", p=128)
    with ExitStack() as ctx:
        def sb(n, shape, d=F32):
            return ctx.enter_context(nc.sbuf_tensor(f"op_{n}", shape, d))
        s = lambda n: ctx.enter_context(nc.semaphore(f"op_{n}"))
        raw = sb("raw", [128, 2, D])
        whi, wlo = sb("whi", [128, KC, D], F32R), sb("wlo", [128, KC, D], F32R)
        chi, clo = sb("chi", [128, 3, KC, 128], F32R), sb("clo", [128, 3, KC, 128], F32R)
        po = ctx.enter_context(nc.psum_tensor("op_ps", [128, 3, D], F32))
        w_in = [s(f"w_in{u}") for u in range(2)]
        whi_done, wlo_done, chi_done, clo_done, summed, added = map(
            s, ("whi", "wlo", "chi", "clo", "summed", "added"))
        with nc.Block() as block:
            @block.sync
            def _(e):
                for k in range(KC):
                    if k >= 2:
                        e.wait_ge(wlo_done, k - 1)
                    e.dma_start(raw[:, k % 2], w_v[:, k]).then_inc(w_in[k % 2], 16)

            @block.scalar
            def _(e):
                for k in range(KC):
                    e.wait_ge(w_in[k % 2], (k // 2 + 1) * 16)
                    nc.scalar.activation(whi[:, k], raw[:, k % 2], ACT.Copy).then_inc(whi_done, 1)
                with e.Fori(0, NT // 3) as i:
                    for u in range(3):
                        e.wait_ge(summed, i * 3 + u + 1)
                        nc.scalar.activation(chi[:, u], cat[:, :, bass.ds((i * 3 + u) * 128, 128)],
                                             ACT.Copy).then_inc(chi_done, 1)

            @block.vector
            def _(e):
                for k in range(KC):
                    e.wait_ge(whi_done, k + 1)
                    nc.vector.tensor_tensor(wlo[:, k], raw[:, k % 2], whi[:, k].bitcast(F32),
                                            ALU.subtract).then_inc(wlo_done, 1)
                nc.vector.sem_inc(added, 3)
                with e.Fori(0, NT // 3) as i:
                    for u in range(3):
                        e.wait_ge(chi_done, i * 3 + u + 1)
                        nc.vector.tensor_tensor(clo[:, u], cat[:, :, bass.ds((i * 3 + u) * 128, 128)],
                                                chi[:, u].bitcast(F32), ALU.subtract).then_inc(clo_done, 1)
                    for u in range(3):
                        e.wait_ge(summed, i * 3 + u + 4)
                        row = P.h[:, bass.ds(i * 3 + u, 1)].rearrange("p a d -> p (a d)")
                        nc.vector.tensor_tensor(row, po[:, u], row, ALU.add).then_inc(added, 1)

            @block.tensor
            def _(e):
                nc.tensor.sem_inc(summed, 3)
                e.wait_ge(wlo_done, KC)
                with e.Fori(0, NT // 3) as i:
                    for u in range(3):
                        e.wait_ge(clo_done, i * 3 + u + 1)
                        e.wait_ge(added, i * 3 + u + 1)
                        for q in range(2):
                            cols = slice(512 * q, 512 * q + 512)
                            for k in range(KC):
                                last = three_passes(nc, po[:, u, cols], (chi[:, u, k], clo[:, u, k]),
                                                    (whi[:, k, cols], wlo[:, k, cols]), k == 0, k == KC - 1)
                        last.then_inc(summed, 1)


def route_scores(P, xhi, xlo, sv, si):
    nc = P.nc
    w_v = P.a["w_peer_q"][0].rearrange("(k p) c -> p k c", p=128)
    keys = P.a["peer_keys"][0].rearrange("h p n c -> (h p) n c")
    with ExitStack() as ctx:
        def sb(n, shape, d=F32):
            return ctx.enter_context(nc.sbuf_tensor(f"rs_{n}", shape, d))
        s = lambda n: ctx.enter_context(nc.semaphore(f"rs_{n}"))
        raw = sb("raw", [128, 2, KC, 128])
        whi, wlo = sb("whi", [128, 2, KC, 128], F32R), sb("wlo", [128, 2, KC, 128], F32R)
        kraw = sb("kraw", [128, 2, 128])
        kt = sb("kt", [128, 2, 128])
        q = sb("q", [128, T])
        rest = sb("rest", [128, NT, 128])
        val16, ind16 = sb("val16", [128, NT, K]), sb("ind16", [128, NT, K], U32)
        pq = ctx.enter_context(nc.psum_tensor("rs_pq", [128, 2, 512], F32))
        pk = ctx.enter_context(nc.psum_tensor("rs_pk", [128, 512], F32))
        psc = ctx.enter_context(nc.psum_tensor("rs_sc", [128, 3, 4, 128], F32))
        scores = [psc[:, t // 4, t % 4] for t in range(NT)]
        w_in = [s(f"w_in{u}") for u in range(2)]
        hi_done, lo_done, q_sum, q_ready, k_t, kt_ready, scored, ranked, self_ok = map(
            s, ("hi", "lo", "q_sum", "q_ready", "k_t", "kt", "scored", "ranked", "self"))
        LAST = HP // 2 - 1
        with nc.Block() as block:
            @block.sync
            def _(e):
                with e.Fori(0, HP // 2) as i:
                    for u in range(2):
                        n = i * 2 + u
                        e.wait_ge(lo_done, n + 1)
                        e.wait_ge(k_t, n + 1)
                        e.dma_start(raw[:, u], w_v[:, :, bass.ds(n * 128, 128)]).then_inc(w_in[u], 16)
                        e.dma_start(kraw[:, u], keys[bass.ds(n, 1)].rearrange("a n c -> n (a c)")
                                    ).then_inc(w_in[u], 16)

            @block.scalar
            def _(e):
                nc.scalar.sem_inc(q_ready, 2)
                nc.scalar.sem_inc(kt_ready, 2)

                def hi(i, u):
                    n = i * 2 + u
                    e.wait_ge(w_in[u], (i + 1) * 32)
                    e.wait_ge(q_sum, (n + 1) * NN)
                    nc.scalar.activation(whi[:, u], raw[:, u], ACT.Copy).then_inc(hi_done, 1)

                def step(i, u):
                    n = i * 2 + u
                    e.wait_ge(k_t, n + 3)
                    e.wait_ge(scored, n + 1)
                    nc.scalar.activation(kt[:, u], pk[:, u * 128:(u + 1) * 128], ACT.Copy).then_inc(kt_ready, 1)
                    for m in range(NN):
                        e.wait_ge(q_sum, (n + 2) * NN + m + 1)
                        nc.scalar.activation(q[:, m * NW:(m + 1) * NW], pq[:, (m + u) % 2, 0:NW],
                                             ACT.Copy).then_inc(q_ready, 1)

                hi(0, 0)
                with e.Fori(0, LAST) as i:
                    hi(i, 1)
                    step(i, 0)
                    hi(i + 1, 0)
                    step(i, 1)
                hi(LAST, 1)
                step(LAST, 0)
                step(LAST, 1)

            @block.vector
            def _(e):
                v = nc.vector
                nc.vector.sem_inc(lo_done, 2)
                nc.vector.sem_inc(ranked, 1)

                def lo(i, u):
                    e.wait_ge(hi_done, i * 2 + u + 1)
                    v.tensor_tensor(wlo[:, u], raw[:, u], whi[:, u].bitcast(F32), ALU.subtract).then_inc(lo_done, 1)

                def rank(i, u):
                    n = i * 2 + u
                    o = Order(e, self_ok, 5 * NT + 1, n)
                    val = [val16[:, t] for t in range(NT)]
                    ind = [ind16[:, t] for t in range(NT)]
                    wait_apart(e, P, scored, n + 2)
                    for t in range(NT):
                        o.did(v.max(val[t][:, 0:8], scores[t]))
                    wait_apart(e, P, o.sem, o.value())
                    for t in range(NT):
                        o.did(v.max_index(ind[t][:, 0:8], val[t][:, 0:8], scores[t]))
                        o.did(v.match_replace(rest[:, t], val[t][:, 0:8], scores[t], LOWEST))
                    wait_apart(e, P, o.sem, o.value())
                    for t in range(NT):
                        o.did(v.max(val[t][:, 8:16], rest[:, t]))
                    wait_apart(e, P, o.sem, o.value())
                    for t in range(NT):
                        o.did(v.max_index(ind[t][:, 8:16], val[t][:, 8:16], rest[:, t]))
                    o.settle()
                    o.did(v.tensor_copy(sv[:, :, bass.ds(n, 1), :].rearrange("p t a n -> p t (a n)"), val16[:]))
                    o.settle()
                    v.tensor_copy(si[:, :, bass.ds(n, 1), :].rearrange("p t a n -> p t (a n)"), ind16[:]
                                  ).then_inc(ranked, 1)
                    o.close()

                lo(0, 0)
                with e.Fori(0, LAST) as i:
                    lo(i, 1)
                    rank(i, 0)
                    lo(i + 1, 0)
                    rank(i, 1)
                lo(LAST, 1)
                rank(LAST, 0)
                rank(LAST, 1)

            @block.tensor
            def _(e):
                nc.tensor.sem_inc(q_sum, 2 * NN)
                nc.tensor.sem_inc(k_t, 2)
                nc.tensor.sem_inc(scored, 1)
                with e.Fori(0, HP // 2) as i:
                    for u in range(2):
                        n = i * 2 + u
                        e.wait_ge(w_in[u], (i + 1) * 32)
                        e.wait_ge(kt_ready, n + 1)
                        nc.tensor.transpose(pk[:, u * 128:(u + 1) * 128], kraw[:, u], P.ident[:]).then_inc(k_t, 1)
                        e.wait_ge(lo_done, n + 3)
                        for m in range(NN):
                            e.wait_ge(q_ready, n * NN + m + 1)
                            cols = slice(m * NW, (m + 1) * NW)
                            for k in range(KC):
                                last = three_passes(nc, pq[:, (m + u) % 2, 0:NW], (whi[:, u, k], wlo[:, u, k]),
                                                    (xhi[:, k, cols], xlo[:, k, cols]), k == 0, k == KC - 1)
                            last.then_inc(q_sum, 1)
                        e.wait_ge(kt_ready, n + 3)
                        e.wait_ge(q_ready, (n + 1) * NN + 2)
                        e.wait_ge(ranked, n + 1)
                        for t in range(NT):
                            last = nc.tensor.matmul(scores[t], q[:, t * 128:(t + 1) * 128], kt[:, u],
                                                    start=True, stop=True)
                        last.then_inc(scored, 1)


def route_picks(P, sv, si, pick_i, pick_j, ghi, glo):
    nc = P.nc
    with ExitStack() as ctx:
        def sb(n, shape, d=F32):
            return ctx.enter_context(nc.sbuf_tensor(f"rp_{n}", shape, d))
        s = lambda n: ctx.enter_context(nc.semaphore(f"rp_{n}"))
        cand, cand2 = sb("cand", [128, PH, K, K]), sb("cand2", [128, PH, K, K])
        best, at = sb("best", [128, PH, K]), sb("at", [128, PH, K], U32)
        ab = sb("ab", [128, 2, PH * K], U32)
        abf = sb("abf", [128, 2, PH * K])
        sif = sb("sif", [128, HP, K])
        eq = sb("eq", [128, 2, PH * K, K])
        rows = sb("rows", [128, 3, PH * K])
        total = sb("total", [128, PH])
        iota_u, iota = sb("iota_u", [128, K], I32), sb("iota", [128, K])
        pt = ctx.enter_context(nc.psum_tensor("rp_pt", [128, 3, 512], F32))
        made, self_ok, shifted, exped, rows_ready, rows_t, hi_done, taken = map(
            s, ("made", "self", "shifted", "exped", "rows", "rows_t", "hi", "taken"))
        with nc.Block() as block:
            @block.gpsimd
            def _(e):
                nc.gpsimd.iota(iota_u[:], [[1, K]], base=0, channel_multiplier=0).then_inc(made, 1)
                e.wait_ge(made, 1)
                nc.gpsimd.tensor_copy(iota[:], iota_u[:]).then_inc(made, 1)

            @block.scalar
            def _(e):
                with e.Fori(0, NT) as i:
                    e.wait_ge(shifted, i + 1)
                    nc.scalar.activation(rows[:, 2], rows[:, 2], ACT.Exp).then_inc(exped, 1)
                    e.wait_ge(rows_t, i + 1)
                    cols = bass.ds(i * 128, 128)
                    for dst, n in ((pick_i, 0), (pick_j, 1), (ghi, 2)):
                        nc.scalar.activation(dst[:, cols], pt[:, n, 0:128], ACT.Copy).then_inc(hi_done, 1)

            @block.vector
            def _(e):
                v = nc.vector
                PER = 6 * PH + 6
                e.wait_ge(made, 2)
                with e.Fori(0, NT) as i:
                    o = Order(e, self_ok, PER, i)
                    one = lambda x: x[:, bass.ds(i, 1)].rearrange("p a n k -> p (a n) k")
                    sv4 = one(sv).rearrange("p (h x) k -> p h x k", x=2)
                    shape = [128, PH, K, K]
                    o.did(v.tensor_tensor(
                        cand[:], sv4[:, :, 0, :].rearrange("p h (k a) -> p h k a", a=1).broadcast_to(shape),
                        sv4[:, :, 1, :].rearrange("p h (a k) -> p h a k", a=1).broadcast_to(shape), ALU.add))
                    o.did(v.tensor_copy(sif[:], one(si)))
                    wait_apart(e, P, o.sem, o.value())
                    flat = [x.rearrange("p a b -> p (a b)") for x in (cand[:, h] for h in range(PH))]
                    flat2 = [x.rearrange("p a b -> p (a b)") for x in (cand2[:, h] for h in range(PH))]
                    for h in range(PH):
                        o.did(v.max(best[:, h, 0:8], flat[h]))
                    wait_apart(e, P, o.sem, o.value())
                    for h in range(PH):
                        o.did(v.max_index(at[:, h, 0:8], best[:, h, 0:8], flat[h]))
                        o.did(v.match_replace(flat2[h], best[:, h, 0:8], flat[h], LOWEST))
                    wait_apart(e, P, o.sem, o.value())
                    for h in range(PH):
                        o.did(v.max(best[:, h, 8:16], flat2[h]))
                    wait_apart(e, P, o.sem, o.value())
                    for h in range(PH):
                        o.did(v.max_index(at[:, h, 8:16], best[:, h, 8:16], flat2[h]))
                    e.wait_ge(taken, i + 1)
                    g = rows[:, 2].rearrange("p (h k) -> p h k", k=K)
                    v.tensor_tensor(g, best[:], best[:, :, 0:1].broadcast_to([128, PH, K]),
                                    ALU.subtract).then_inc(shifted, 1)
                    o.settle()
                    atf = at[:].rearrange("p h k -> p (h k)")
                    o.did(v.tensor_single_scalar(ab[:, 0], atf, 4, ALU.logical_shift_right))
                    o.did(v.tensor_single_scalar(ab[:, 1], atf, K - 1, ALU.bitwise_and))
                    o.settle()
                    o.did(v.tensor_copy(abf[:], ab[:]))
                    o.settle()
                    sif4 = sif[:].rearrange("p (h x) k -> p h x k", x=2)
                    for x in range(2):
                        o.did(v.tensor_tensor(
                            eq[:, x], abf[:, x].rearrange("p (n a) -> p n a", a=1).broadcast_to([128, PH * K, K]),
                            iota[:].rearrange("p (a k) -> p a k", a=1).broadcast_to([128, PH * K, K]),
                            ALU.is_equal))
                    o.settle()
                    for x in range(2):
                        q4 = eq[:, x].rearrange("p (h k) a -> p h k a", k=K)
                        o.did(v.tensor_tensor(q4, q4, sif4[:, :, x, :].rearrange("p h (a k) -> p h a k", a=1)
                                              .broadcast_to(shape), ALU.mult))
                    o.settle()
                    for x in range(2):
                        o.did(v.tensor_reduce(rows[:, x], eq[:, x], AX.X, ALU.add))
                    e.wait_ge(exped, i + 1)
                    o.did(v.tensor_reduce(total[:], g, AX.X, ALU.add))
                    o.settle()
                    o.did(v.reciprocal(total[:], total[:]))
                    o.settle()
                    v.tensor_tensor(g, g, total[:].rearrange("p (h a) -> p h a", a=1).broadcast_to([128, PH, K]),
                                    ALU.mult).then_inc(rows_ready, 1)
                    e.wait_ge(hi_done, i * 3 + 3)
                    cols = bass.ds(i * 128, 128)
                    o.did(v.tensor_tensor(glo[:, cols], pt[:, 2, 0:128], ghi[:, cols].bitcast(F32), ALU.subtract))
                    o.close()

            @block.tensor
            def _(e):
                nc.tensor.sem_inc(taken, 1)
                with e.Fori(0, NT) as i:
                    e.wait_ge(rows_ready, i + 1)
                    for n in range(3):
                        last = nc.tensor.transpose(pt[:, n, 0:128], rows[:, n], P.ident[:])
                    last.then_inc(rows_t, 1)
                    e.wait_ge(rows_t, i + 1)
                    nc.tensor.sem_inc(taken, 1)


SUB = 32
NSUB = T // SUB
QUAD = 4


def expert_weights(P, pick_i, pick_j, ghi, glo, w_dram):
    nc = P.nc
    RING = 4
    NQ = SUB // QUAD
    with ExitStack() as ctx:
        def sb(n, shape, d=F32):
            return ctx.enter_context(nc.sbuf_tensor(f"ew_{n}", shape, d))
        s = lambda n: ctx.enter_context(nc.semaphore(f"ew_{n}"))
        iota_u, iota = sb("iota_u", [128, NK], I32), sb("iota", [128, NK])
        cur = sb("cur", [128, 2, 4, SUB])
        am, bh, bl = (sb(n, [128, RING, QUAD, NK], F32R) for n in ("am", "bh", "bl"))
        wt = sb("wt", [128, 2, NK, SUB])
        pw = ctx.enter_context(nc.psum_tensor("ew_pw", [128, RING, QUAD, NK], F32))
        w_out = [s(f"w_out{u}") for u in range(2)]
        made, cur_ready, onehot, summed, w_ready = map(s, ("made", "cur", "onehot", "summed", "w"))
        with nc.Block() as block:
            @block.gpsimd
            def _(e):
                nc.gpsimd.iota(iota_u[:], [[1, NK]], base=0, channel_multiplier=0).then_inc(made, 1)
                e.wait_ge(made, 1)
                nc.gpsimd.tensor_copy(iota[:], iota_u[:]).then_inc(made, 1)

            @block.sync
            def _(e):
                for u in range(2):
                    nc.sync.sem_inc(w_out[u], 16)
                with e.Fori(0, NSUB // 2) as i:
                    for u in range(2):
                        e.wait_ge(w_ready, (i * 2 + u + 1) * NQ + RING)
                        e.dma_start(w_dram[:, bass.ds(i * 2 + u, 1)].rearrange("p a j t -> p (a j t)"),
                                    wt[:, u].rearrange("p j t -> p (j t)")).then_inc(w_out[u], 16)
                for u in range(2):
                    e.wait_ge(w_out[u], (NSUB // 2 + 1) * 16)

            @block.vector
            def _(e):
                v = nc.vector
                e.wait_ge(made, 2)
                with e.Fori(0, NSUB // 2) as i:
                    for u in range(2):
                        n = i * 2 + u
                        cols = bass.ds(n * SUB, SUB)
                        for x, src in enumerate((pick_i[:], pick_j[:], ghi[:].bitcast(F32), glo[:])):
                            v.tensor_copy(cur[:, u, x], src[:, cols]).then_inc(cur_ready, 1)
                        e.wait_ge(cur_ready, (n + 1) * 4)
                        for q in range(NQ):
                            e.wait_ge(summed, n * NQ + q + 1)
                            for t in range(QUAD):
                                c = slice(q * QUAD + t, q * QUAD + t + 1)
                                v.tensor_scalar(am[:, q % RING, t], iota[:], cur[:, u, 0, c], None, ALU.is_equal)
                                v.tensor_scalar(bh[:, q % RING, t], iota[:], cur[:, u, 1, c], cur[:, u, 2, c],
                                                ALU.is_equal, ALU.mult)
                                last = v.tensor_scalar(bl[:, q % RING, t], iota[:], cur[:, u, 1, c],
                                                       cur[:, u, 3, c], ALU.is_equal, ALU.mult)
                            last.then_inc(onehot, 1)

            @block.tensor
            def _(e):
                nc.tensor.sem_inc(summed, RING)
                with e.Fori(0, NSUB // 2) as i:
                    for u in range(2):
                        for q in range(NQ):
                            m = (i * 2 + u) * NQ + q
                            e.wait_ge(onehot, m + 1)
                            e.wait_ge(w_ready, m + 1)
                            for t in range(QUAD):
                                r = q % RING
                                nc.tensor.matmul(pw[:, r, t], am[:, r, t], bh[:, r, t], start=True, stop=False)
                                last = nc.tensor.matmul(pw[:, r, t], am[:, r, t], bl[:, r, t], start=False, stop=True)
                            last.then_inc(summed, 1)

            @block.scalar
            def _(e):
                nc.scalar.sem_inc(w_ready, RING)
                with e.Fori(0, NSUB // 2) as i:
                    for u in range(2):
                        e.wait_ge(w_out[u], (i + 1) * 16)
                        for q in range(NQ):
                            e.wait_ge(summed, (i * 2 + u) * NQ + q + 1 + RING)
                            dst = wt[:, u, :, q * QUAD:(q + 1) * QUAD].rearrange("p j t -> p t j")
                            nc.scalar.activation(dst, pw[:, q % RING], ACT.Copy).then_inc(w_ready, 1)


def expert_activations(P, xhi, xlo, act_dram):
    nc = P.nc
    u_v = P.a["peer_u"][0].rearrange("(i j) d -> i j d", j=NK)
    with ExitStack() as ctx:
        def sb(n, shape, d=F32):
            return ctx.enter_context(nc.sbuf_tensor(f"ea_{n}", shape, d))
        s = lambda n: ctx.enter_context(nc.semaphore(f"ea_{n}"))
        raw = sb("raw", [128, 2, D])
        uhi, ulo = sb("uhi", [128, 2, KC, 128], F32R), sb("ulo", [128, 2, KC, 128], F32R)
        stage = sb("stage", [128, 2, T])
        pt = ctx.enter_context(nc.psum_tensor("ea_pt", [128, KC, 128], F32))
        pa = ctx.enter_context(nc.psum_tensor("ea_pa", [128, 2 * NN, 512], F32))
        u_in = [s(f"u_in{u}") for u in range(2)]
        stored = [s(f"stored{u}") for u in range(2)]
        u_t, hi_done, lo_done, summed, gelued = map(s, ("u_t", "hi", "lo", "summed", "gelued"))
        LAST = NK // 2 - 1
        with nc.Block() as block:
            @block.sync
            def _(e):
                for u in range(2):
                    nc.sync.sem_inc(stored[u], 16)

                def load(i, u):
                    e.wait_ge(u_t, i * 2 + u + 1)
                    e.dma_start(raw[:, u], u_v[:, bass.ds(i * 2 + u, 1)].rearrange("p a d -> p (a d)")
                                ).then_inc(u_in[u], 16)

                def store(i, u):
                    e.wait_ge(gelued, (i * 2 + u + 1) * NN + 2 * NN)
                    e.dma_start(act_dram[:, bass.ds(i * 2 + u, 1)].rearrange("p a t -> p (a t)"),
                                stage[:, u]).then_inc(stored[u], 16)

                load(0, 0)
                load(0, 1)
                with e.Fori(0, LAST) as i:
                    load(i + 1, 0)
                    store(i, 0)
                    load(i + 1, 1)
                    store(i, 1)
                store(LAST, 0)
                store(LAST, 1)
                for u in range(2):
                    e.wait_ge(stored[u], (NK // 2 + 1) * 16)

            @block.scalar
            def _(e):
                nc.scalar.sem_inc(gelued, 2 * NN)

                def hi(i, u):
                    e.wait_ge(u_t, i * 2 + u + 3)
                    e.wait_ge(summed, (i * 2 + u + 1) * NN)
                    nc.scalar.activation(uhi[:, u], pt[:], ACT.Copy).then_inc(hi_done, 1)

                def gelu(i, u):
                    e.wait_ge(stored[u], (i + 1) * 16)
                    for n in range(NN):
                        e.wait_ge(summed, (i * 2 + u + 2) * NN + n + 1)
                        nc.scalar.activation(stage[:, u, n * NW:(n + 1) * NW], pa[:, NN * u + n, 0:NW],
                                             ACT.Gelu_apprx_tanh).then_inc(gelued, 1)

                hi(0, 0)
                with e.Fori(0, LAST) as i:
                    hi(i, 1)
                    gelu(i, 0)
                    hi(i + 1, 0)
                    gelu(i, 1)
                hi(LAST, 1)
                gelu(LAST, 0)
                gelu(LAST, 1)

            @block.vector
            def _(e):
                nc.vector.sem_inc(lo_done, 1)
                with e.Fori(0, NK // 2) as i:
                    for u in range(2):
                        e.wait_ge(hi_done, i * 2 + u + 1)
                        nc.vector.tensor_tensor(ulo[:, u], pt[:], uhi[:, u].bitcast(F32),
                                                ALU.subtract).then_inc(lo_done, 1)

            @block.tensor
            def _(e):
                nc.tensor.sem_inc(u_t, 2)
                nc.tensor.sem_inc(summed, 2 * NN)

                def turn(i, u):
                    e.wait_ge(u_in[u], (i + 1) * 16)
                    e.wait_ge(lo_done, i * 2 + u + 1)
                    for k in range(KC):
                        last = nc.tensor.transpose(pt[:, k], raw[:, u, k * 128:(k + 1) * 128], P.ident[:])
                    last.then_inc(u_t, 1)

                def product(i, u):
                    e.wait_ge(lo_done, i * 2 + u + 2)
                    for n in range(NN):
                        e.wait_ge(gelued, (i * 2 + u) * NN + n + 1)
                        cols = slice(n * NW, (n + 1) * NW)
                        for k in range(KC):
                            last = three_passes(nc, pa[:, NN * u + n, 0:NW], (uhi[:, u, k], ulo[:, u, k]),
                                                (xhi[:, k, cols], xlo[:, k, cols]), k == 0, k == KC - 1)
                        last.then_inc(summed, 1)

                turn(0, 0)
                with e.Fori(0, LAST) as i:
                    turn(i, 1)
                    product(i, 0)
                    turn(i + 1, 0)
                    product(i, 1)
                turn(LAST, 1)
                product(LAST, 0)
                product(LAST, 1)


GRP = 4


def expert_outputs(P, w_dram, act_dram):
    nc = P.nc
    NG = NK // GRP
    v_v = P.a["peer_v"][0].rearrange("(i j) d -> i j d", j=NK)
    with ExitStack() as ctx:
        def sb(n, shape, d=F32):
            return ctx.enter_context(nc.sbuf_tensor(f"eo_{n}", shape, d))
        s = lambda n: ctx.enter_context(nc.semaphore(f"eo_{n}"))
        wt = sb("wt", [128, 2, NSUB, GRP, SUB])
        at = sb("at", [128, 2, GRP, T])
        raw = sb("raw", [128, 2, D])
        vhi, vlo = sb("vhi", [128, 2, GRP, D], F32R), sb("vlo", [128, 2, GRP, D], F32R)
        prod = sb("prod", [128, 3, GRP, 128])
        phi, plo = sb("phi", [128, 3, GRP, 128], F32R), sb("plo", [128, 3, GRP, 128], F32R)
        po = ctx.enter_context(nc.psum_tensor("eo_ps", [128, 3, D], F32))
        wa_in = [s(f"wa_in{u}") for u in range(2)]
        v_in = [s(f"v_in{u}") for u in range(2)]
        vhi_done, vlo_done, prod_done, phi_done, plo_done, summed, added = map(
            s, ("vhi", "vlo", "prod", "phi", "plo", "summed", "added"))
        PAIRS = NG // 2

        def in_pairs(e, first, body):
            first()
            with e.Fori(0, PAIRS - 1) as i:
                body(i * 2, 0, False)
                body(i * 2 + 1, 1, False)
            body(NG - 2, 0, False)
            body(NG - 1, 1, True)

        V_TILES = {1: 0, 3: 1, 5: 2, 7: 3}

        with nc.Block() as block:
            @block.sync
            def _(e):
                def weights(g, u):
                    e.wait_ge(prod_done, g * NT + NT)
                    e.dma_start(wt[:, u].rearrange("p s j t -> p s (j t)"),
                                w_dram[:, :, bass.ds(g * GRP, GRP), :].rearrange("p s j t -> p s (j t)")
                                ).then_inc(wa_in[u], 16)
                    e.dma_start(at[:, u].rearrange("p j t -> p (j t)"),
                                act_dram[:, bass.ds(g * GRP, GRP), :].rearrange("p j t -> p (j t)")
                                ).then_inc(wa_in[u], 16)

                def rows(g):
                    for jj in range(GRP):
                        e.wait_ge(vlo_done, g * GRP + jj + 1)
                        e.dma_start(raw[:, jj % 2], v_v[:, bass.ds(g * GRP + jj, 1)].rearrange("p a d -> p (a d)")
                                    ).then_inc(v_in[jj % 2], 16)

                def first():
                    weights(0, 0)
                    rows(0)

                def body(g, u, last):
                    if not last:
                        weights(g + 1, 1 - u)
                        rows(g + 1)

                in_pairs(e, first, body)

            @block.scalar
            def _(e):
                def v_hi(g, u, jj):
                    e.wait_ge(v_in[jj % 2], (g * 2 + jj // 2 + 1) * 16)
                    e.wait_ge(summed, g * NT + NT)
                    nc.scalar.activation(vhi[:, u, jj], raw[:, jj % 2], ACT.Copy).then_inc(vhi_done, 1)

                def p_hi(g, t):
                    e.wait_ge(prod_done, g * NT + t + 1 + 2 * NT)
                    e.wait_ge(summed, g * NT + t + 2 * NT - 2)
                    nc.scalar.activation(phi[:, t % 3], prod[:, t % 3], ACT.Copy).then_inc(phi_done, 1)

                def first():
                    for jj in range(GRP):
                        v_hi(0, 0, jj)
                    p_hi(0, 0)
                    p_hi(0, 1)

                def body(g, u, last):
                    for t in range(NT):
                        if t + 2 < NT or not last:
                            p_hi(g + (t + 2) // NT, (t + 2) % NT)
                        if t in V_TILES and not last:
                            v_hi(g + 1, 1 - u, V_TILES[t])

                in_pairs(e, first, body)

            @block.vector
            def _(e):
                v = nc.vector
                v.sem_inc(vlo_done, 2)
                v.sem_inc(prod_done, 2 * NT)
                v.sem_inc(added, 3)

                def v_lo(g, u, jj):
                    e.wait_ge(vhi_done, g * GRP + jj + 1)
                    v.tensor_tensor(vlo[:, u, jj], raw[:, jj % 2], vhi[:, u, jj].bitcast(F32),
                                    ALU.subtract).then_inc(vlo_done, 1)

                def product(g, u, t):
                    e.wait_ge(wa_in[u], (g // 2 if isinstance(g, int) else g // 2) * 32 + 32)
                    e.wait_ge(summed, g * NT + t + 2 * NT - 2)
                    w = wt[:, u, 4 * t:4 * t + 4].rearrange("p s j t -> p j s t")
                    x = at[:, u, :, t * 128:(t + 1) * 128].rearrange("p j (s t) -> p j s t", t=SUB)
                    v.tensor_tensor(prod[:, t % 3].rearrange("p j (s t) -> p j s t", t=SUB), w, x,
                                    ALU.mult).then_inc(prod_done, 1)

                def p_lo(g, t):
                    e.wait_ge(phi_done, g * NT + t + 1)
                    v.tensor_tensor(plo[:, t % 3], prod[:, t % 3], phi[:, t % 3].bitcast(F32),
                                    ALU.subtract).then_inc(plo_done, 1)

                def add(g, t):
                    e.wait_ge(summed, g * NT + t + 1 + 2 * NT)
                    e.wait_ge(added, g * NT + t + 1)
                    v.tensor_tensor(P.h[:, t], po[:, t % 3], P.h[:, t], ALU.add).then_inc(added, 1)

                def first():
                    for jj in range(GRP):
                        v_lo(0, 0, jj)
                    for t in range(2):
                        product(0, 0, t)
                        p_lo(0, t)

                def body(g, u, last):
                    for t in range(NT):
                        more = t + 2 < NT or not last
                        ng, nt = g + (t + 2) // NT, (t + 2) % NT
                        nu = u if t + 2 < NT else 1 - u
                        if more:
                            product(ng, nu, nt)
                        if t in V_TILES and not last:
                            v_lo(g + 1, 1 - u, V_TILES[t])
                        if more:
                            p_lo(ng, nt)
                        add(g, t)

                in_pairs(e, first, body)

            @block.tensor
            def _(e):
                nc.tensor.sem_inc(summed, 2 * NT)

                def body(g, u, last):
                    e.wait_ge(vlo_done, g * GRP + GRP + 2)
                    for t in range(NT):
                        e.wait_ge(plo_done, g * NT + t + 1)
                        e.wait_ge(added, g * NT + t + 1)
                        for q in range(2):
                            cols = slice(512 * q, 512 * q + 512)
                            for jj in range(GRP):
                                mm = three_passes(nc, po[:, t % 3, cols], (phi[:, t % 3, jj], plo[:, t % 3, jj]),
                                                  (vhi[:, u, jj, cols], vlo[:, u, jj, cols]),
                                                  jj == 0, jj == GRP - 1)
                        mm.then_inc(summed, 1)

                in_pairs(e, lambda: None, body)


def input_embedding(P, xhi, xlo):
    nc, a = P.nc, P.a
    PK = a["w_ple"].shape[1] // 128
    wg_v = a["w_ple_gate"][0].rearrange("(k p) c -> p k c", p=128)
    wp_v = a["w_ple"][0].rearrange("(k p) c -> p k c", p=128)
    p_rows = a["p_prompt"][0, 0].rearrange("(t p) c -> p t c", p=128)
    s_rows = a["p_sample"][0].rearrange("b s c -> (b s) c")
    with ExitStack() as ctx:
        def sb(n, shape, d=F32):
            return ctx.enter_context(nc.sbuf_tensor(f"ie_{n}", shape, d))
        s = lambda n: ctx.enter_context(nc.semaphore(f"ie_{n}"))
        HALF = D // 2
        NW_ = 2 * (KC + PK)
        raw = sb("raw", [128, 2, HALF])
        whi, wlo = sb("whi", [128, KC + PK, HALF], F32R), sb("wlo", [128, KC + PK, HALF], F32R)
        ptok = sb("ptok", [128, NT, PK * 128])
        phi, plo = sb("phi", [128, PK, T], F32R), sb("plo", [128, PK, T], F32R)
        gate = sb("gate", [128, 2, HALF])
        stat, rstd = sb("stat", [128, NT]), sb("rstd", [128, NT])
        gbc = sb("gbc", [128, D])
        pt = ctx.enter_context(nc.psum_tensor("ie_pt", [128, 2, 512], F32))
        pg = ctx.enter_context(nc.psum_tensor("ie_pg", [128, 2, 512], F32))
        pp = ctx.enter_context(nc.psum_tensor("ie_pp", [128, 2, 512], F32))
        w_in = [s(f"w_in{u}") for u in range(2)]
        (p_in, p_t, phi_done, plo_done, whi_done, wlo_done, summed, gated, mixed, added, squared, meaned, rooted,
         rstd_ready, out_ready, stored, half_used) = map(s, (
             "p_in", "p_t", "phi", "plo", "whi", "wlo", "summed", "gated", "mixed", "added", "squared", "meaned",
             "rooted", "rstd", "out", "stored", "half_used"))
        NB = KC + PK
        with nc.Block() as block:
            @block.sync
            def _(e):
                e.dma_start(ptok[:, 0:NPT], p_rows).then_inc(p_in, 16)
                e.dma_start(ptok[:, NPT], s_rows).then_inc(p_in, 16)
                e.dma_start(gbc[:], a["g_final"].rearrange("(a n) -> a n", a=1).broadcast_to([128, D])
                            ).then_inc(p_in, 16)
                for q in range(2):
                    cols = slice(HALF * q, HALF * q + HALF)
                    for b in range(NB):
                        n = q * NB + b
                        if n >= 2:
                            e.wait_ge(wlo_done, n - 1)
                        src = wg_v[:, b, cols] if b < KC else wp_v[:, b - KC, cols]
                        e.dma_start(raw[:, n % 2], src).then_inc(w_in[n % 2], 16)
                yp = P.out["y_p"][0].rearrange("(t p) d -> p t d", p=128)
                ys = P.out["y_s"].rearrange("b s d -> (b s) d")
                for t in range(NT):
                    e.wait_ge(out_ready, t + 1)
                    e.dma_start(yp[:, t] if t < NPT else ys, P.h[:, t]).then_inc(stored, 16)
                e.wait_ge(stored, NT * 16)

            def w_split(e, q, engine):
                for b in range(NB):
                    n = q * NB + b
                    if engine == "act":
                        e.wait_ge(w_in[n % 2], (n // 2 + 1) * 16)
                        nc.scalar.activation(whi[:, b], raw[:, n % 2], ACT.Copy).then_inc(whi_done, 1)
                    else:
                        e.wait_ge(whi_done, n + 1)
                        nc.vector.tensor_tensor(wlo[:, b], raw[:, n % 2], whi[:, b].bitcast(F32),
                                                ALU.subtract).then_inc(wlo_done, 1)

            @block.scalar
            def _(e):
                w_split(e, 0, "act")
                for t in range(NT):
                    e.wait_ge(p_t, t + 1)
                    nc.scalar.activation(phi[:, :, t * 128:(t + 1) * 128],
                                         pt[:, t % 2, 0:PK * 128].rearrange("p (k n) -> p k n", k=PK),
                                         ACT.Copy).then_inc(phi_done, 1)
                for q in range(2):
                    if q == 1:
                        e.wait_ge(summed, NT)
                        w_split(e, 1, "act")
                    for t in range(NT):
                        n = q * NT + t
                        e.wait_ge(summed, n + 1)
                        if n >= 2:
                            e.wait_ge(added, n - 1)
                        nc.scalar.activation(gate[:, n % 2], pg[:, n % 2], ACT.Sigmoid).then_inc(gated, 1)
                for t in range(NT):
                    e.wait_ge(added, NT + t + 1)
                    if t >= 1:
                        e.wait_ge(squared, t)
                    nc.scalar.activation(raw[:].rearrange("p a n -> p (a n)"), P.h[:, t], ACT.Square,
                                         accum_out=stat[:, t:t + 1]).then_inc(squared, 1)
                e.wait_ge(meaned, 1)
                nc.scalar.activation(rstd[:], stat[:], ACT.Sqrt).then_inc(rooted, 1)

            @block.vector
            def _(e):
                v = nc.vector
                w_split(e, 0, "dve")
                for t in range(NT):
                    e.wait_ge(phi_done, t + 1)
                    cols = slice(t * 128, (t + 1) * 128)
                    v.tensor_tensor(plo[:, :, cols], pt[:, t % 2, 0:PK * 128].rearrange("p (k n) -> p k n", k=PK),
                                    phi[:, :, cols].bitcast(F32), ALU.subtract).then_inc(plo_done, 1)
                for q in range(2):
                    cols = slice(HALF * q, HALF * q + HALF)
                    for t in range(NT):
                        n = q * NT + t
                        e.wait_ge(gated, n + 1)
                        v.tensor_tensor(gate[:, n % 2], pp[:, n % 2], gate[:, n % 2], ALU.mult).then_inc(mixed, 1)
                        e.wait_ge(mixed, n + 1)
                        v.tensor_tensor(P.h[:, t, cols], P.h[:, t, cols], gate[:, n % 2], ALU.add).then_inc(added, 1)
                    if q == 0:
                        w_split(e, 1, "dve")
                e.wait_ge(squared, NT)
                v.tensor_scalar(stat[:], stat[:], 1.0 / D, EPS, ALU.mult, ALU.add).then_inc(meaned, 1)
                e.wait_ge(rooted, 1)
                v.reciprocal(rstd[:], rstd[:]).then_inc(rstd_ready, 1)
                e.wait_ge(rstd_ready, 1)
                e.wait_ge(p_in, 48)
                e.wait_ge(added, 2 * NT)
                for t in range(NT):
                    v.scalar_tensor_tensor(out=P.h[:, t], in0=P.h[:, t], scalar=rstd[:, t:t + 1], in1=gbc[:],
                                           op0=ALU.mult, op1=ALU.mult).then_inc(out_ready, 1)

            @block.tensor
            def _(e):
                e.wait_ge(p_in, 48)
                for t in range(NT):
                    if t >= 2:
                        e.wait_ge(plo_done, t - 1)
                    for k in range(PK):
                        last = nc.tensor.transpose(pt[:, t % 2, k * 128:(k + 1) * 128],
                                                   ptok[:, t, k * 128:(k + 1) * 128], P.ident[:])
                    last.then_inc(p_t, 1)
                e.wait_ge(plo_done, NT)
                for q in range(2):
                    e.wait_ge(wlo_done, (q + 1) * NB)
                    for t in range(NT):
                        n = q * NT + t
                        if n >= 2:
                            e.wait_ge(mixed, n - 1)
                        cols = slice(t * 128, (t + 1) * 128)
                        for k in range(KC):
                            three_passes(nc, pg[:, n % 2], (xhi[:, k, cols], xlo[:, k, cols]),
                                         (whi[:, k], wlo[:, k]), k == 0, k == KC - 1)
                        for k in range(PK):
                            last = three_passes(nc, pp[:, n % 2], (phi[:, k, cols], plo[:, k, cols]),
                                                (whi[:, KC + k], wlo[:, KC + k]), k == 0, k == PK - 1)
                        last.then_inc(summed, 1)


def build(nc, a, out):
    with ExitStack() as ctx:
        P = Program(nc, a, out, ctx)
        scratch = lambda n, shape: nc.dram_tensor(n, shape, F32, kind="Internal").ap()
        z_dram = scratch("z_scratch", (a["w_in"].shape[2] // 128, 128, T))
        w_dram = scratch("w_scratch", (128, NSUB, NK, SUB))
        act_dram = scratch("act_scratch", (128, NK, T))
        load_and_constants(P)

        def split_x():
            c = ExitStack()
            n = len(splits)
            splits.append(c)
            return c, *(c.enter_context(nc.sbuf_tensor(f"x{part}{n}", [128, KC, T], F32R)) for part in ("hi", "lo"))

        splits = []
        c, xhi, xlo = split_x()
        with c:
            norm_transpose(P, "mix", a["g_mix"][0], xhi, xlo)
            project_inputs(P, xhi, xlo, z_dram)
        with nc.sbuf_tensor("cat", [128, KC, T], F32) as cat:
            mixers(P, z_dram, cat)
            output_projection(P, cat)
        c, xhi, xlo = split_x()
        with c:
            norm_transpose(P, "ffn", a["g_ffn"][0], xhi, xlo)
            with ExitStack() as r:
                pick_i, pick_j, glo = (r.enter_context(nc.sbuf_tensor(n, [128, T], F32))
                                       for n in ("pick_i", "pick_j", "glo"))
                ghi = r.enter_context(nc.sbuf_tensor("ghi", [128, T], F32R))
                with (nc.sbuf_tensor("best_scores", [128, NT, HP, K], F32) as sv,
                      nc.sbuf_tensor("best_subkeys", [128, NT, HP, K], U32) as si):
                    route_scores(P, xhi, xlo, sv, si)
                    route_picks(P, sv, si, pick_i, pick_j, ghi, glo)
                expert_weights(P, pick_i, pick_j, ghi, glo, w_dram)
            expert_activations(P, xhi, xlo, act_dram)
        expert_outputs(P, w_dram, act_dram)
        c, xhi, xlo = split_x()
        with c:
            norm_transpose(P, "ple", a["g_ple"][0], xhi, xlo)
            input_embedding(P, xhi, xlo)


_INS = ("x_prompt", "x_sample", "state_hgrn", "state_rglru", "state_conv", "p_prompt", "p_sample", "g_mix", "w_in",
        "lower_bounds", "g_hgrn_norm", "conv_w", "conv_b", "w_rg_a", "b_rg_a", "w_rg_x", "b_rg_x", "lambda_rg",
        "w_out", "g_ffn", "w_peer_q", "peer_keys", "peer_u", "peer_v", "g_ple", "w_ple_gate", "w_ple", "g_final")
_OUTS = (("y_p", (1, SEQ, D)), ("y_s", (DB, DS, D)), ("hgrn_p", (1, 1, HA, 128, 128)), ("rglru_p", (1, 1, 512)),
         ("conv_p", (1, 1, 3, 512)), ("hgrn_s", (1, DB, HA, 128, 128)), ("rglru_s", (1, DB, 512)),
         ("conv_s", (1, DB, 3, 512)))


def kernel(**inputs):
    import concourse.bacc as bacc
    from concourse.bass_utils import run_bass_kernel_spmd

    nc = bacc.Bacc("TRN2", target_bir_lowering=False, num_devices=1)
    arrays, a, out = {}, {}, {}
    for name in _INS:
        x = np.ascontiguousarray(inputs[name])
        arrays[f"in_{name}"] = x
        a[name] = nc.dram_tensor(f"in_{name}", x.shape, mybir.dt.from_np(x.dtype), kind="ExternalInput").ap()
    for name, shape in _OUTS:
        out[name] = nc.dram_tensor(f"out_{name}", shape, F32, kind="ExternalOutput").ap()
    build(nc, a, out)
    r = run_bass_kernel_spmd(nc, [arrays], core_ids=[0])
    return tuple(r.results[0][f"out_{name}"] for name, _ in _OUTS)
```

```python
import numpy as np
from contextlib import ExitStack

import concourse.bass as bass
from concourse import mybir

F32 = mybir.dt.float32
F32R = mybir.dt.float32r
F16 = mybir.dt.float16
U32 = mybir.dt.uint32
I32 = mybir.dt.int32
ALU = mybir.AluOpType
ACT = mybir.ActivationFunctionType
AX = mybir.AxisListType

D = 1024
KC = D // 128
SEQ, DB, DS = 1024, 8, 16
T = SEQ + DB * DS
NT = T // 128
NPT = SEQ // 128
CH = 64
NCH = SEQ // CH
HA = 4
HP = 16
PH = 8
K = 16
NK = 128
NN, NW = 3, T // 3
EPS = 1e-6
LOWEST = -3.0e38


class Order:

    def __init__(self, eng, sem, per=None, i=0):
        self.eng, self.sem, self.per, self.i, self.n = eng, sem, per, i, 0

    def did(self, ins):
        ins.then_inc(self.sem, 1)
        self.n += 1
        return self.value()

    def value(self):
        return self.n if self.per is None else self.i * self.per + self.n

    def settle(self):
        self.eng.wait_ge(self.sem, self.value())

    def close(self):
        assert self.per is None or self.n == self.per, (self.n, self.per)


class Program:

    def __init__(self, nc, a, out, ctx):
        self.nc, self.a, self.out, self.ctx = nc, a, out, ctx
        self.h = ctx.enter_context(nc.sbuf_tensor("h", [128, NT, D], F32))
        self.ident = ctx.enter_context(nc.sbuf_tensor("ident", [128, 128], F32))
        self.apart = None


def wait_apart(e, P, sem, value):
    e.wait_ge(sem, value)
    e.sem_inc(P.apart, 1)


def token_rows(x_prompt, x_sample):
    return x_prompt[0].rearrange("(t p) d -> p t d", p=128), x_sample.rearrange("b s d -> (b s) d")


def column(vec, first, n=128):
    return vec[first:first + n].rearrange("(p a) -> p a", a=1)


def load_and_constants(P):
    nc, a = P.nc, P.a
    loaded, zeroed, made = (P.ctx.enter_context(nc.semaphore(x)) for x in ("h_loaded", "ident_zeroed", "ident_made"))
    P.apart = P.ctx.enter_context(nc.semaphore("apart"))
    with nc.Block() as block:
        @block.sync
        def _(e):
            rows_p, rows_s = token_rows(a["x_prompt"], a["x_sample"])
            e.dma_start(P.h[:, 0:NPT, :], rows_p).then_inc(loaded, 16)
            e.dma_start(P.h[:, NPT, :], rows_s).then_inc(loaded, 16)
            e.wait_ge(loaded, 32)

        @block.gpsimd
        def _(e):
            nc.gpsimd.memset(P.ident[:], 0.0).then_inc(zeroed, 1)
            e.wait_ge(zeroed, 1)
            nc.gpsimd.affine_select(out=P.ident[:], in_=P.ident[:], compare_op=ALU.not_equal, fill=1.0,
                                    base=0, pattern=[[-1, 128]], channel_multiplier=1).then_inc(made, 1)


def norm_transpose(P, name, gain, xhi, xlo):
    nc = P.nc
    with ExitStack() as ctx:
        sb = lambda n, s, d=F32: ctx.enter_context(nc.sbuf_tensor(f"{name}_{n}", s, d))
        gbc = sb("gain", [128, D])
        junk = sb("squares", [128, 2, D])
        stat = sb("stat", [128, NT])
        rstd = sb("rstd", [128, NT])
        un = sb("normed", [128, 3, D])
        pt = ctx.enter_context(nc.psum_tensor(f"{name}_pt", [128, 3, KC, 128], F32))
        s = lambda n: ctx.enter_context(nc.semaphore(f"{name}_{n}"))
        gain_in, squared, mean_ready, rooted, rstd_ready = map(s, ("gain_in", "squared", "mean", "rooted", "rstd"))
        normed, transposed, hi_done, lo_done = map(s, ("normed", "transposed", "hi", "lo"))
        with nc.Block() as block:
            @block.sync
            def _(e):
                e.dma_start(gbc[:], gain.rearrange("(a n) -> a n", a=1).broadcast_to([128, D])).then_inc(gain_in, 16)

            @block.scalar
            def _(e):
                for t in range(NT):
                    if t >= 2:
                        e.wait_ge(squared, t - 1)
                    nc.scalar.activation(junk[:, t % 2], P.h[:, t], ACT.Square,
                                         accum_out=stat[:, t:t + 1]).then_inc(squared, 1)
                e.wait_ge(mean_ready, 1)
                nc.scalar.activation(rstd[:], stat[:], ACT.Sqrt).then_inc(rooted, 1)
                with e.Fori(0, NT // 3) as i:
                    for u in range(3):
                        e.wait_ge(transposed, i * 3 + u + 1)
                        nc.scalar.activation(xhi[:, :, bass.ds((i * 3 + u) * 128, 128)], pt[:, u],
                                             ACT.Copy).then_inc(hi_done, 1)

            @block.vector
            def _(e):
                e.wait_ge(squared, NT)
                nc.vector.tensor_scalar(stat[:], stat[:], 1.0 / D, EPS, ALU.mult, ALU.add).then_inc(mean_ready, 1)
                e.wait_ge(rooted, 1)
                nc.vector.reciprocal(rstd[:], rstd[:]).then_inc(rstd_ready, 1)
                e.wait_ge(rstd_ready, 1)
                e.wait_ge(gain_in, 16)
                nc.vector.sem_inc(lo_done, 3)
                with e.Fori(0, NT // 3) as i:
                    for u in range(3):
                        e.wait_ge(lo_done, i * 3 + u + 1)
                        nc.vector.scalar_tensor_tensor(
                            out=un[:, u], in0=P.h[:, bass.ds(i * 3 + u, 1), :].rearrange("p a d -> p (a d)"),
                            scalar=rstd[:, bass.ds(i * 3 + u, 1)], in1=gbc[:],
                            op0=ALU.mult, op1=ALU.mult).then_inc(normed, 1)
                    for u in range(3):
                        e.wait_ge(hi_done, i * 3 + u + 1)
                        cols = bass.ds((i * 3 + u) * 128, 128)
                        nc.vector.tensor_tensor(xlo[:, :, cols], pt[:, u], xhi[:, :, cols].bitcast(F32),
                                                ALU.subtract).then_inc(lo_done, 1)

            @block.tensor
            def _(e):
                with e.Fori(0, NT // 3) as i:
                    for u in range(3):
                        e.wait_ge(normed, i * 3 + u + 1)
                        e.wait_ge(lo_done, i * 3 + u + 1)
                        for k in range(KC):
                            last = nc.tensor.transpose(pt[:, u, k], un[:, u, k * 128:(k + 1) * 128], P.ident[:])
                        last.then_inc(transposed, 1)


def three_passes(nc, out, w, x, first, last):
    nc.tensor.matmul(out, w[0], x[0], start=first, stop=False)
    nc.tensor.matmul(out, w[0], x[1], start=False, stop=False)
    return nc.tensor.matmul(out, w[1], x[0], start=False, stop=last)


def project_inputs(P, xhi, xlo, z_dram):
    nc = P.nc
    NB = P.a["w_in"].shape[2] // 128
    w_v = P.a["w_in"][0].rearrange("(k p) c -> p k c", p=128)
    with ExitStack() as ctx:
        raw = ctx.enter_context(nc.sbuf_tensor("win_raw", [128, 2, KC, 128], F32))
        whi = ctx.enter_context(nc.sbuf_tensor("win_hi", [128, 2, KC, 128], F32R))
        wlo = ctx.enter_context(nc.sbuf_tensor("win_lo", [128, 2, KC, 128], F32R))
        zst = ctx.enter_context(nc.sbuf_tensor("z_stage", [128, 2, T], F32))
        pz = ctx.enter_context(nc.psum_tensor("pz", [128, NN, 512], F32))
        s = lambda n: ctx.enter_context(nc.semaphore(n))
        w_in = [s(f"win_in{u}") for u in range(2)]
        z_out = [s(f"z_out{u}") for u in range(2)]
        hi_done, lo_done, mm_done, z_ready = map(s, ("win_hi_done", "win_lo_done", "z_summed", "z_ready"))
        with nc.Block() as block:
            @block.sync
            def _(e):
                nc.sync.sem_inc(z_out[0], 16)
                nc.sync.sem_inc(z_out[1], 16)

                def load(i, u):
                    e.wait_ge(lo_done, i * 2 + u + 1)
                    e.dma_start(raw[:, u], w_v[:, :, bass.ds((i * 2 + u) * 128, 128)]).then_inc(w_in[u], 16)

                def store(i, u):
                    e.wait_ge(z_ready, (i * 2 + u + 2) * NN)
                    e.dma_start(z_dram[bass.ds(i * 2 + u, 1)].rearrange("a p t -> p (a t)"),
                                zst[:, u]).then_inc(z_out[u], 16)

                load(0, 0)
                load(0, 1)
                with e.Fori(0, NB // 2 - 1) as i:
                    load(i + 1, 0)
                    store(i, 0)
                    load(i + 1, 1)
                    store(i, 1)
                store(NB // 2 - 1, 0)
                store(NB // 2 - 1, 1)
                e.wait_ge(z_out[0], (NB // 2 + 1) * 16)
                e.wait_ge(z_out[1], (NB // 2 + 1) * 16)

            @block.scalar
            def _(e):
                nc.scalar.sem_inc(z_ready, NN)

                def hi(i, u):
                    e.wait_ge(w_in[u], (i + 1) * 16)
                    e.wait_ge(mm_done, (i * 2 + u + 1) * NN)
                    nc.scalar.activation(whi[:, u], raw[:, u], ACT.Copy).then_inc(hi_done, 1)

                def evacuate(i, u):
                    e.wait_ge(z_out[u], (i + 1) * 16)
                    for n in range(NN):
                        e.wait_ge(mm_done, (i * 2 + u + 2) * NN + n + 1)
                        nc.scalar.activation(zst[:, u, n * NW:(n + 1) * NW], pz[:, n, 0:NW],
                                             ACT.Copy).then_inc(z_ready, 1)

                hi(0, 0)
                with e.Fori(0, NB // 2 - 1) as i:
                    hi(i, 1)
                    evacuate(i, 0)
                    hi(i + 1, 0)
                    evacuate(i, 1)
                last = NB // 2 - 1
                hi(last, 1)
                evacuate(last, 0)
                evacuate(last, 1)

            @block.vector
            def _(e):
                nc.vector.sem_inc(lo_done, 2)
                with e.Fori(0, NB // 2) as i:
                    for u in range(2):
                        e.wait_ge(hi_done, i * 2 + u + 1)
                        nc.vector.tensor_tensor(wlo[:, u], raw[:, u], whi[:, u].bitcast(F32),
                                                ALU.subtract).then_inc(lo_done, 1)

            @block.tensor
            def _(e):
                nc.tensor.sem_inc(mm_done, 2 * NN)
                with e.Fori(0, NB // 2) as i:
                    for u in range(2):
                        e.wait_ge(lo_done, i * 2 + u + 3)
                        for n in range(NN):
                            e.wait_ge(z_ready, (i * 2 + u) * NN + n + 1)
                            for k in range(KC):
                                mm = three_passes(nc, pz[:, n, 0:NW], (whi[:, u, k], wlo[:, u, k]),
                                                  (xhi[:, k, n * NW:(n + 1) * NW], xlo[:, k, n * NW:(n + 1) * NW]),
                                                  k == 0, k == KC - 1)
                            mm.then_inc(mm_done, 1)


def mixers(P, z_dram, cat):
    nc, a, out = P.nc, P.a, P.out
    with ExitStack() as ctx:
        def sb(n, shape, d=F32):
            return ctx.enter_context(nc.sbuf_tensor(f"mx_{n}", shape, d))
        used = []

        def s(n):
            used.append(nc.alloc_semaphore(f"mx_{n}"))
            return used[-1]


        zq, zf, zv, zg, zy = (sb(n, [128, T]) for n in ("zq", "zf", "zv", "zg", "zy"))
        xp = sb("xp", [128, SEQ + 3])
        xs = sb("xs", [128, DB, DS + 3])
        sf, sq, cum, e1, e2, e3, xc, r, ig = (sb(n, [128, T]) for n in (
            "sf", "sq", "cum", "e1", "e2", "e3", "xc", "r", "ig"))
        scan_mask = sb("scan_mask", [128, T])
        vtok, kdtok, att, on = (sb(n, [128, NT, 128]) for n in ("vtok", "kdtok", "att", "on"))
        states = sb("states", [128, NCH + 1, 128])
        s0 = sb("s0", [128, DB, 128])
        snew = sb("snew", [128, DB, 128])
        vmask = sb("vmask", [128, DB, 128])
        qdz = sb("qdz", [128, DB * (128 + DS)])
        wg = sb("wg", [128, 2, 128])
        rows_in = sb("rows_in", [128, 128])
        cols_out = sb("cols_out", [128, 128])
        rows_out = sb("rows_out", [36, 128])
        mask_p = sb("mask_p", [128, 128])
        mask_s = sb("mask_s", [128, 128])
        bmask = sb("bmask", [128, DB])
        rs = sb("rs", [128, NT])
        NPAR = 12
        LB, LB1, GN, CB, BA, BX, SP8, NSP8 = range(8)
        CW = 8
        par = sb("par", [128, 4, NPAR])
        cur = sb("cur", [128, NPAR])
        lbraw = sb("lbraw", [128, 2, 4])
        tmp = sb("tmp", [128, 6, 4])
        gps = ctx.enter_context(nc.psum_tensor("mx_ps", [128, 8, 512], F32))
        flat = gps[:].rearrange("p b n -> p (b n)")
        ps_v = flat[:, 0:T].rearrange("p (t c) -> p t c", c=128)
        ps_kd = flat[:, 1536:1536 + T].rearrange("p (t c) -> p t c", c=128)
        ps_ds = flat[:, 0:2048].rearrange("p (c n) -> p c n", n=128)
        ds_of = lambda c: ps_ds[:, (c % 2) * (NCH // 2) + c // 2]
        ps_dss = flat[:, 2048:3072].rearrange("p (c n) -> p c n", n=128)
        ps_att, ps_o, ps_ont = ps_v, ps_kd, ps_v
        ps_state = gps[:, 6, 0:128]
        ps_rows = gps[:, 6, 128:256]

        consts, par_in, par_ready = s("consts"), s("par_in"), s("par_ready")
        act_par, dve_par = s("act_par"), s("dve_par")
        with nc.Block() as block:
            @block.sync
            def _(e):
                with nc.allow_non_contiguous_dma(reason="small per-channel vectors"):
                    for j, v in ((GN, a["g_hgrn_norm"]), (CB, a["conv_b"]), (BA, a["b_rg_a"]), (BX, a["b_rg_x"]),
                                 (SP8, a["lambda_rg"])):
                        e.dma_start(par[:, :, j], v[0].rearrange("(i p) -> p i", p=128)).then_inc(par_in, 16)
                    for j in range(4):
                        e.dma_start(par[:, :, CW + j], a["conv_w"][0, j].rearrange("(i p) -> p i", p=128)
                                    ).then_inc(par_in, 16)
                    for j in range(2):
                        e.dma_start(lbraw[:, j], a["lower_bounds"][j].rearrange("(i p) -> p i", p=128)
                                    ).then_inc(par_in, 16)
                    e.wait_ge(par_in, 11 * 16)

            @block.gpsimd
            def _(e):
                o = Order(e, consts)
                for m, value in ((mask_p, 1.0), (mask_s, 1.0), (bmask, 1.0), (scan_mask, 1.0), (att, 0.0), (qdz, 0.0),
                                 (wg, 0.0), (rows_in, 0.0), (cols_out, 0.0)):
                    o.did(nc.gpsimd.memset(m[:], value))
                o.did(nc.gpsimd.memset(states[:, 0], 0.0))
                o.did(nc.gpsimd.memset(xp[:, 0:3], 0.0))
                o.settle()
                for m in (mask_p, mask_s):
                    o.did(nc.gpsimd.affine_select(out=m[:], in_=m[:], compare_op=ALU.is_ge, fill=0.0, base=0,
                                                  pattern=[[1, 128]], channel_multiplier=-1))
                for m, pat in ((bmask[:], [[-DS, DB]]),):
                    o.did(nc.gpsimd.affine_select(out=m, in_=m, compare_op=ALU.is_ge, fill=0.0, base=0,
                                                  pattern=pat, channel_multiplier=1))
                o.did(nc.gpsimd.memset(scan_mask[:, 0:SEQ].rearrange("p (c n) -> p c n", n=CH)[:, :, 0:1], 0.0))
                o.did(nc.gpsimd.memset(scan_mask[:, SEQ:T].rearrange("p (c n) -> p c n", n=DS)[:, :, 0:1], 0.0))
                o.settle()
                o.did(nc.gpsimd.memset(mask_p[0:CH, CH:128], 0.0))
                o.did(nc.gpsimd.affine_select(out=mask_s[:].rearrange("p (b r) -> p b r", r=DS),
                                              in_=mask_s[:].rearrange("p (b r) -> p b r", r=DS),
                                              compare_op=ALU.is_ge, fill=0.0, base=0,
                                              pattern=[[-DS, DB], [0, DS]], channel_multiplier=1))
                o.did(nc.gpsimd.affine_select(out=bmask[:], in_=bmask[:], compare_op=ALU.is_ge, fill=0.0,
                                              base=DS - 1, pattern=[[DS, DB]], channel_multiplier=-1))
                o.settle()

            @block.scalar
            def _(e):
                e.wait_ge(dve_par, 1)
                nc.scalar.activation(tmp[:, 0:2], tmp[:, 0:2], ACT.Exp).then_inc(act_par, 1)
                nc.scalar.activation(tmp[:, 3], tmp[:, 3], ACT.Exp, scale=-1.0).then_inc(act_par, 1)
                e.wait_ge(dve_par, 2)
                nc.scalar.activation(tmp[:, 5], tmp[:, 4], ACT.Ln).then_inc(act_par, 1)

            @block.vector
            def _(e):
                v = nc.vector
                o = Order(e, par_ready)

                def link(ins):
                    o.did(ins)
                    o.settle()

                e.wait_ge(par_in, 11 * 16)
                link(v.tensor_tensor(tmp[:, 2], lbraw[:, 0], lbraw[:, 1], ALU.max))
                link(v.tensor_tensor(tmp[:, 0], lbraw[:, 0], tmp[:, 2], ALU.subtract))
                link(v.tensor_tensor(tmp[:, 1], lbraw[:, 1], tmp[:, 2], ALU.subtract))
                link(v.tensor_scalar(tmp[:, 3], par[:, :, SP8], -1.0, None, ALU.mult))
                v.tensor_tensor(tmp[:, 3], tmp[:, 3], par[:, :, SP8], ALU.max).then_inc(dve_par, 1)
                e.wait_ge(act_par, 2)
                link(v.tensor_tensor(tmp[:, 2], tmp[:, 0], tmp[:, 1], ALU.add))
                link(v.reciprocal(tmp[:, 2], tmp[:, 2]))
                link(v.tensor_tensor(par[:, :, LB], tmp[:, 0], tmp[:, 2], ALU.mult))
                link(v.tensor_scalar(par[:, :, LB1], par[:, :, LB], -1.0, 1.0, ALU.mult, ALU.add))
                v.tensor_scalar(tmp[:, 4], tmp[:, 3], 1.0, None, ALU.add).then_inc(dve_par, 1)
                e.wait_ge(act_par, 3)
                link(v.tensor_scalar(tmp[:, 0], tmp[:, 4], 1.0, None, ALU.is_equal))
                link(v.scalar_tensor_tensor(out=tmp[:, 1], in0=tmp[:, 4], scalar=-1.0, in1=tmp[:, 0],
                                            op0=ALU.add, op1=ALU.add))
                link(v.reciprocal(tmp[:, 1], tmp[:, 1]))
                link(v.tensor_tensor(tmp[:, 5], tmp[:, 5], tmp[:, 0], ALU.add))
                link(v.tensor_tensor(tmp[:, 5], tmp[:, 5], tmp[:, 1], ALU.mult))
                link(v.tensor_tensor(tmp[:, 5], tmp[:, 5], tmp[:, 3], ALU.mult))
                link(v.tensor_scalar(tmp[:, 2], par[:, :, SP8], -1.0, 0.0, ALU.mult, ALU.max))
                link(v.tensor_tensor(tmp[:, 2], tmp[:, 2], tmp[:, 5], ALU.add))
                link(v.tensor_scalar(par[:, :, SP8], tmp[:, 2], 8.0, None, ALU.mult))
                link(v.tensor_scalar(par[:, :, NSP8], tmp[:, 2], -8.0, None, ALU.mult))

        (loaded, stored, cur_ready, all_used, sig_f, sig_q, sig_g, sig_r, sig_i, f_ready, ln_f, cum_ready, dl_ready,
         exp_cum, exp_dl, exp_a, qk_ready, kdec_ready, v_t, kdec_t, v_tok, kdec_tok, vmask_ready, ds_ready, dss_ready,
         st_ready, sn_ready, att_sum, att_ready, qdz_ready, o_sum, o_sq, ms_ready, rms_root, on_ready, on_t,
         state_t, xc_ready, gates, va_ready, sqrt_b, gelu_y, oc_ready, oc_t, rows_ready, self_ok) = (s(n) for n in (
             "loaded", "stored", "cur", "used", "sig_f", "sig_q", "sig_g", "sig_r", "sig_i", "f", "ln_f", "cum", "dl",
             "exp_cum", "exp_dl", "exp_a", "qk", "kdec", "v_t", "kdec_t", "v_tok", "kdec_tok", "vmask", "ds", "dss",
             "st", "sn", "att_sum", "att", "qdz", "o_sum", "o_sq", "ms", "rms_root", "on", "on_t",
             "state_t", "xc", "gates", "va", "sqrt_b", "gelu_y", "oc", "oc_t", "rows", "self"))
        NLOAD, NSTORE = 14, 6
        PROMPT, SAMPLE = slice(0, SEQ), slice(SEQ, T)

        def by(x, n):
            return x.rearrange("p (c n) -> p c n", n=n)

        with nc.Block() as block:
            @block.sync
            def _(e):
                nc.sync.sem_inc(stored, NSTORE * 16)
                with e.Fori(0, 4) as i:
                    e.wait_ge(all_used, i + 1)
                    zsrc = lambda c: z_dram[bass.ds(i + 4 * c, 1)].rearrange("a p t -> p (a t)")
                    for dst, c in ((zf, 1), (zq, 0), (zv, 2), (zg, 3), (zy, 5)):
                        e.dma_start(dst[:], zsrc(c)).then_inc(loaded, 16)
                    e.dma_start(xp[:, 3:], zsrc(4)[:, PROMPT]).then_inc(loaded, 16)
                    e.dma_start(xs[:, :, 3:], by(zsrc(4)[:, SAMPLE], DS)).then_inc(loaded, 16)
                    cols = bass.ds(i * 128, 128)
                    for w, src in ((0, a["w_rg_a"]), (1, a["w_rg_x"])):
                        for q in range(2):
                            e.dma_start(wg[64 * q:64 * q + 64, w, 64 * q:64 * q + 64],
                                        src[0, bass.ds(i * 2 + q, 1)].rearrange("a c d -> c (a d)")
                                        ).then_inc(loaded, 16)
                    e.dma_start(s0[:], a["state_hgrn"][0, :, bass.ds(i, 1)].rearrange("b a d v -> d (b a) v")
                                ).then_inc(loaded, 16)
                    e.dma_start(rows_in[0:24, :], a["state_conv"][0, :, :, cols].rearrange("b j c -> (b j) c")
                                ).then_inc(loaded, 16)
                    e.dma_start(rows_in[24:32, :], a["state_rglru"][0, :, cols]).then_inc(loaded, 16)
                    e.wait_ge(st_ready, i + 1)
                    e.dma_start(out["hgrn_p"][0, 0, bass.ds(i, 1)].rearrange("a d v -> d (a v)"),
                                states[:, NCH]).then_inc(stored, 16)
                    e.wait_ge(sn_ready, i + 1)
                    e.dma_start(out["hgrn_s"][0, :, bass.ds(i, 1)].rearrange("b a d v -> d (b a) v"),
                                snew[:]).then_inc(stored, 16)
                    e.wait_ge(rows_ready, i + 1)
                    e.dma_start(out["conv_p"][0, 0, :, cols], rows_out[0:3, :]).then_inc(stored, 16)
                    e.dma_start(out["conv_s"][0, :, :, cols].rearrange("b j c -> (b j) c"),
                                rows_out[3:27, :]).then_inc(stored, 16)
                    e.dma_start(out["rglru_p"][0, :, cols], rows_out[27:28, :]).then_inc(stored, 16)
                    e.dma_start(out["rglru_s"][0, :, cols], rows_out[28:36, :]).then_inc(stored, 16)
                e.wait_ge(stored, 5 * NSTORE * 16)

            @block.scalar
            def _(e):
                f = nc.scalar.activation
                with e.Fori(0, 4) as i:
                    e.wait_ge(loaded, (i + 1) * NLOAD * 16)
                    e.wait_ge(cur_ready, i + 1)
                    f(sf[:], zf[:], ACT.Sigmoid).then_inc(sig_f, 1)
                    f(sq[:], zq[:], ACT.Sigmoid).then_inc(sig_q, 1)
                    f(e3[:], zg[:], ACT.Sigmoid).then_inc(sig_g, 1)
                    e.wait_ge(gates, i + 1)
                    for dst, at, bias, done in ((r, 0, BA, sig_r), (ig, 3, BX, sig_i)):
                        f(dst[:].rearrange("p (n w) -> p n w", w=NW), gps[:, at:at + 3, 0:NW], ACT.Sigmoid,
                          bias=cur[:, bias:bias + 1]).then_inc(done, 1)
                    e.wait_ge(v_t, i + 1)
                    f(vtok[:], ps_v, ACT.Copy).then_inc(v_tok, 1)
                    e.wait_ge(f_ready, i + 1)
                    f(cum[:], sf[:], ACT.Ln).then_inc(ln_f, 1)
                    e.wait_ge(cum_ready, i + 1)
                    f(e1[:], sf[:], ACT.Exp).then_inc(exp_cum, 1)
                    f(e2[:], sf[:], ACT.Exp, scale=-1.0).then_inc(exp_cum, 1)
                    e.wait_ge(dl_ready, i + 1)
                    f(e3[:], cum[:], ACT.Exp).then_inc(exp_dl, 1)
                    e.wait_ge(sig_r, i + 1)
                    e.wait_ge(exp_cum, i * 2 + 2)
                    f(sf[:], r[:], ACT.Tanh, scale=cur[:, SP8:SP8 + 1]).then_inc(exp_a, 1)
                    e.wait_ge(exp_a, i * 2 + 1)
                    f(r[:], r[:], ACT.Exp, scale=cur[:, NSP8:NSP8 + 1]).then_inc(exp_a, 1)
                    e.wait_ge(va_ready, i + 1)
                    f(sf[:], sf[:], ACT.Sqrt).then_inc(sqrt_b, 1)
                    e.wait_ge(o_sum, i + 1)
                    f(cum[:].rearrange("p (t c) -> p t c", c=128), ps_o, ACT.Square).then_inc(o_sq, 1)
                    e.wait_ge(ms_ready, i + 1)
                    f(rs[:], rs[:], ACT.Sqrt).then_inc(rms_root, 1)
                    f(zy[:], zy[:], ACT.Gelu_apprx_tanh).then_inc(gelu_y, 1)

            @block.vector
            def _(e):
                v = nc.vector
                nc.vector.sem_inc(all_used, 1)
                PER = 41
                with e.Fori(0, 4) as i:
                    o = Order(e, self_ok, PER, i)

                    def link(ins):
                        o.did(ins)
                        o.settle()

                    e.wait_ge(all_used, i + 1)
                    v.tensor_copy(cur[:], par[:, bass.ds(i, 1)].rearrange("p a n -> p (a n)")).then_inc(cur_ready, 1)
                    e.wait_ge(cur_ready, i + 1)
                    e.wait_ge(state_t, i + 1)
                    link(v.tensor_copy(xs[:, :, 0:3], ps_state[:, 0:24].rearrange("p (b j) -> p b j", j=3)))
                    link(v.tensor_scalar(xc[:, PROMPT], xp[:, 0:SEQ], cur[:, CW:CW + 1], cur[:, CB:CB + 1],
                                         ALU.mult, ALU.add))
                    link(v.tensor_scalar(by(xc[:, SAMPLE], DS), xs[:, :, 0:DS], cur[:, CW:CW + 1],
                                         cur[:, CB:CB + 1], ALU.mult, ALU.add))
                    for j in range(1, 4):
                        tap = cur[:, CW + j:CW + j + 1]
                        link(v.scalar_tensor_tensor(out=xc[:, PROMPT], in0=xp[:, j:j + SEQ], scalar=tap,
                                                    in1=xc[:, PROMPT], op0=ALU.mult, op1=ALU.add))
                        ins = v.scalar_tensor_tensor(out=by(xc[:, SAMPLE], DS), in0=xs[:, :, j:j + DS], scalar=tap,
                                                     in1=by(xc[:, SAMPLE], DS), op0=ALU.mult, op1=ALU.add)
                        if j < 3:
                            link(ins)
                        else:
                            ins.then_inc(xc_ready, 1)
                    e.wait_ge(xc_ready, i + 1)
                    e.wait_ge(sig_f, i + 1)
                    v.tensor_scalar(sf[:], sf[:], cur[:, LB1:LB1 + 1], cur[:, LB:LB + 1],
                                    ALU.mult, ALU.add).then_inc(f_ready, 1)
                    e.wait_ge(f_ready, i + 1)
                    link(v.tensor_scalar(zf[:], sf[:], -1.0, 1.0, ALU.mult, ALU.add))
                    e.wait_ge(sig_q, i + 1)
                    link(v.tensor_tensor(zq[:], zq[:], sq[:], ALU.mult))
                    e.wait_ge(sig_g, i + 1)
                    link(v.tensor_tensor(zg[:], zg[:], e3[:], ALU.mult))
                    e.wait_ge(ln_f, i + 1)
                    v.tensor_tensor_scan(sf[:], scan_mask[:], cum[:], 0.0, ALU.mult, ALU.add).then_inc(cum_ready, 1)
                    e.wait_ge(cum_ready, i + 1)
                    for cols, n in ((PROMPT, CH), (SAMPLE, DS)):
                        c = by(sf[:, cols], n)
                        ins = v.tensor_tensor(by(cum[:, cols], n), c[:, :, n - 1:n].broadcast_to(list(c.shape)), c,
                                              ALU.subtract)
                        if n == DS:
                            ins.then_inc(dl_ready, 1)
                        else:
                            o.did(ins)
                    e.wait_ge(exp_cum, i * 2 + 2)
                    o.did(v.tensor_tensor(zq[:], zq[:], e1[:], ALU.mult))
                    v.tensor_tensor(e2[:], zf[:], e2[:], ALU.mult).then_inc(qk_ready, 1)
                    e.wait_ge(exp_dl, i + 1)
                    v.tensor_tensor(e3[:], zf[:], e3[:], ALU.mult).then_inc(kdec_ready, 1)
                    o.settle()
                    v.tensor_copy(by(qdz[:], 128 + DS)[:, :, 0:DS], by(zq[:, SAMPLE], DS)).then_inc(qdz_ready, 1)
                    e.wait_ge(v_tok, i + 1)
                    for b in range(DB):
                        ins = v.tensor_scalar(vmask[:, b], vtok[:, NPT], bmask[:, b:b + 1], None, ALU.mult)
                    ins.then_inc(vmask_ready, 1)
                    e.wait_ge(kdec_t, i + 1)
                    v.tensor_copy(kdtok[:], ps_kd).then_inc(kdec_tok, 1)
                    e.wait_ge(ds_ready, i + 1)
                    e.wait_ge(stored, (i + 1) * NSTORE * 16)
                    for c in range(NCH):
                        at = (c + 1) * CH - 1
                        ins = v.scalar_tensor_tensor(out=states[:, c + 1], in0=states[:, c], scalar=e1[:, at:at + 1],
                                                     in1=ds_of(c), op0=ALU.mult, op1=ALU.add)
                        if c < NCH - 1:
                            link(ins)
                        else:
                            ins.then_inc(st_ready, 1)
                    e.wait_ge(dss_ready, i + 1)
                    for b in range(DB):
                        at = SEQ + (b + 1) * DS - 1
                        ins = v.scalar_tensor_tensor(out=snew[:, b], in0=s0[:, b], scalar=e1[:, at:at + 1],
                                                     in1=ps_dss[:, b], op0=ALU.mult, op1=ALU.add)
                    ins.then_inc(sn_ready, 1)
                    wait_apart(e, P, att_sum, i + 1)
                    v.copy_predicated(att[:, 0:NPT], mask_p[:].bitcast(I32).rearrange("p (a n) -> p a n", a=1)
                                      .broadcast_to([128, NPT, 128]), ps_att[:, 0:NPT])
                    v.copy_predicated(att[:, NPT], mask_s[:].bitcast(I32), ps_att[:, NPT]).then_inc(att_ready, 1)
                    e.wait_ge(exp_a, i * 2 + 2)
                    link(v.tensor_tensor(cum[:], r[:], r[:], ALU.mult))
                    v.scalar_tensor_tensor(out=sf[:], in0=cum[:], scalar=1.0, in1=sf[:],
                                           op0=ALU.add, op1=ALU.mult).then_inc(va_ready, 1)
                    e.wait_ge(sig_i, i + 1)
                    link(v.tensor_tensor(ig[:], ig[:], xc[:], ALU.mult))
                    e.wait_ge(sqrt_b, i + 1)
                    link(v.tensor_tensor(ig[:], ig[:], sf[:], ALU.mult))
                    first_a, first_b = by(r[:, SAMPLE], DS)[:, :, 0], by(ig[:, SAMPLE], DS)[:, :, 0]
                    link(v.tensor_tensor(e3[:, 0:DB], first_a, ps_state[:, 24:32], ALU.mult))
                    link(v.tensor_tensor(first_b, first_b, e3[:, 0:DB], ALU.add))
                    link(v.memset(first_a, 0.0))
                    link(v.tensor_tensor_scan(xc[:], r[:], ig[:], 0.0, ALU.mult, ALU.add))
                    o.did(v.tensor_copy(cols_out[:, 0:3], xp[:, SEQ:SEQ + 3]))
                    o.did(v.tensor_copy(cols_out[:, 3:27].rearrange("p (b j) -> p b j", j=3), xs[:, :, DS:DS + 3]))
                    o.did(v.tensor_copy(cols_out[:, 27:28], xc[:, SEQ - 1:SEQ]))
                    v.tensor_copy(cols_out[:, 28:36], by(xc[:, SAMPLE], DS)[:, :, DS - 1]).then_inc(oc_ready, 1)
                    e.wait_ge(o_sq, i + 1)
                    link(v.tensor_reduce(rs[:], cum[:].rearrange("p (t c) -> p t c", c=128), AX.X, ALU.add))
                    v.tensor_scalar(rs[:], rs[:], 1.0 / 128, EPS, ALU.mult, ALU.add).then_inc(ms_ready, 1)
                    e.wait_ge(rms_root, i + 1)
                    link(v.reciprocal(rs[:], rs[:]))
                    v.tensor_tensor(on[:], ps_o, rs[:].rearrange("p (t a) -> p t a", a=1).broadcast_to([128, NT, 128]),
                                    ALU.mult).then_inc(on_ready, 1)
                    e.wait_ge(gelu_y, i + 1)
                    link(v.tensor_tensor(cat[:, bass.ds(i + 4, 1)].rearrange("p a t -> p (a t)"), xc[:], zy[:],
                                         ALU.mult))
                    e.wait_ge(oc_t, i + 1)
                    v.tensor_copy(rows_out[:], ps_rows[0:36]).then_inc(rows_ready, 1)
                    e.wait_ge(on_t, i + 1)
                    e.wait_ge(stored, (i + 1) * NSTORE * 16)
                    v.scalar_tensor_tensor(out=cat[:, bass.ds(i, 1)].rearrange("p a t -> p (a t)"),
                                           in0=flat[:, 0:T], scalar=cur[:, GN:GN + 1], in1=zg[:],
                                           op0=ALU.mult, op1=ALU.mult).then_inc(all_used, 1)
                    o.close()

            @block.tensor
            def _(e):
                mm, tr = nc.tensor.matmul, nc.tensor.transpose
                with e.Fori(0, 4) as i:
                    e.wait_ge(loaded, (i + 1) * NLOAD * 16)
                    tr(ps_state, rows_in[:], P.ident[:]).then_inc(state_t, 1)
                    e.wait_ge(xc_ready, i + 1)
                    e.wait_ge(all_used, i + 1)
                    for n in range(NN):
                        for w in range(2):
                            last = mm(gps[:, 3 * w + n, 0:NW], wg[:, w], xc[:, n * NW:(n + 1) * NW],
                                      start=True, stop=True)
                    last.then_inc(gates, 1)
                    e.wait_ge(sig_r, i + 1)
                    for t in range(NT):
                        last = tr(ps_v[:, t], zv[:, t * 128:(t + 1) * 128], P.ident[:])
                    last.then_inc(v_t, 1)
                    e.wait_ge(sig_i, i + 1)
                    e.wait_ge(kdec_ready, i + 1)
                    for t in range(NT):
                        last = tr(ps_kd[:, t], e3[:, t * 128:(t + 1) * 128], P.ident[:])
                    last.then_inc(kdec_t, 1)
                    e.wait_ge(v_tok, i + 1)
                    e.wait_ge(kdec_tok, i + 1)
                    for c in range(NCH):
                        t, half = c // 2, slice(CH * (c % 2), CH * (c % 2) + CH)
                        last = mm(ds_of(c), kdtok[half, t], vtok[half, t], start=True, stop=True)
                    last.then_inc(ds_ready, 1)
                    e.wait_ge(vmask_ready, i + 1)
                    for q in range(2):
                        last = mm(ps_dss[:, 4 * q:4 * q + 4].rearrange("p b n -> p (b n)"), kdtok[:, NPT],
                                  vmask[:, 4 * q:4 * q + 4].rearrange("p b n -> p (b n)"), start=True, stop=True)
                    last.then_inc(dss_ready, 1)
                    e.wait_ge(qk_ready, i + 1)
                    e.wait_ge(st_ready, i + 1)
                    for t in range(NT):
                        cols = slice(t * 128, (t + 1) * 128)
                        last = mm(ps_att[:, t], e2[:, cols], zq[:, cols], start=True, stop=True)
                    last.then_inc(att_sum, 1)
                    e.wait_ge(att_ready, i + 1)
                    e.wait_ge(sn_ready, i + 1)
                    e.wait_ge(qdz_ready, i + 1)
                    for t in range(NPT):
                        mm(ps_o[:, t], att[:, t], vtok[:, t], start=True, stop=False, skip_group_check=True)
                        for q in range(2):
                            half = slice(CH * q, CH * q + CH)
                            mm(ps_o[half, t], zq[:, t * 128 + CH * q:t * 128 + CH * q + CH], states[:, 2 * t + q],
                               start=False, stop=True, skip_group_check=True)
                    mm(ps_o[:, NPT], att[:, NPT], vtok[:, NPT], start=True, stop=False, skip_group_check=True)
                    for b in range(DB):
                        last = mm(ps_o[:, NPT], qdz[:, b * 128:(b + 1) * 128], s0[:, b], start=False,
                                  stop=b == DB - 1, skip_group_check=True)
                    last.then_inc(o_sum, 1)
                    e.wait_ge(oc_ready, i + 1)
                    tr(ps_rows, cols_out[:], P.ident[:]).then_inc(oc_t, 1)
                    e.wait_ge(on_ready, i + 1)
                    for t in range(NT):
                        last = tr(ps_ont[:, t], on[:, t], P.ident[:])
                    last.then_inc(on_t, 1)
        nc.clear_and_free_semaphores(used)
        nc.all_engine_barrier()


def output_projection(P, cat):
    nc = P.nc
    w_v = P.a["w_out"][0].rearrange("(k p) c -> p k c", p=128)
    with ExitStack() as ctx:
        def sb(n, shape, d=F32):
            return ctx.enter_context(nc.sbuf_tensor(f"op_{n}", shape, d))
        s = lambda n: ctx.enter_context(nc.semaphore(f"op_{n}"))
        raw = sb("raw", [128, 2, D])
        whi, wlo = sb("whi", [128, KC, D], F32R), sb("wlo", [128, KC, D], F32R)
        chi, clo = sb("chi", [128, 3, KC, 128], F32R), sb("clo", [128, 3, KC, 128], F32R)
        po = ctx.enter_context(nc.psum_tensor("op_ps", [128, 3, D], F32))
        w_in = [s(f"w_in{u}") for u in range(2)]
        whi_done, wlo_done, chi_done, clo_done, summed, added = map(
            s, ("whi", "wlo", "chi", "clo", "summed", "added"))
        with nc.Block() as block:
            @block.sync
            def _(e):
                for k in range(KC):
                    if k >= 2:
                        e.wait_ge(wlo_done, k - 1)
                    e.dma_start(raw[:, k % 2], w_v[:, k]).then_inc(w_in[k % 2], 16)

            @block.scalar
            def _(e):
                for k in range(KC):
                    e.wait_ge(w_in[k % 2], (k // 2 + 1) * 16)
                    nc.scalar.activation(whi[:, k], raw[:, k % 2], ACT.Copy).then_inc(whi_done, 1)
                with e.Fori(0, NT // 3) as i:
                    for u in range(3):
                        e.wait_ge(summed, i * 3 + u + 1)
                        nc.scalar.activation(chi[:, u], cat[:, :, bass.ds((i * 3 + u) * 128, 128)],
                                             ACT.Copy).then_inc(chi_done, 1)

            @block.vector
            def _(e):
                for k in range(KC):
                    e.wait_ge(whi_done, k + 1)
                    nc.vector.tensor_tensor(wlo[:, k], raw[:, k % 2], whi[:, k].bitcast(F32),
                                            ALU.subtract).then_inc(wlo_done, 1)
                nc.vector.sem_inc(added, 3)
                with e.Fori(0, NT // 3) as i:
                    for u in range(3):
                        e.wait_ge(chi_done, i * 3 + u + 1)
                        nc.vector.tensor_tensor(clo[:, u], cat[:, :, bass.ds((i * 3 + u) * 128, 128)],
                                                chi[:, u].bitcast(F32), ALU.subtract).then_inc(clo_done, 1)
                    for u in range(3):
                        e.wait_ge(summed, i * 3 + u + 4)
                        row = P.h[:, bass.ds(i * 3 + u, 1)].rearrange("p a d -> p (a d)")
                        nc.vector.tensor_tensor(row, po[:, u], row, ALU.add).then_inc(added, 1)

            @block.tensor
            def _(e):
                nc.tensor.sem_inc(summed, 3)
                e.wait_ge(wlo_done, KC)
                with e.Fori(0, NT // 3) as i:
                    for u in range(3):
                        e.wait_ge(clo_done, i * 3 + u + 1)
                        e.wait_ge(added, i * 3 + u + 1)
                        for q in range(2):
                            cols = slice(512 * q, 512 * q + 512)
                            for k in range(KC):
                                last = three_passes(nc, po[:, u, cols], (chi[:, u, k], clo[:, u, k]),
                                                    (whi[:, k, cols], wlo[:, k, cols]), k == 0, k == KC - 1)
                        last.then_inc(summed, 1)


def route_scores(P, xhi, xlo, sv, si):
    nc = P.nc
    w_v = P.a["w_peer_q"][0].rearrange("(k p) c -> p k c", p=128)
    keys = P.a["peer_keys"][0].rearrange("h p n c -> (h p) n c")
    with ExitStack() as ctx:
        def sb(n, shape, d=F32):
            return ctx.enter_context(nc.sbuf_tensor(f"rs_{n}", shape, d))
        s = lambda n: ctx.enter_context(nc.semaphore(f"rs_{n}"))
        raw = sb("raw", [128, 2, KC, 128])
        whi, wlo = sb("whi", [128, 2, KC, 128], F32R), sb("wlo", [128, 2, KC, 128], F32R)
        kraw = sb("kraw", [128, 2, 128])
        kt = sb("kt", [128, 2, 128])
        q = sb("q", [128, T])
        rest = sb("rest", [128, NT, 128])
        val16, ind16 = sb("val16", [128, NT, K]), sb("ind16", [128, NT, K], U32)
        pq = ctx.enter_context(nc.psum_tensor("rs_pq", [128, 2, 512], F32))
        pk = ctx.enter_context(nc.psum_tensor("rs_pk", [128, 512], F32))
        psc = ctx.enter_context(nc.psum_tensor("rs_sc", [128, 3, 4, 128], F32))
        scores = [psc[:, t // 4, t % 4] for t in range(NT)]
        w_in = [s(f"w_in{u}") for u in range(2)]
        hi_done, lo_done, q_sum, q_ready, k_t, kt_ready, scored, ranked, self_ok = map(
            s, ("hi", "lo", "q_sum", "q_ready", "k_t", "kt", "scored", "ranked", "self"))
        LAST = HP // 2 - 1
        with nc.Block() as block:
            @block.sync
            def _(e):
                with e.Fori(0, HP // 2) as i:
                    for u in range(2):
                        n = i * 2 + u
                        e.wait_ge(lo_done, n + 1)
                        e.wait_ge(k_t, n + 1)
                        e.dma_start(raw[:, u], w_v[:, :, bass.ds(n * 128, 128)]).then_inc(w_in[u], 16)
                        e.dma_start(kraw[:, u], keys[bass.ds(n, 1)].rearrange("a n c -> n (a c)")
                                    ).then_inc(w_in[u], 16)

            @block.scalar
            def _(e):
                nc.scalar.sem_inc(q_ready, 2)
                nc.scalar.sem_inc(kt_ready, 2)

                def hi(i, u):
                    n = i * 2 + u
                    e.wait_ge(w_in[u], (i + 1) * 32)
                    e.wait_ge(q_sum, (n + 1) * NN)
                    nc.scalar.activation(whi[:, u], raw[:, u], ACT.Copy).then_inc(hi_done, 1)

                def step(i, u):
                    n = i * 2 + u
                    e.wait_ge(k_t, n + 3)
                    e.wait_ge(scored, n + 1)
                    nc.scalar.activation(kt[:, u], pk[:, u * 128:(u + 1) * 128], ACT.Copy).then_inc(kt_ready, 1)
                    for m in range(NN):
                        e.wait_ge(q_sum, (n + 2) * NN + m + 1)
                        nc.scalar.activation(q[:, m * NW:(m + 1) * NW], pq[:, (m + u) % 2, 0:NW],
                                             ACT.Copy).then_inc(q_ready, 1)

                hi(0, 0)
                with e.Fori(0, LAST) as i:
                    hi(i, 1)
                    step(i, 0)
                    hi(i + 1, 0)
                    step(i, 1)
                hi(LAST, 1)
                step(LAST, 0)
                step(LAST, 1)

            @block.vector
            def _(e):
                v = nc.vector
                nc.vector.sem_inc(lo_done, 2)
                nc.vector.sem_inc(ranked, 1)

                def lo(i, u):
                    e.wait_ge(hi_done, i * 2 + u + 1)
                    v.tensor_tensor(wlo[:, u], raw[:, u], whi[:, u].bitcast(F32), ALU.subtract).then_inc(lo_done, 1)

                def rank(i, u):
                    n = i * 2 + u
                    o = Order(e, self_ok, 5 * NT + 1, n)
                    val = [val16[:, t] for t in range(NT)]
                    ind = [ind16[:, t] for t in range(NT)]
                    wait_apart(e, P, scored, n + 2)
                    for t in range(NT):
                        o.did(v.max(val[t][:, 0:8], scores[t]))
                    wait_apart(e, P, o.sem, o.value())
                    for t in range(NT):
                        o.did(v.max_index(ind[t][:, 0:8], val[t][:, 0:8], scores[t]))
                        o.did(v.match_replace(rest[:, t], val[t][:, 0:8], scores[t], LOWEST))
                    wait_apart(e, P, o.sem, o.value())
                    for t in range(NT):
                        o.did(v.max(val[t][:, 8:16], rest[:, t]))
                    wait_apart(e, P, o.sem, o.value())
                    for t in range(NT):
                        o.did(v.max_index(ind[t][:, 8:16], val[t][:, 8:16], rest[:, t]))
                    o.settle()
                    o.did(v.tensor_copy(sv[:, :, bass.ds(n, 1), :].rearrange("p t a n -> p t (a n)"), val16[:]))
                    o.settle()
                    v.tensor_copy(si[:, :, bass.ds(n, 1), :].rearrange("p t a n -> p t (a n)"), ind16[:]
                                  ).then_inc(ranked, 1)
                    o.close()

                lo(0, 0)
                with e.Fori(0, LAST) as i:
                    lo(i, 1)
                    rank(i, 0)
                    lo(i + 1, 0)
                    rank(i, 1)
                lo(LAST, 1)
                rank(LAST, 0)
                rank(LAST, 1)

            @block.tensor
            def _(e):
                nc.tensor.sem_inc(q_sum, 2 * NN)
                nc.tensor.sem_inc(k_t, 2)
                nc.tensor.sem_inc(scored, 1)
                with e.Fori(0, HP // 2) as i:
                    for u in range(2):
                        n = i * 2 + u
                        e.wait_ge(w_in[u], (i + 1) * 32)
                        e.wait_ge(kt_ready, n + 1)
                        nc.tensor.transpose(pk[:, u * 128:(u + 1) * 128], kraw[:, u], P.ident[:]).then_inc(k_t, 1)
                        e.wait_ge(lo_done, n + 3)
                        for m in range(NN):
                            e.wait_ge(q_ready, n * NN + m + 1)
                            cols = slice(m * NW, (m + 1) * NW)
                            for k in range(KC):
                                last = three_passes(nc, pq[:, (m + u) % 2, 0:NW], (whi[:, u, k], wlo[:, u, k]),
                                                    (xhi[:, k, cols], xlo[:, k, cols]), k == 0, k == KC - 1)
                            last.then_inc(q_sum, 1)
                        e.wait_ge(kt_ready, n + 3)
                        e.wait_ge(q_ready, (n + 1) * NN + 2)
                        e.wait_ge(ranked, n + 1)
                        for t in range(NT):
                            last = nc.tensor.matmul(scores[t], q[:, t * 128:(t + 1) * 128], kt[:, u],
                                                    start=True, stop=True)
                        last.then_inc(scored, 1)


SUB = 32
NSUB = T // SUB
QUAD = 4
NQ = SUB // QUAD
G_SCALE = float(2 ** 15)


def experts(P, xhi, xlo, sv, si_of, region, act_dram, w_dram):
    nc = P.nc
    u_v = P.a["peer_u"][0].rearrange("(i j) d -> i j d", j=NK)
    with ExitStack() as ctx:
        def sb(n, shape, d=F32):
            return ctx.enter_context(nc.sbuf_tensor(f"ea_{n}", shape, d))
        s = lambda n: ctx.enter_context(nc.semaphore(f"ea_{n}"))
        raw = sb("raw", [128, 2, D])
        uhi, ulo = sb("uhi", [128, 2, KC, 128], F32R), sb("ulo", [128, 2, KC, 128], F32R)
        stage = sb("stage", [128, 2, T])
        best, at = sb("best", [128, PH, K]), sb("at", [128, PH, K], U32)
        ab = sb("ab", [128, 2, PH * K], U32)
        sif = sb("sif", [128, HP, K])
        rows = sb("rows", [128, 3, PH * K])
        total = sb("total", [128, PH])
        iota = sb("iota", [128, NK], F16)
        iota_u = rows[:, 0].bitcast(I32)
        cand = region[:, 4608:6656].rearrange("p (h a b) -> p h a b", a=K, b=K)
        eq = region[:, 6656:8704].rearrange("p (n a) -> p n a", a=K)
        si = si_of(region)
        picks = sb("picks", [128, 4, T], F16)
        cur = sb("cur", [128, 2, 4, SUB], F16)
        wt = region[:, 0:2 * NK * SUB].rearrange("p (u j t) -> p u j t", u=2, t=SUB)
        RING = 4
        hot = region[:, 8192:8192 + 3072].bitcast(F16).rearrange("p (x r q n) -> p x r q n", x=3, r=RING, q=QUAD)
        pt = ctx.enter_context(nc.psum_tensor("ea_pt", [128, KC, 128], F32))
        pa = ctx.enter_context(nc.psum_tensor("ea_pa", [128, NN, 512], F32))
        pr = ctx.enter_context(nc.psum_tensor("ea_pr", [128, 4, 128], F32))
        pw = ctx.enter_context(nc.psum_tensor("ea_pw", [128, 2, QUAD, NK], F32))
        u_in = [s(f"u_in{u}") for u in range(2)]
        stored = [s(f"stored{u}") for u in range(2)]
        w_out = [s(f"w_out{u}") for u in range(2)]
        u_t, hi_done, lo_done, summed, gelued = map(s, ("u_t", "hi", "lo", "summed", "gelued"))
        made, self_ok, shifted, exped, rows_ready, rows_t, picks_hi, picks_done = map(
            s, ("made", "self", "shifted", "exped", "rows", "rows_t", "picks_hi", "picks_done"))
        cur_ready, onehot_i, onehot_j, w_summed, w_ready = map(s, ("cur", "onehot_i", "onehot_j", "w_summed", "w"))
        A_STEPS = 4
        B0 = NT * A_STEPS // 2
        C0 = B0 + NSUB
        LAST = NK // 2 - 1

        def nxt(p, u):
            return (p, 1) if u == 0 else (p + 1, 0)

        with nc.Block() as block:
            @block.gpsimd
            def _(e):
                nc.gpsimd.iota(iota_u, [[1, NK]], base=0, channel_multiplier=0).then_inc(made, 1)
                e.wait_ge(made, 1)
                nc.gpsimd.tensor_copy(iota[:], iota_u).then_inc(made, 1)
                e.wait_ge(made, 2)
                with e.Fori(0, NSUB // 2) as i:
                    for v in range(2):
                        for q in range(NQ):
                            m = (i * 2 + v) * NQ + q
                            e.wait_ge(cur_ready, i * 2 + v + 1)
                            wait_apart(e, P, w_summed, m + 1)
                            for t in range(QUAD):
                                c = q * QUAD + t
                                last = nc.gpsimd.tensor_scalar(hot[:, 0, q % RING, t], iota[:],
                                                               cur[:, v, 0, c:c + 1], None, ALU.is_equal)
                            last.then_inc(onehot_i, 1)

            @block.sync
            def _(e):
                for u in range(2):
                    nc.sync.sem_inc(stored[u], 16)
                    nc.sync.sem_inc(w_out[u], 16)

                def load(p, u):
                    e.wait_ge(u_t, p * 2 + u + 1)
                    e.dma_start(raw[:, u], u_v[:, bass.ds(p * 2 + u, 1)].rearrange("p a d -> p (a d)")
                                ).then_inc(u_in[u], 16)

                def store(p, u):
                    e.wait_ge(gelued, (p * 2 + u + 1) * NN + NN)
                    e.dma_start(act_dram[:, bass.ds(p * 2 + u, 1)].rearrange("p a t -> p (a t)"),
                                stage[:, u]).then_inc(stored[u], 16)

                def pair(p):
                    for u in range(2):
                        load(p + 1, u)
                        store(p, u)

                def store_weights(n, v):
                    e.wait_ge(w_ready, (n + 1) * NQ + 2)
                    e.dma_start(w_dram[:, bass.ds(n, 1)].rearrange("p a j t -> p (a j t)"),
                                wt[:, v].rearrange("p j t -> p (j t)")).then_inc(w_out[v], 16)

                load(0, 0)
                load(0, 1)
                with e.Fori(0, B0) as i:
                    pair(i)
                with e.Fori(0, NSUB // 2) as i:
                    for v in range(2):
                        pair(i * 2 + (B0 + v))
                        store_weights(i * 2 + v, v)
                with e.Fori(0, LAST - C0) as i:
                    pair(i + C0)
                for u in range(2):
                    store(LAST, u)
                for u in range(2):
                    e.wait_ge(stored[u], (NK // 2 + 1) * 16)
                    e.wait_ge(w_out[u], (NSUB // 2 + 1) * 16)

            @block.scalar
            def _(e):
                nc.scalar.sem_inc(gelued, NN)
                nc.scalar.sem_inc(w_ready, 2)

                def hi(p, u):
                    e.wait_ge(u_t, p * 2 + u + 3)
                    e.wait_ge(summed, (p * 2 + u + 1) * NN)
                    nc.scalar.activation(uhi[:, u], pt[:], ACT.Copy).then_inc(hi_done, 1)

                def gelu(p, u, n):
                    e.wait_ge(stored[u], (p + 1) * 16)
                    e.wait_ge(summed, (p * 2 + u + 2) * NN + n + 1)
                    nc.scalar.activation(stage[:, u, n * NW:(n + 1) * NW], pa[:, n, 0:NW],
                                         ACT.Gelu_apprx_tanh).then_inc(gelued, 1)

                def weights(i, v, q):
                    e.wait_ge(w_out[v], (i + 1) * 16)
                    e.wait_ge(w_summed, (i * 2 + v) * NQ + q + 1 + RING)
                    dst = wt[:, v, :, q * QUAD:(q + 1) * QUAD].rearrange("p j t -> p t j")
                    nc.scalar.activation(dst, pw[:, q % 2], ACT.Copy, scale=1.0 / G_SCALE).then_inc(w_ready, 1)

                hi(0, 0)
                with e.Fori(0, NT) as i:
                    for st in range(A_STEPS):
                        p, u = i * 2 + st // 2, st % 2
                        hi(*nxt(p, u))
                        if st == 2:
                            e.wait_ge(shifted, i + 1)
                            nc.scalar.activation(rows[:, 2], rows[:, 2], ACT.Exp).then_inc(exped, 1)
                        for n in range(NN):
                            gelu(p, u, n)
                    e.wait_ge(rows_t, i + 1)
                    cols = bass.ds(i * 128, 128)
                    for x, scale in ((0, 1.0), (1, 1.0), (2, G_SCALE)):
                        nc.scalar.activation(picks[:, x, cols], pr[:, x], ACT.Copy, scale=scale).then_inc(picks_hi, 1)
                with e.Fori(0, NSUB // 2) as i:
                    for v in range(2):
                        for u in range(2):
                            p = i * 2 + (B0 + v)
                            hi(*nxt(p, u))
                            for n in range(NN):
                                gelu(p, u, n)
                                weights(i, v, 4 * u + n)
                            weights(i, v, 4 * u + NN)
                with e.Fori(0, LAST - C0) as i:
                    for u in range(2):
                        hi(*nxt(i + C0, u))
                        for n in range(NN):
                            gelu(i + C0, u, n)
                hi(LAST, 1)
                for u in range(2):
                    for n in range(NN):
                        gelu(LAST, u, n)

            @block.vector
            def _(e):
                v_ = nc.vector
                nc.vector.sem_inc(lo_done, 1)

                def lo(p, u):
                    e.wait_ge(hi_done, p * 2 + u + 1)
                    nc.vector.tensor_tensor(ulo[:, u], pt[:], uhi[:, u].bitcast(F32),
                                            ALU.subtract).then_inc(lo_done, 1)

                PER = 6 * PH + 4
                flat = [cand[:, h].rearrange("p a b -> p (a b)") for h in range(PH)]
                shape = [128, PH, K, K]
                g = rows[:, 2].rearrange("p (h k) -> p h k", k=K)
                sif4 = sif[:].rearrange("p (h x) k -> p h x k", x=2)

                def over_k(x):
                    return x.rearrange("p h (k a) -> p h k a", a=1).broadcast_to(shape)

                def over_a(x):
                    return x.rearrange("p h (a k) -> p h a k", a=1).broadcast_to(shape)

                def best_sums(o, i):
                    one = lambda x: x[:, bass.ds(i, 1)].rearrange("p a n k -> p (a n) k")
                    sv4 = one(sv).rearrange("p (h x) k -> p h x k", x=2)
                    o.did(v_.tensor_tensor(cand, over_k(sv4[:, :, 0, :]), over_a(sv4[:, :, 1, :]), ALU.add))
                    o.did(v_.tensor_copy(sif[:], one(si)))
                    wait_apart(e, P, o.sem, o.value())
                    for h in range(PH):
                        o.did(v_.max(best[:, h, 0:8], flat[h]))
                    wait_apart(e, P, o.sem, o.value())
                    for h in range(PH):
                        o.did(v_.max_index(at[:, h, 0:8], best[:, h, 0:8], flat[h]))
                    wait_apart(e, P, o.sem, o.value())
                    for h in range(PH):
                        o.did(v_.match_replace(flat[h], best[:, h, 0:8], flat[h], LOWEST))

                def next_sums(o, i):
                    wait_apart(e, P, o.sem, o.value())
                    for h in range(PH):
                        o.did(v_.max(best[:, h, 8:16], flat[h]))
                    wait_apart(e, P, o.sem, o.value())
                    for h in range(PH):
                        o.did(v_.max_index(at[:, h, 8:16], best[:, h, 8:16], flat[h]))
                    e.wait_ge(picks_done, i + 1)
                    v_.tensor_tensor(g, best[:], best[:, :, 0:1].broadcast_to([128, PH, K]),
                                     ALU.subtract).then_inc(shifted, 1)
                    o.settle()
                    places = at[:].rearrange("p h k -> p (h k)")
                    o.did(v_.tensor_single_scalar(ab[:, 0], places, 4, ALU.logical_shift_right))
                    o.did(v_.tensor_single_scalar(ab[:, 1], places, K - 1, ALU.bitwise_and))

                def subkey(o, x):
                    o.settle()
                    o.did(v_.tensor_tensor(
                        eq, ab[:, x].rearrange("p (n a) -> p n a", a=1).broadcast_to([128, PH * K, K]),
                        iota[:, 0:K].rearrange("p (a k) -> p a k", a=1).broadcast_to([128, PH * K, K]),
                        ALU.is_equal))
                    o.settle()
                    q4 = eq.rearrange("p (h k) a -> p h k a", k=K)
                    o.did(v_.tensor_tensor(q4, q4, over_a(sif4[:, :, x, :]), ALU.mult))
                    o.settle()
                    o.did(v_.tensor_reduce(rows[:, x], eq, AX.X, ALU.add))

                def softmax(o, i):
                    e.wait_ge(exped, i + 1)
                    o.did(v_.tensor_reduce(total[:], g, AX.X, ALU.add))
                    o.settle()
                    o.did(v_.reciprocal(total[:], total[:]))
                    o.settle()
                    v_.tensor_tensor(g, g, total[:].rearrange("p (h a) -> p h a", a=1).broadcast_to([128, PH, K]),
                                     ALU.mult).then_inc(rows_ready, 1)
                    e.wait_ge(picks_hi, i * 3 + 3)
                    cols = bass.ds(i * 128, 128)
                    v_.scalar_tensor_tensor(out=picks[:, 3, cols], in0=pr[:, 2], scalar=G_SCALE,
                                            in1=picks[:, 2, cols], op0=ALU.mult,
                                            op1=ALU.subtract).then_inc(picks_done, 1)

                def one_hots(n, v, q):
                    e.wait_ge(w_summed, n * NQ + q + 1)
                    r = q % RING
                    for t in range(QUAD):
                        j_, gh, gl = (cur[:, v, x, q * QUAD + t:q * QUAD + t + 1] for x in range(1, 4))
                        v_.tensor_scalar(hot[:, 1, r, t], iota[:], j_, gh, ALU.is_equal, ALU.mult)
                        last = v_.tensor_scalar(hot[:, 2, r, t], iota[:], j_, gl, ALU.is_equal, ALU.mult)
                    last.then_inc(onehot_j, 1)

                lo(0, 0)
                e.wait_ge(made, 2)
                v_.sem_inc(picks_done, 1)
                with e.Fori(0, NT) as i:
                    o = Order(e, self_ok, PER, i)
                    lo(i * 2, 1)
                    best_sums(o, i)
                    lo(i * 2 + 1, 0)
                    next_sums(o, i)
                    lo(i * 2 + 1, 1)
                    subkey(o, 0)
                    lo(i * 2 + 2, 0)
                    subkey(o, 1)
                    softmax(o, i)
                    o.close()
                e.wait_ge(picks_done, NT + 1)
                with e.Fori(0, NSUB // 2) as i:
                    for v in range(2):
                        n = i * 2 + v
                        v_.tensor_copy(cur[:, v], picks[:, :, bass.ds(n * SUB, SUB)]).then_inc(cur_ready, 1)
                        e.wait_ge(cur_ready, n + 1)
                        for u in range(2):
                            lo(*nxt(i * 2 + (B0 + v), u))
                            for q in range(4 * u, 4 * u + 4):
                                one_hots(n, v, q)
                with e.Fori(0, LAST - C0) as i:
                    for u in range(2):
                        lo(*nxt(i + C0, u))
                lo(LAST, 1)

            @block.tensor
            def _(e):
                nc.tensor.sem_inc(u_t, 2)
                nc.tensor.sem_inc(summed, 2 * NN)
                nc.tensor.sem_inc(w_summed, RING)

                def turn(p, u):
                    e.wait_ge(u_in[u], (p + 1) * 16)
                    e.wait_ge(lo_done, p * 2 + u + 1)
                    for k in range(KC):
                        last = nc.tensor.transpose(pt[:, k], raw[:, u, k * 128:(k + 1) * 128], P.ident[:])
                    last.then_inc(u_t, 1)

                def product(p, u, n):
                    e.wait_ge(lo_done, p * 2 + u + 2)
                    e.wait_ge(gelued, (p * 2 + u) * NN + n + 1)
                    cols = slice(n * NW, (n + 1) * NW)
                    for k in range(KC):
                        last = three_passes(nc, pa[:, n, 0:NW], (uhi[:, u, k], ulo[:, u, k]),
                                            (xhi[:, k, cols], xlo[:, k, cols]), k == 0, k == KC - 1)
                    last.then_inc(summed, 1)

                def weights(n, q):
                    e.wait_ge(onehot_i, n * NQ + q + 1)
                    e.wait_ge(onehot_j, n * NQ + q + 1)
                    e.wait_ge(w_ready, n * NQ + q + 1)
                    r = q % RING
                    for t in range(QUAD):
                        nc.tensor.matmul(pw[:, q % 2, t], hot[:, 0, r, t], hot[:, 1, r, t], start=True, stop=False)
                        last = nc.tensor.matmul(pw[:, q % 2, t], hot[:, 0, r, t], hot[:, 2, r, t],
                                                start=False, stop=True)
                    last.then_inc(w_summed, 1)

                turn(0, 0)
                with e.Fori(0, NT) as i:
                    for st in range(A_STEPS):
                        p, u = i * 2 + st // 2, st % 2
                        turn(*nxt(p, u))
                        for n in range(NN):
                            product(p, u, n)
                    e.wait_ge(rows_ready, i + 1)
                    for n in range(3):
                        last = nc.tensor.transpose(pr[:, n], rows[:, n], P.ident[:])
                    last.then_inc(rows_t, 1)
                with e.Fori(0, NSUB // 2) as i:
                    for v in range(2):
                        for u in range(2):
                            p = i * 2 + (B0 + v)
                            turn(*nxt(p, u))
                            for n in range(NN):
                                product(p, u, n)
                                weights(i * 2 + v, 4 * u + n)
                            weights(i * 2 + v, 4 * u + NN)
                with e.Fori(0, LAST - C0) as i:
                    for u in range(2):
                        turn(*nxt(i + C0, u))
                        for n in range(NN):
                            product(i + C0, u, n)
                turn(LAST, 1)
                for u in range(2):
                    for n in range(NN):
                        product(LAST, u, n)


GRP = 4


def expert_outputs(P, w_dram, act_dram):
    nc = P.nc
    NG = NK // GRP
    v_v = P.a["peer_v"][0].rearrange("(i j) d -> i j d", j=NK)
    with ExitStack() as ctx:
        def sb(n, shape, d=F32):
            return ctx.enter_context(nc.sbuf_tensor(f"eo_{n}", shape, d))
        s = lambda n: ctx.enter_context(nc.semaphore(f"eo_{n}"))
        wt = sb("wt", [128, 2, NSUB, GRP, SUB])
        at = sb("at", [128, 2, GRP, T])
        raw = sb("raw", [128, 2, D])
        vhi, vlo = sb("vhi", [128, 2, GRP, D], F32R), sb("vlo", [128, 2, GRP, D], F32R)
        prod = sb("prod", [128, 3, GRP, 128])
        phi, plo = sb("phi", [128, 3, GRP, 128], F32R), sb("plo", [128, 3, GRP, 128], F32R)
        po = ctx.enter_context(nc.psum_tensor("eo_ps", [128, 3, D], F32))
        wa_in = [s(f"wa_in{u}") for u in range(2)]
        v_in = [s(f"v_in{u}") for u in range(2)]
        vhi_done, vlo_done, prod_done, phi_done, plo_done, summed, added = map(
            s, ("vhi", "vlo", "prod", "phi", "plo", "summed", "added"))
        PAIRS = NG // 2

        def in_pairs(e, first, body):
            first()
            with e.Fori(0, PAIRS - 1) as i:
                body(i * 2, 0, False)
                body(i * 2 + 1, 1, False)
            body(NG - 2, 0, False)
            body(NG - 1, 1, True)

        V_TILES = {1: 0, 3: 1, 5: 2, 7: 3}

        with nc.Block() as block:
            @block.sync
            def _(e):
                def weights(g, u):
                    e.wait_ge(prod_done, g * NT + NT)
                    e.dma_start(wt[:, u].rearrange("p s j t -> p s (j t)"),
                                w_dram[:, :, bass.ds(g * GRP, GRP), :].rearrange("p s j t -> p s (j t)")
                                ).then_inc(wa_in[u], 16)
                    e.dma_start(at[:, u].rearrange("p j t -> p (j t)"),
                                act_dram[:, bass.ds(g * GRP, GRP), :].rearrange("p j t -> p (j t)")
                                ).then_inc(wa_in[u], 16)

                def rows(g):
                    for jj in range(GRP):
                        e.wait_ge(vlo_done, g * GRP + jj + 1)
                        e.dma_start(raw[:, jj % 2], v_v[:, bass.ds(g * GRP + jj, 1)].rearrange("p a d -> p (a d)")
                                    ).then_inc(v_in[jj % 2], 16)

                def first():
                    weights(0, 0)
                    rows(0)

                def body(g, u, last):
                    if not last:
                        weights(g + 1, 1 - u)
                        rows(g + 1)

                in_pairs(e, first, body)

            @block.scalar
            def _(e):
                def v_hi(g, u, jj):
                    e.wait_ge(v_in[jj % 2], (g * 2 + jj // 2 + 1) * 16)
                    e.wait_ge(summed, g * NT + NT)
                    nc.scalar.activation(vhi[:, u, jj], raw[:, jj % 2], ACT.Copy).then_inc(vhi_done, 1)

                def p_hi(g, t):
                    e.wait_ge(prod_done, g * NT + t + 1 + 2 * NT)
                    e.wait_ge(summed, g * NT + t + 2 * NT - 2)
                    nc.scalar.activation(phi[:, t % 3], prod[:, t % 3], ACT.Copy).then_inc(phi_done, 1)

                def first():
                    for jj in range(GRP):
                        v_hi(0, 0, jj)
                    p_hi(0, 0)
                    p_hi(0, 1)

                def body(g, u, last):
                    for t in range(NT):
                        if t + 2 < NT or not last:
                            p_hi(g + (t + 2) // NT, (t + 2) % NT)
                        if t in V_TILES and not last:
                            v_hi(g + 1, 1 - u, V_TILES[t])

                in_pairs(e, first, body)

            @block.vector
            def _(e):
                v = nc.vector
                v.sem_inc(vlo_done, 2)
                v.sem_inc(prod_done, 2 * NT)
                v.sem_inc(added, 3)

                def v_lo(g, u, jj):
                    e.wait_ge(vhi_done, g * GRP + jj + 1)
                    v.tensor_tensor(vlo[:, u, jj], raw[:, jj % 2], vhi[:, u, jj].bitcast(F32),
                                    ALU.subtract).then_inc(vlo_done, 1)

                def product(g, u, t):
                    e.wait_ge(wa_in[u], (g // 2 if isinstance(g, int) else g // 2) * 32 + 32)
                    e.wait_ge(summed, g * NT + t + 2 * NT - 2)
                    w = wt[:, u, 4 * t:4 * t + 4].rearrange("p s j t -> p j s t")
                    x = at[:, u, :, t * 128:(t + 1) * 128].rearrange("p j (s t) -> p j s t", t=SUB)
                    v.tensor_tensor(prod[:, t % 3].rearrange("p j (s t) -> p j s t", t=SUB), w, x,
                                    ALU.mult).then_inc(prod_done, 1)

                def p_lo(g, t):
                    e.wait_ge(phi_done, g * NT + t + 1)
                    v.tensor_tensor(plo[:, t % 3], prod[:, t % 3], phi[:, t % 3].bitcast(F32),
                                    ALU.subtract).then_inc(plo_done, 1)

                def add(g, t):
                    e.wait_ge(summed, g * NT + t + 1 + 2 * NT)
                    e.wait_ge(added, g * NT + t + 1)
                    v.tensor_tensor(P.h[:, t], po[:, t % 3], P.h[:, t], ALU.add).then_inc(added, 1)

                def first():
                    for jj in range(GRP):
                        v_lo(0, 0, jj)
                    for t in range(2):
                        product(0, 0, t)
                        p_lo(0, t)

                def body(g, u, last):
                    for t in range(NT):
                        more = t + 2 < NT or not last
                        ng, nt = g + (t + 2) // NT, (t + 2) % NT
                        nu = u if t + 2 < NT else 1 - u
                        if more:
                            product(ng, nu, nt)
                        if t in V_TILES and not last:
                            v_lo(g + 1, 1 - u, V_TILES[t])
                        if more:
                            p_lo(ng, nt)
                        add(g, t)

                in_pairs(e, first, body)

            @block.tensor
            def _(e):
                nc.tensor.sem_inc(summed, 2 * NT)

                def body(g, u, last):
                    e.wait_ge(vlo_done, g * GRP + GRP + 2)
                    for t in range(NT):
                        e.wait_ge(plo_done, g * NT + t + 1)
                        e.wait_ge(added, g * NT + t + 1)
                        for q in range(2):
                            cols = slice(512 * q, 512 * q + 512)
                            for jj in range(GRP):
                                mm = three_passes(nc, po[:, t % 3, cols], (phi[:, t % 3, jj], plo[:, t % 3, jj]),
                                                  (vhi[:, u, jj, cols], vlo[:, u, jj, cols]),
                                                  jj == 0, jj == GRP - 1)
                        mm.then_inc(summed, 1)

                in_pairs(e, lambda: None, body)


def input_embedding(P, xhi, xlo):
    nc, a = P.nc, P.a
    PK = a["w_ple"].shape[1] // 128
    wg_v = a["w_ple_gate"][0].rearrange("(k p) c -> p k c", p=128)
    wp_v = a["w_ple"][0].rearrange("(k p) c -> p k c", p=128)
    p_rows = a["p_prompt"][0, 0].rearrange("(t p) c -> p t c", p=128)
    s_rows = a["p_sample"][0].rearrange("b s c -> (b s) c")
    with ExitStack() as ctx:
        def sb(n, shape, d=F32):
            return ctx.enter_context(nc.sbuf_tensor(f"ie_{n}", shape, d))
        s = lambda n: ctx.enter_context(nc.semaphore(f"ie_{n}"))
        HALF = D // 2
        NW_ = 2 * (KC + PK)
        raw = sb("raw", [128, 2, HALF])
        whi, wlo = sb("whi", [128, KC + PK, HALF], F32R), sb("wlo", [128, KC + PK, HALF], F32R)
        ptok = sb("ptok", [128, NT, PK * 128])
        phi, plo = sb("phi", [128, PK, T], F32R), sb("plo", [128, PK, T], F32R)
        gate = sb("gate", [128, 2, HALF])
        stat, rstd = sb("stat", [128, NT]), sb("rstd", [128, NT])
        gbc = sb("gbc", [128, D])
        pt = ctx.enter_context(nc.psum_tensor("ie_pt", [128, 2, 512], F32))
        pg = ctx.enter_context(nc.psum_tensor("ie_pg", [128, 2, 512], F32))
        pp = ctx.enter_context(nc.psum_tensor("ie_pp", [128, 2, 512], F32))
        w_in = [s(f"w_in{u}") for u in range(2)]
        (p_in, p_t, phi_done, plo_done, whi_done, wlo_done, summed, gated, mixed, added, squared, meaned, rooted,
         rstd_ready, out_ready, stored, half_used) = map(s, (
             "p_in", "p_t", "phi", "plo", "whi", "wlo", "summed", "gated", "mixed", "added", "squared", "meaned",
             "rooted", "rstd", "out", "stored", "half_used"))
        NB = KC + PK
        with nc.Block() as block:
            @block.sync
            def _(e):
                e.dma_start(ptok[:, 0:NPT], p_rows).then_inc(p_in, 16)
                e.dma_start(ptok[:, NPT], s_rows).then_inc(p_in, 16)
                e.dma_start(gbc[:], a["g_final"].rearrange("(a n) -> a n", a=1).broadcast_to([128, D])
                            ).then_inc(p_in, 16)
                for q in range(2):
                    cols = slice(HALF * q, HALF * q + HALF)
                    for b in range(NB):
                        n = q * NB + b
                        if n >= 2:
                            e.wait_ge(wlo_done, n - 1)
                        src = wg_v[:, b, cols] if b < KC else wp_v[:, b - KC, cols]
                        e.dma_start(raw[:, n % 2], src).then_inc(w_in[n % 2], 16)
                yp = P.out["y_p"][0].rearrange("(t p) d -> p t d", p=128)
                ys = P.out["y_s"].rearrange("b s d -> (b s) d")
                for t in range(NT):
                    e.wait_ge(out_ready, t + 1)
                    e.dma_start(yp[:, t] if t < NPT else ys, P.h[:, t]).then_inc(stored, 16)
                e.wait_ge(stored, NT * 16)

            def w_split(e, q, engine):
                for b in range(NB):
                    n = q * NB + b
                    if engine == "act":
                        e.wait_ge(w_in[n % 2], (n // 2 + 1) * 16)
                        nc.scalar.activation(whi[:, b], raw[:, n % 2], ACT.Copy).then_inc(whi_done, 1)
                    else:
                        e.wait_ge(whi_done, n + 1)
                        nc.vector.tensor_tensor(wlo[:, b], raw[:, n % 2], whi[:, b].bitcast(F32),
                                                ALU.subtract).then_inc(wlo_done, 1)

            @block.scalar
            def _(e):
                w_split(e, 0, "act")
                for t in range(NT):
                    e.wait_ge(p_t, t + 1)
                    nc.scalar.activation(phi[:, :, t * 128:(t + 1) * 128],
                                         pt[:, t % 2, 0:PK * 128].rearrange("p (k n) -> p k n", k=PK),
                                         ACT.Copy).then_inc(phi_done, 1)
                for q in range(2):
                    if q == 1:
                        e.wait_ge(summed, NT)
                        w_split(e, 1, "act")
                    for t in range(NT):
                        n = q * NT + t
                        e.wait_ge(summed, n + 1)
                        if n >= 2:
                            e.wait_ge(added, n - 1)
                        nc.scalar.activation(gate[:, n % 2], pg[:, n % 2], ACT.Sigmoid).then_inc(gated, 1)
                for t in range(NT):
                    e.wait_ge(added, NT + t + 1)
                    if t >= 1:
                        e.wait_ge(squared, t)
                    nc.scalar.activation(raw[:].rearrange("p a n -> p (a n)"), P.h[:, t], ACT.Square,
                                         accum_out=stat[:, t:t + 1]).then_inc(squared, 1)
                e.wait_ge(meaned, 1)
                nc.scalar.activation(rstd[:], stat[:], ACT.Sqrt).then_inc(rooted, 1)

            @block.vector
            def _(e):
                v = nc.vector
                w_split(e, 0, "dve")
                for t in range(NT):
                    e.wait_ge(phi_done, t + 1)
                    cols = slice(t * 128, (t + 1) * 128)
                    v.tensor_tensor(plo[:, :, cols], pt[:, t % 2, 0:PK * 128].rearrange("p (k n) -> p k n", k=PK),
                                    phi[:, :, cols].bitcast(F32), ALU.subtract).then_inc(plo_done, 1)
                for q in range(2):
                    cols = slice(HALF * q, HALF * q + HALF)
                    for t in range(NT):
                        n = q * NT + t
                        e.wait_ge(gated, n + 1)
                        v.tensor_tensor(gate[:, n % 2], pp[:, n % 2], gate[:, n % 2], ALU.mult).then_inc(mixed, 1)
                        e.wait_ge(mixed, n + 1)
                        v.tensor_tensor(P.h[:, t, cols], P.h[:, t, cols], gate[:, n % 2], ALU.add).then_inc(added, 1)
                    if q == 0:
                        w_split(e, 1, "dve")
                e.wait_ge(squared, NT)
                v.tensor_scalar(stat[:], stat[:], 1.0 / D, EPS, ALU.mult, ALU.add).then_inc(meaned, 1)
                e.wait_ge(rooted, 1)
                v.reciprocal(rstd[:], rstd[:]).then_inc(rstd_ready, 1)
                e.wait_ge(rstd_ready, 1)
                e.wait_ge(p_in, 48)
                e.wait_ge(added, 2 * NT)
                for t in range(NT):
                    v.scalar_tensor_tensor(out=P.h[:, t], in0=P.h[:, t], scalar=rstd[:, t:t + 1], in1=gbc[:],
                                           op0=ALU.mult, op1=ALU.mult).then_inc(out_ready, 1)

            @block.tensor
            def _(e):
                e.wait_ge(p_in, 48)
                for t in range(NT):
                    if t >= 2:
                        e.wait_ge(plo_done, t - 1)
                    for k in range(PK):
                        last = nc.tensor.transpose(pt[:, t % 2, k * 128:(k + 1) * 128],
                                                   ptok[:, t, k * 128:(k + 1) * 128], P.ident[:])
                    last.then_inc(p_t, 1)
                e.wait_ge(plo_done, NT)
                for q in range(2):
                    e.wait_ge(wlo_done, (q + 1) * NB)
                    for t in range(NT):
                        n = q * NT + t
                        if n >= 2:
                            e.wait_ge(mixed, n - 1)
                        cols = slice(t * 128, (t + 1) * 128)
                        for k in range(KC):
                            three_passes(nc, pg[:, n % 2], (xhi[:, k, cols], xlo[:, k, cols]),
                                         (whi[:, k], wlo[:, k]), k == 0, k == KC - 1)
                        for k in range(PK):
                            last = three_passes(nc, pp[:, n % 2], (phi[:, k, cols], plo[:, k, cols]),
                                                (whi[:, KC + k], wlo[:, KC + k]), k == 0, k == PK - 1)
                        last.then_inc(summed, 1)


def build(nc, a, out):
    with ExitStack() as ctx:
        P = Program(nc, a, out, ctx)
        scratch = lambda n, shape: nc.dram_tensor(n, shape, F32, kind="Internal").ap()
        z_dram = scratch("z_scratch", (a["w_in"].shape[2] // 128, 128, T))
        w_dram = scratch("w_scratch", (128, NSUB, NK, SUB))
        act_dram = scratch("act_scratch", (128, NK, T))
        load_and_constants(P)

        def split_x():
            c = ExitStack()
            n = len(splits)
            splits.append(c)
            return c, *(c.enter_context(nc.sbuf_tensor(f"x{part}{n}", [128, KC, T], F32R)) for part in ("hi", "lo"))

        splits = []
        c, xhi, xlo = split_x()
        with c:
            norm_transpose(P, "mix", a["g_mix"][0], xhi, xlo)
            project_inputs(P, xhi, xlo, z_dram)
        with nc.sbuf_tensor("cat", [128, KC, T], F32) as cat:
            mixers(P, z_dram, cat)
            output_projection(P, cat)
        c, xhi, xlo = split_x()
        with c:
            norm_transpose(P, "ffn", a["g_ffn"][0], xhi, xlo)
            with nc.sbuf_tensor("region", [128, 11264], F32) as region:
                words = NT * HP * K
                sv = region[:, 0:words].rearrange("p (t n k) -> p t n k", n=HP, k=K)

                def si_of(r):
                    return r[:, words:2 * words].bitcast(U32).rearrange("p (t n k) -> p t n k", n=HP, k=K)

                route_scores(P, xhi, xlo, sv, si_of(region))
                experts(P, xhi, xlo, sv, si_of, region, act_dram, w_dram)
        expert_outputs(P, w_dram, act_dram)
        c, xhi, xlo = split_x()
        with c:
            norm_transpose(P, "ple", a["g_ple"][0], xhi, xlo)
            input_embedding(P, xhi, xlo)


_INS = ("x_prompt", "x_sample", "state_hgrn", "state_rglru", "state_conv", "p_prompt", "p_sample", "g_mix", "w_in",
        "lower_bounds", "g_hgrn_norm", "conv_w", "conv_b", "w_rg_a", "b_rg_a", "w_rg_x", "b_rg_x", "lambda_rg",
        "w_out", "g_ffn", "w_peer_q", "peer_keys", "peer_u", "peer_v", "g_ple", "w_ple_gate", "w_ple", "g_final")
_OUTS = (("y_p", (1, SEQ, D)), ("y_s", (DB, DS, D)), ("hgrn_p", (1, 1, HA, 128, 128)), ("rglru_p", (1, 1, 512)),
         ("conv_p", (1, 1, 3, 512)), ("hgrn_s", (1, DB, HA, 128, 128)), ("rglru_s", (1, DB, 512)),
         ("conv_s", (1, DB, 3, 512)))


def kernel(**inputs):
    import concourse.bacc as bacc
    from concourse.bass_utils import run_bass_kernel_spmd

    nc = bacc.Bacc("TRN2", target_bir_lowering=False, num_devices=1)
    arrays, a, out = {}, {}, {}
    for name in _INS:
        x = np.ascontiguousarray(inputs[name])
        arrays[f"in_{name}"] = x
        a[name] = nc.dram_tensor(f"in_{name}", x.shape, mybir.dt.from_np(x.dtype), kind="ExternalInput").ap()
    for name, shape in _OUTS:
        out[name] = nc.dram_tensor(f"out_{name}", shape, F32, kind="ExternalOutput").ap()
    build(nc, a, out)
    r = run_bass_kernel_spmd(nc, [arrays], core_ids=[0])
    return tuple(r.results[0][f"out_{name}"] for name, _ in _OUTS)
```

```python
import numpy as np
from contextlib import ExitStack

import concourse.bass as bass
from concourse import mybir

F32 = mybir.dt.float32
F32R = mybir.dt.float32r
F16 = mybir.dt.float16
U32 = mybir.dt.uint32
I32 = mybir.dt.int32
ALU = mybir.AluOpType
ACT = mybir.ActivationFunctionType
AX = mybir.AxisListType

D = 1024
KC = D // 128
SEQ, DB, DS = 1024, 8, 16
T = SEQ + DB * DS
NT = T // 128
NPT = SEQ // 128
CH = 64
NCH = SEQ // CH
HA = 4
HP = 16
PH = 8
K = 16
NK = 128
NN, NW = 3, T // 3
EPS = 1e-6
LOWEST = -3.0e38


class Order:

    def __init__(self, eng, sem, per=None, i=0, before=0):
        self.eng, self.sem, self.per, self.i, self.n = eng, sem, per, i, 0
        self.before = before

    def did(self, ins):
        ins.then_inc(self.sem, 1)
        self.n += 1
        return self.value()

    def value(self):
        return self.n if self.per is None else self.i * self.per + (self.before + self.n)

    def settle(self):
        self.eng.wait_ge(self.sem, self.value())

    def close(self):
        assert self.per is None or self.n == self.per, (self.n, self.per)


class Program:

    def __init__(self, nc, a, out, ctx):
        self.nc, self.a, self.out, self.ctx = nc, a, out, ctx
        self.h = ctx.enter_context(nc.sbuf_tensor("h", [128, NT, D], F32))
        self.ident = ctx.enter_context(nc.sbuf_tensor("ident", [128, 128], F32))
        self.apart = None


def wait_apart(e, P, sem, value):
    e.wait_ge(sem, value)
    e.sem_inc(P.apart, 1)


def token_rows(x_prompt, x_sample):
    return x_prompt[0].rearrange("(t p) d -> p t d", p=128), x_sample.rearrange("b s d -> (b s) d")


def load_and_constants(P):
    nc, a = P.nc, P.a
    zeroed, made = (P.ctx.enter_context(nc.semaphore(x)) for x in ("ident_zeroed", "ident_made"))
    P.h_in = [P.ctx.enter_context(nc.semaphore(f"h_in{i}")) for i in range(NT // 3)]
    P.apart = P.ctx.enter_context(nc.semaphore("apart"))
    with nc.Block() as block:
        @block.sync
        def _(e):
            rows_p, rows_s = token_rows(a["x_prompt"], a["x_sample"])
            for t in range(NT):
                e.dma_start(P.h[:, t, :], rows_p[:, t] if t < NPT else rows_s).then_inc(P.h_in[t // 3], 16)

        @block.gpsimd
        def _(e):
            nc.gpsimd.memset(P.ident[:], 0.0).then_inc(zeroed, 1)
            e.wait_ge(zeroed, 1)
            nc.gpsimd.affine_select(out=P.ident[:], in_=P.ident[:], compare_op=ALU.not_equal, fill=1.0,
                                    base=0, pattern=[[-1, 128]], channel_multiplier=1).then_inc(made, 1)


QR, QC, QD = 4, KC, 32


NORM_GROUPS = tuple((t, t + 3) for t in range(0, NT, 3))


def norm_transpose(P, name, gain, xhi, xlo, blocks=False, beside=None, loading=False):
    nc = P.nc
    with ExitStack() as ctx:
        sb = lambda n, s, d=F32: ctx.enter_context(nc.sbuf_tensor(f"{name}_{n}", s, d))
        gbc = sb("gain", [128, D])
        junk = sb("squares", [128, 2, D])
        stat = sb("stat", [128, NT])
        rstd = sb("rstd", [128, NT])
        un = sb("normed", [128, 3, D])
        pt = ctx.enter_context(nc.psum_tensor(f"{name}_pt", [128, 3, KC, 128], F32))
        s = lambda n: ctx.enter_context(nc.semaphore(f"{name}_{n}"))
        gain_in, squared, mean_ready, rooted, rstd_ready = map(s, ("gain_in", "squared", "mean", "rooted", "rstd"))
        normed, transposed, hi_done, lo_done = map(s, ("normed", "transposed", "hi", "lo"))
        with nc.Block() as block:
            @block.sync
            def _(e):
                e.dma_start(gbc[:], gain.rearrange("(a n) -> a n", a=1).broadcast_to([128, D])).then_inc(gain_in, 16)
                if beside is not None:
                    beside(e)

            @block.scalar
            def _(e):
                def squares(i):
                    for t in range(*NORM_GROUPS[i]):
                        if loading and t % 3 == 0:
                            e.wait_ge(P.h_in[t // 3], 3 * 16)
                        if t >= 2:
                            e.wait_ge(squared, t - 1)
                        nc.scalar.activation(junk[:, t % 2], P.h[:, t], ACT.Square,
                                             accum_out=stat[:, t:t + 1]).then_inc(squared, 1)

                def root(i):
                    e.wait_ge(mean_ready, i + 1)
                    of = slice(*NORM_GROUPS[i])
                    nc.scalar.activation(rstd[:, of], stat[:, of], ACT.Sqrt).then_inc(rooted, 1)

                squares(0)
                root(0)
                for i, group in enumerate(NORM_GROUPS):
                    if i + 1 < len(NORM_GROUPS):
                        squares(i + 1)
                        root(i + 1)
                    for t in range(*group):
                        e.wait_ge(transposed, t + 1)
                        nc.scalar.activation(xhi[:, :, t * 128:(t + 1) * 128], pt[:, t % 3],
                                             ACT.Copy).then_inc(hi_done, 1)

            @block.vector
            def _(e):
                def mean(i):
                    first, end = NORM_GROUPS[i]
                    e.wait_ge(squared, end)
                    s3 = stat[:, first:end]
                    nc.vector.tensor_scalar(s3, s3, 1.0 / D, EPS, ALU.mult, ALU.add).then_inc(mean_ready, 1)

                mean(0)
                nc.vector.sem_inc(lo_done, 3)
                for i, group in enumerate(NORM_GROUPS):
                    e.wait_ge(rooted, i + 1)
                    r3 = rstd[:, group[0]:group[1]]
                    nc.vector.reciprocal(r3, r3).then_inc(rstd_ready, 1)
                    e.wait_ge(rstd_ready, i + 1)
                    if i == 0:
                        e.wait_ge(gain_in, 16)
                    for t in range(*group):
                        u = t % 3
                        e.wait_ge(lo_done, t + 1)
                        h_t = P.h[:, t]
                        parts = [(un[:, u], h_t, gbc[:])]
                        if blocks:
                            parts = [(un[:, u].rearrange("p (c r d) -> p r c d", c=QC, r=QR)[:, r],
                                      *(x[:, r * QC * QD:(r + 1) * QC * QD].rearrange("p (c d) -> p c d", d=QD)
                                        for x in (h_t, gbc[:]))) for r in range(QR)]
                        for dst, x, g in parts:
                            last = nc.vector.scalar_tensor_tensor(
                                out=dst, in0=x, scalar=rstd[:, t:t + 1], in1=g,
                                op0=ALU.mult, op1=ALU.mult)
                        last.then_inc(normed, 1)
                    if i + 1 < len(NORM_GROUPS):
                        mean(i + 1)
                    for t in range(*group):
                        e.wait_ge(hi_done, t + 1)
                        cols = slice(t * 128, (t + 1) * 128)
                        nc.vector.tensor_tensor(xlo[:, :, cols], pt[:, t % 3], xhi[:, :, cols].bitcast(F32),
                                                ALU.subtract).then_inc(lo_done, 1)

            @block.tensor
            def _(e):
                for t in range(NT):
                    e.wait_ge(normed, t + 1)
                    e.wait_ge(lo_done, t + 1)
                    for k in range(KC):
                        last = nc.tensor.transpose(pt[:, t % 3, k], un[:, t % 3, k * 128:(k + 1) * 128], P.ident[:])
                    last.then_inc(transposed, 1)


def three_passes(nc, out, w, x, first, last):
    nc.tensor.matmul(out, w[0], x[0], start=first, stop=False)
    nc.tensor.matmul(out, w[0], x[1], start=False, stop=False)
    return nc.tensor.matmul(out, w[1], x[0], start=False, stop=last)


LB, LB1, GN, CB, BA, BX, SP8, NSP8, CW = range(9)
NPAR = CW + 4


class ChannelParameters:

    def __init__(self, P):
        nc, self.P = P.nc, P
        sb = lambda n, shape: P.ctx.enter_context(nc.sbuf_tensor(n, shape, F32))
        self.par = sb("par", [128, 4, NPAR])
        self.lbraw = sb("lbraw", [128, 2, 4])
        self.tmp = sb("par_tmp", [128, 6, 4])
        self.par_in, self.par_ready, self.act_par, self.dve_par = (
            P.ctx.enter_context(nc.semaphore(n)) for n in ("par_in", "par_ready", "act_par", "dve_par"))

    def load(self, e):
        nc, a, par, lbraw, par_in = self.P.nc, self.P.a, self.par, self.lbraw, self.par_in
        with nc.allow_non_contiguous_dma(reason="small per-channel vectors"):
            for j, v in ((GN, a["g_hgrn_norm"]), (CB, a["conv_b"]), (BA, a["b_rg_a"]), (BX, a["b_rg_x"]),
                         (SP8, a["lambda_rg"])):
                e.dma_start(par[:, :, j], v[0].rearrange("(i p) -> p i", p=128)).then_inc(par_in, 16)
            for j in range(4):
                e.dma_start(par[:, :, CW + j], a["conv_w"][0, j].rearrange("(i p) -> p i", p=128)
                            ).then_inc(par_in, 16)
            for j in range(2):
                e.dma_start(lbraw[:, j], a["lower_bounds"][j].rearrange("(i p) -> p i", p=128)
                            ).then_inc(par_in, 16)

    def scalar(self, e):
        nc, tmp, act_par, dve_par = self.P.nc, self.tmp, self.act_par, self.dve_par
        e.wait_ge(dve_par, 1)
        nc.scalar.activation(tmp[:, 0:2], tmp[:, 0:2], ACT.Exp).then_inc(act_par, 1)
        nc.scalar.activation(tmp[:, 3], tmp[:, 3], ACT.Exp, scale=-1.0).then_inc(act_par, 1)
        e.wait_ge(dve_par, 2)
        nc.scalar.activation(tmp[:, 5], tmp[:, 4], ACT.Ln).then_inc(act_par, 1)

    def vector(self, e):
        nc, par, lbraw, tmp = self.P.nc, self.par, self.lbraw, self.tmp
        par_in, par_ready, act_par, dve_par = self.par_in, self.par_ready, self.act_par, self.dve_par
        v = nc.vector
        o = Order(e, par_ready)

        def link(ins):
            o.did(ins)
            o.settle()

        e.wait_ge(par_in, 11 * 16)
        link(v.tensor_tensor(tmp[:, 2], lbraw[:, 0], lbraw[:, 1], ALU.max))
        link(v.tensor_tensor(tmp[:, 0], lbraw[:, 0], tmp[:, 2], ALU.subtract))
        link(v.tensor_tensor(tmp[:, 1], lbraw[:, 1], tmp[:, 2], ALU.subtract))
        link(v.tensor_scalar(tmp[:, 3], par[:, :, SP8], -1.0, None, ALU.mult))
        v.tensor_tensor(tmp[:, 3], tmp[:, 3], par[:, :, SP8], ALU.max).then_inc(dve_par, 1)
        e.wait_ge(act_par, 2)
        link(v.tensor_tensor(tmp[:, 2], tmp[:, 0], tmp[:, 1], ALU.add))
        link(v.reciprocal(tmp[:, 2], tmp[:, 2]))
        link(v.tensor_tensor(par[:, :, LB], tmp[:, 0], tmp[:, 2], ALU.mult))
        link(v.tensor_scalar(par[:, :, LB1], par[:, :, LB], -1.0, 1.0, ALU.mult, ALU.add))
        v.tensor_scalar(tmp[:, 4], tmp[:, 3], 1.0, None, ALU.add).then_inc(dve_par, 1)
        e.wait_ge(act_par, 3)
        link(v.tensor_scalar(tmp[:, 0], tmp[:, 4], 1.0, None, ALU.is_equal))
        link(v.scalar_tensor_tensor(out=tmp[:, 1], in0=tmp[:, 4], scalar=-1.0, in1=tmp[:, 0],
                                    op0=ALU.add, op1=ALU.add))
        link(v.reciprocal(tmp[:, 1], tmp[:, 1]))
        link(v.tensor_tensor(tmp[:, 5], tmp[:, 5], tmp[:, 0], ALU.add))
        link(v.tensor_tensor(tmp[:, 5], tmp[:, 5], tmp[:, 1], ALU.mult))
        link(v.tensor_tensor(tmp[:, 5], tmp[:, 5], tmp[:, 3], ALU.mult))
        link(v.tensor_scalar(tmp[:, 2], par[:, :, SP8], -1.0, 0.0, ALU.mult, ALU.max))
        link(v.tensor_tensor(tmp[:, 2], tmp[:, 2], tmp[:, 5], ALU.add))
        link(v.tensor_scalar(par[:, :, SP8], tmp[:, 2], 8.0, None, ALU.mult))
        link(v.tensor_scalar(par[:, :, NSP8], tmp[:, 2], -8.0, None, ALU.mult))


class InputWeights:

    def __init__(self, P, ctx):
        self.w_v = P.a["w_in"][0].rearrange("(k p) c -> p k c", p=128)
        self.raw = ctx.enter_context(P.nc.sbuf_tensor("win_raw", [128, 2, KC, 128], F32))
        self.w_in = [ctx.enter_context(P.nc.semaphore(f"win_in{u}")) for u in range(2)]

    def load(self, e, n, u):
        e.dma_start(self.raw[:, u], self.w_v[:, :, bass.ds(n * 128, 128)]).then_inc(self.w_in[u], 16)

    def first(self, e):
        self.load(e, 0, 0)
        self.load(e, 1, 1)


def project_inputs(P, xhi, xlo, z_dram, loads):
    nc = P.nc
    NB = P.a["w_in"].shape[2] // 128
    raw, w_in = loads.raw, loads.w_in
    with ExitStack() as ctx:
        whi = ctx.enter_context(nc.sbuf_tensor("win_hi", [128, 2, KC, 128], F32R))
        wlo = ctx.enter_context(nc.sbuf_tensor("win_lo", [128, 2, KC, 128], F32R))
        zst = ctx.enter_context(nc.sbuf_tensor("z_stage", [128, 2, T], F32))
        pz = ctx.enter_context(nc.psum_tensor("pz", [128, NN, 512], F32))
        s = lambda n: ctx.enter_context(nc.semaphore(n))
        z_out = [s(f"z_out{u}") for u in range(2)]
        hi_done, lo_done, mm_done, z_ready = map(s, ("win_hi_done", "win_lo_done", "z_summed", "z_ready"))
        with nc.Block() as block:
            @block.sync
            def _(e):
                nc.sync.sem_inc(z_out[0], 16)
                nc.sync.sem_inc(z_out[1], 16)

                def load(i, u):
                    e.wait_ge(lo_done, i * 2 + u + 1)
                    loads.load(e, i * 2 + u, u)

                def store(i, u):
                    e.wait_ge(z_ready, (i * 2 + u + 2) * NN)
                    e.dma_start(z_dram[bass.ds(i * 2 + u, 1)].rearrange("a p t -> p (a t)"),
                                zst[:, u]).then_inc(z_out[u], 16)

                P.channels.load(e)
                with e.Fori(0, NB // 2 - 1) as i:
                    load(i + 1, 0)
                    store(i, 0)
                    load(i + 1, 1)
                    store(i, 1)
                store(NB // 2 - 1, 0)
                store(NB // 2 - 1, 1)
                e.wait_ge(z_out[0], (NB // 2 + 1) * 16)
                e.wait_ge(z_out[1], (NB // 2 + 1) * 16)

            @block.scalar
            def _(e):
                nc.scalar.sem_inc(z_ready, NN)

                def hi(i, u):
                    e.wait_ge(w_in[u], (i + 1) * 16)
                    e.wait_ge(mm_done, (i * 2 + u + 1) * NN)
                    nc.scalar.activation(whi[:, u], raw[:, u], ACT.Copy).then_inc(hi_done, 1)

                def evacuate(i, u):
                    e.wait_ge(z_out[u], (i + 1) * 16)
                    for n in range(NN):
                        e.wait_ge(mm_done, (i * 2 + u + 2) * NN + n + 1)
                        nc.scalar.activation(zst[:, u, n * NW:(n + 1) * NW], pz[:, n, 0:NW],
                                             ACT.Copy).then_inc(z_ready, 1)

                hi(0, 0)
                P.channels.scalar(e)
                with e.Fori(0, NB // 2 - 1) as i:
                    hi(i, 1)
                    evacuate(i, 0)
                    hi(i + 1, 0)
                    evacuate(i, 1)
                last = NB // 2 - 1
                hi(last, 1)
                evacuate(last, 0)
                evacuate(last, 1)

            @block.vector
            def _(e):
                nc.vector.sem_inc(lo_done, 2)

                def lo(i, u):
                    e.wait_ge(hi_done, i * 2 + u + 1)
                    nc.vector.tensor_tensor(wlo[:, u], raw[:, u], whi[:, u].bitcast(F32),
                                            ALU.subtract).then_inc(lo_done, 1)

                lo(0, 0)
                P.channels.vector(e)
                with e.Fori(0, NB // 2 - 1) as i:
                    lo(i, 1)
                    lo(i + 1, 0)
                lo(NB // 2 - 1, 1)

            @block.tensor
            def _(e):
                nc.tensor.sem_inc(mm_done, 2 * NN)
                with e.Fori(0, NB // 2) as i:
                    for u in range(2):
                        e.wait_ge(lo_done, i * 2 + u + 3)
                        for n in range(NN):
                            e.wait_ge(z_ready, (i * 2 + u) * NN + n + 1)
                            for k in range(KC):
                                mm = three_passes(nc, pz[:, n, 0:NW], (whi[:, u, k], wlo[:, u, k]),
                                                  (xhi[:, k, n * NW:(n + 1) * NW], xlo[:, k, n * NW:(n + 1) * NW]),
                                                  k == 0, k == KC - 1)
                            mm.then_inc(mm_done, 1)


def mixers(P, z_dram, cat):
    nc, a, out = P.nc, P.a, P.out
    with ExitStack() as ctx:
        def sb(n, shape, d=F32):
            return ctx.enter_context(nc.sbuf_tensor(f"mx_{n}", shape, d))
        used = []

        def s(n):
            used.append(nc.alloc_semaphore(f"mx_{n}"))
            return used[-1]

        zq, zf, zv, zg, zy = (sb(n, [128, T]) for n in ("zq", "zf", "zv", "zg", "zy"))
        xp = sb("xp", [128, SEQ + 3])
        xs = sb("xs", [128, DB, DS + 3])
        sf, sq, cum, e1, e2, e3, xc, r, ig = (sb(n, [128, T]) for n in (
            "sf", "sq", "cum", "e1", "e2", "e3", "xc", "r", "ig"))
        gs = sb("gs", [128, T])
        scan_mask = sb("scan_mask", [128, T])
        vtok, kdtok, att, on = (sb(n, [128, NT, 128]) for n in ("vtok", "kdtok", "att", "on"))
        states = sb("states", [128, NCH + 1, 128])
        s0 = sb("s0", [128, DB, 128])
        snew = sb("snew", [128, DB, 128])
        vmask = sb("vmask", [128, DB, 128])
        qdz = sb("qdz", [128, DB * (128 + DS)])
        wg = sb("wg", [128, 2, 128])
        rows_in = sb("rows_in", [128, 128])
        cols_out = sb("cols_out", [128, 128])
        rows_out = sb("rows_out", [36, 128])
        mask_p = sb("mask_p", [128, 128])
        mask_s = sb("mask_s", [128, 128])
        bmask = sb("bmask", [128, DB])
        rs = sb("rs", [128, NT])
        par = P.channels.par
        cur = sb("cur", [128, NPAR])
        gps = ctx.enter_context(nc.psum_tensor("mx_ps", [128, 8, 512], F32))
        flat = gps[:].rearrange("p b n -> p (b n)")
        ps_v = flat[:, 0:T].rearrange("p (t c) -> p t c", c=128)
        ps_kd = flat[:, 1536:1536 + T].rearrange("p (t c) -> p t c", c=128)
        ps_ds = flat[:, 0:2048].rearrange("p (c n) -> p c n", n=128)
        ds_of = lambda c: ps_ds[:, (c % 2) * (NCH // 2) + c // 2]
        ps_dss = flat[:, 2048:3072].rearrange("p (c n) -> p c n", n=128)
        ps_att, ps_o, ps_ont = ps_v, ps_kd, ps_v
        ps_state = gps[:, 6, 0:128]
        ps_rows = gps[:, 6, 128:256]

        PROMPT, SAMPLE = slice(0, SEQ), slice(SEQ, T)

        def by(x, n):
            return x.rearrange("p (c n) -> p c n", n=n)

        consts, in_f, in_q, in_v, in_g, in_y, in_x, in_s, in_rows, in_wg = map(s, (
            "consts", "in_f", "in_q", "in_v", "in_g", "in_y", "in_x", "in_s", "in_rows", "in_wg"))

        def z_of(i, c):
            return z_dram[bass.ds(i + 4 * c, 1)].rearrange("a p t -> p (a t)")

        def load_z(e, dst, i, c, sem):
            e.dma_start(dst[:], z_of(i, c)).then_inc(sem, 16)

        def load_f(e, i):
            load_z(e, zf, i, 1, in_f)

        def load_q(e, i):
            load_z(e, zq, i, 0, in_q)

        def load_v(e, i):
            load_z(e, zv, i, 2, in_v)

        def load_g(e, i):
            load_z(e, zg, i, 3, in_g)

        def load_y(e, i):
            load_z(e, zy, i, 5, in_y)

        def load_x(e, i):
            e.dma_start(xp[:, 3:], z_of(i, 4)[:, PROMPT]).then_inc(in_x, 16)
            e.dma_start(xs[:, :, 3:], by(z_of(i, 4)[:, SAMPLE], DS)).then_inc(in_x, 16)

        def load_s(e, i):
            e.dma_start(s0[:], a["state_hgrn"][0, :, bass.ds(i, 1)].rearrange("b a d v -> d (b a) v")
                        ).then_inc(in_s, 16)

        def load_rows(e, i):
            cols = bass.ds(i * 128, 128)
            e.dma_start(rows_in[0:24, :], a["state_conv"][0, :, :, cols].rearrange("b j c -> (b j) c")
                        ).then_inc(in_rows, 16)
            e.dma_start(rows_in[24:32, :], a["state_rglru"][0, :, cols]).then_inc(in_rows, 16)

        def load_wg(e, i):
            for w, src in ((0, a["w_rg_a"]), (1, a["w_rg_x"])):
                for q in range(2):
                    e.dma_start(wg[64 * q:64 * q + 64, w, 64 * q:64 * q + 64],
                                src[0, bass.ds(i * 2 + q, 1)].rearrange("a c d -> c (a d)")).then_inc(in_wg, 16)

        with nc.Block() as block:
            @block.sync
            def _(e):
                for load in (load_f, load_x, load_v, load_q, load_g, load_s, load_y):
                    load(e, 0)


            @block.gpsimd
            def _(e):
                o = Order(e, consts)
                for m, value in ((mask_p, 1.0), (mask_s, 1.0), (bmask, 1.0), (scan_mask, 1.0), (att, 0.0), (qdz, 0.0),
                                 (wg, 0.0), (rows_in, 0.0), (cols_out, 0.0)):
                    o.did(nc.gpsimd.memset(m[:], value))
                o.did(nc.gpsimd.memset(states[:, 0], 0.0))
                o.did(nc.gpsimd.memset(xp[:, 0:3], 0.0))
                o.settle()
                for m in (mask_p, mask_s):
                    o.did(nc.gpsimd.affine_select(out=m[:], in_=m[:], compare_op=ALU.is_ge, fill=0.0, base=0,
                                                  pattern=[[1, 128]], channel_multiplier=-1))
                o.did(nc.gpsimd.affine_select(out=bmask[:], in_=bmask[:], compare_op=ALU.is_ge, fill=0.0, base=0,
                                              pattern=[[-DS, DB]], channel_multiplier=1))
                o.did(nc.gpsimd.memset(scan_mask[:, 0:SEQ].rearrange("p (c n) -> p c n", n=CH)[:, :, 0:1], 0.0))
                o.did(nc.gpsimd.memset(scan_mask[:, SEQ:T].rearrange("p (c n) -> p c n", n=DS)[:, :, 0:1], 0.0))
                o.settle()
                o.did(nc.gpsimd.memset(mask_p[0:CH, CH:128], 0.0))
                o.did(nc.gpsimd.affine_select(out=mask_s[:].rearrange("p (b r) -> p b r", r=DS),
                                              in_=mask_s[:].rearrange("p (b r) -> p b r", r=DS),
                                              compare_op=ALU.is_ge, fill=0.0, base=0,
                                              pattern=[[-DS, DB], [0, DS]], channel_multiplier=1))
                o.did(nc.gpsimd.affine_select(out=bmask[:], in_=bmask[:], compare_op=ALU.is_ge, fill=0.0,
                                              base=DS - 1, pattern=[[DS, DB]], channel_multiplier=-1))
                o.settle()

        (stored, cur_ready, all_used, sig_f, sig_q, sig_g, sig_r, sig_i, f_ready, ln_f, cum_ready, dl_ready,
         exp_cum, exp_dl, exp_a, qk_ready, kdec_ready, v_t, kdec_t, v_tok, kdec_tok, vmask_ready, ds_ready, dss_ready,
         st_ready, sn_ready, att_sum, att_ready, qdz_ready, o_sum, o_sq, ms_ready, rms_root, on_ready, on_t,
         state_t, xc_ready, silu_g, gates, va_ready, sqrt_b, gelu_y, oc_ready, oc_t, rows_ready, self_ok) = (s(n) for n in (
             "stored", "cur", "used", "sig_f", "sig_q", "sig_g", "sig_r", "sig_i", "f", "ln_f", "cum", "dl",
             "exp_cum", "exp_dl", "exp_a", "qk", "kdec", "v_t", "kdec_t", "v_tok", "kdec_tok", "vmask", "ds", "dss",
             "st", "sn", "att_sum", "att", "qdz", "o_sum", "o_sq", "ms", "rms_root", "on", "on_t",
             "state_t", "xc", "silu_g", "gates", "va", "sqrt_b", "gelu_y", "oc", "oc_t", "rows", "self"))
        NSTORE = 6

        with nc.Block() as block:
            @block.sync
            def _(e):
                nc.sync.sem_inc(stored, NSTORE * 16)

                def unit(i, more):
                    cols = bass.ds(i * 128, 128)
                    if more:
                        e.wait_ge(state_t, i + 1)
                        load_rows(e, i + 1)
                        e.wait_ge(v_t, i + 1)
                        load_v(e, i + 1)
                        e.wait_ge(gates, i + 1)
                        load_wg(e, i + 1)
                        e.wait_ge(kdec_ready, i + 1)
                        load_f(e, i + 1)
                        load_g(e, i + 1)
                    e.wait_ge(st_ready, i + 1)
                    e.dma_start(out["hgrn_p"][0, 0, bass.ds(i, 1)].rearrange("a d v -> d (a v)"),
                                states[:, NCH]).then_inc(stored, 16)
                    e.wait_ge(sn_ready, i + 1)
                    e.dma_start(out["hgrn_s"][0, :, bass.ds(i, 1)].rearrange("b a d v -> d (b a) v"),
                                snew[:]).then_inc(stored, 16)
                    if more:
                        e.wait_ge(o_sum, i + 1)
                        load_q(e, i + 1)
                        load_s(e, i + 1)
                        e.wait_ge(oc_ready, i + 1)
                        load_x(e, i + 1)
                        e.wait_ge(gelu_y, i + 1)
                        load_y(e, i + 1)
                    e.wait_ge(rows_ready, i + 1)
                    e.dma_start(out["conv_p"][0, 0, :, cols], rows_out[0:3, :]).then_inc(stored, 16)
                    e.dma_start(out["conv_s"][0, :, :, cols].rearrange("b j c -> (b j) c"),
                                rows_out[3:27, :]).then_inc(stored, 16)
                    e.dma_start(out["rglru_p"][0, :, cols], rows_out[27:28, :]).then_inc(stored, 16)
                    e.dma_start(out["rglru_s"][0, :, cols], rows_out[28:36, :]).then_inc(stored, 16)

                load_rows(e, 0)
                load_wg(e, 0)
                with e.Fori(0, 3) as i:
                    unit(i, True)
                unit(3, False)
                e.wait_ge(stored, 5 * NSTORE * 16)

            @block.scalar
            def _(e):
                f = nc.scalar.activation
                with e.Fori(0, 4) as i:
                    e.wait_ge(all_used, i + 1)
                    e.wait_ge(in_f, (i + 1) * 16)
                    f(sf[:], zf[:], ACT.Sigmoid).then_inc(sig_f, 1)
                    e.wait_ge(in_q, (i + 1) * 16)
                    f(sq[:], zq[:], ACT.Sigmoid).then_inc(sig_q, 1)
                    e.wait_ge(in_g, (i + 1) * 16)
                    f(e3[:], zg[:], ACT.Sigmoid).then_inc(sig_g, 1)
                    e.wait_ge(v_t, i + 1)
                    f(vtok[:], ps_v, ACT.Copy).then_inc(v_tok, 1)
                    e.wait_ge(f_ready, i + 1)
                    f(cum[:], sf[:], ACT.Ln).then_inc(ln_f, 1)
                    e.wait_ge(cum_ready, i + 1)
                    f(e1[:], sf[:], ACT.Exp).then_inc(exp_cum, 1)
                    f(e2[:], sf[:], ACT.Exp, scale=-1.0).then_inc(exp_cum, 1)
                    e.wait_ge(dl_ready, i + 1)
                    e.wait_ge(silu_g, i + 1)
                    f(e3[:], cum[:], ACT.Exp).then_inc(exp_dl, 1)
                    e.wait_ge(cur_ready, i + 1)
                    e.wait_ge(gates, i + 1)
                    for dst, at, bias, done in ((r, 0, BA, sig_r), (ig, 3, BX, sig_i)):
                        f(dst[:].rearrange("p (n w) -> p n w", w=NW), gps[:, at:at + 3, 0:NW], ACT.Sigmoid,
                          bias=cur[:, bias:bias + 1]).then_inc(done, 1)
                    e.wait_ge(sig_r, i + 1)
                    e.wait_ge(exp_cum, i * 2 + 2)
                    f(sf[:], r[:], ACT.Tanh, scale=cur[:, SP8:SP8 + 1]).then_inc(exp_a, 1)
                    e.wait_ge(exp_a, i * 2 + 1)
                    f(r[:], r[:], ACT.Exp, scale=cur[:, NSP8:NSP8 + 1]).then_inc(exp_a, 1)
                    e.wait_ge(va_ready, i + 1)
                    f(sf[:], sf[:], ACT.Sqrt).then_inc(sqrt_b, 1)
                    e.wait_ge(o_sum, i + 1)
                    f(cum[:].rearrange("p (t c) -> p t c", c=128), ps_o, ACT.Square).then_inc(o_sq, 1)
                    e.wait_ge(ms_ready, i + 1)
                    f(rs[:], rs[:], ACT.Sqrt).then_inc(rms_root, 1)
                    e.wait_ge(in_y, (i + 1) * 16)
                    f(sq[:], zy[:], ACT.Gelu_apprx_tanh).then_inc(gelu_y, 1)

            @block.vector
            def _(e):
                v = nc.vector
                nc.vector.sem_inc(all_used, 1)
                PER = 40
                with e.Fori(0, 4) as i:
                    o = Order(e, self_ok, PER, i)

                    def link(ins):
                        o.did(ins)
                        o.settle()

                    e.wait_ge(all_used, i + 1)
                    v.tensor_copy(cur[:], par[:, bass.ds(i, 1)].rearrange("p a n -> p (a n)")).then_inc(cur_ready, 1)
                    e.wait_ge(cur_ready, i + 1)
                    e.wait_ge(state_t, i + 1)
                    e.wait_ge(in_x, (i + 1) * 32)
                    link(v.tensor_copy(xs[:, :, 0:3], ps_state[:, 0:24].rearrange("p (b j) -> p b j", j=3)))
                    link(v.tensor_scalar(xc[:, PROMPT], xp[:, 0:SEQ], cur[:, CW:CW + 1], cur[:, CB:CB + 1],
                                         ALU.mult, ALU.add))
                    link(v.tensor_scalar(by(xc[:, SAMPLE], DS), xs[:, :, 0:DS], cur[:, CW:CW + 1],
                                         cur[:, CB:CB + 1], ALU.mult, ALU.add))
                    e.wait_ge(sig_f, i + 1)
                    v.tensor_scalar(sf[:], sf[:], cur[:, LB1:LB1 + 1], cur[:, LB:LB + 1],
                                    ALU.mult, ALU.add).then_inc(f_ready, 1)
                    e.wait_ge(f_ready, i + 1)
                    link(v.tensor_scalar(zf[:], sf[:], -1.0, 1.0, ALU.mult, ALU.add))
                    for j in range(1, 4):
                        tap = cur[:, CW + j:CW + j + 1]
                        link(v.scalar_tensor_tensor(out=xc[:, PROMPT], in0=xp[:, j:j + SEQ], scalar=tap,
                                                    in1=xc[:, PROMPT], op0=ALU.mult, op1=ALU.add))
                        ins = v.scalar_tensor_tensor(out=by(xc[:, SAMPLE], DS), in0=xs[:, :, j:j + DS], scalar=tap,
                                                     in1=by(xc[:, SAMPLE], DS), op0=ALU.mult, op1=ALU.add)
                        if j < 3:
                            link(ins)
                        else:
                            ins.then_inc(xc_ready, 1)
                    e.wait_ge(xc_ready, i + 1)
                    e.wait_ge(ln_f, i + 1)
                    v.tensor_tensor_scan(sf[:], scan_mask[:], cum[:], 0.0, ALU.mult, ALU.add).then_inc(cum_ready, 1)
                    e.wait_ge(cum_ready, i + 1)
                    for cols, n in ((PROMPT, CH), (SAMPLE, DS)):
                        c = by(sf[:, cols], n)
                        ins = v.tensor_tensor(by(cum[:, cols], n), c[:, :, n - 1:n].broadcast_to(list(c.shape)), c,
                                              ALU.subtract)
                        if n == DS:
                            ins.then_inc(dl_ready, 1)
                        else:
                            o.did(ins)
                    e.wait_ge(sig_q, i + 1)
                    link(v.tensor_tensor(zq[:], zq[:], sq[:], ALU.mult))
                    e.wait_ge(sig_g, i + 1)
                    v.tensor_tensor(gs[:], zg[:], e3[:], ALU.mult).then_inc(silu_g, 1)
                    e.wait_ge(exp_cum, i * 2 + 2)
                    o.did(v.tensor_tensor(zq[:], zq[:], e1[:], ALU.mult))
                    v.tensor_tensor(e2[:], zf[:], e2[:], ALU.mult).then_inc(qk_ready, 1)
                    e.wait_ge(exp_dl, i + 1)
                    v.tensor_tensor(e3[:], zf[:], e3[:], ALU.mult).then_inc(kdec_ready, 1)
                    o.settle()
                    v.tensor_copy(by(qdz[:], 128 + DS)[:, :, 0:DS], by(zq[:, SAMPLE], DS)).then_inc(qdz_ready, 1)
                    e.wait_ge(v_tok, i + 1)
                    for b in range(DB):
                        ins = v.tensor_scalar(vmask[:, b], vtok[:, NPT], bmask[:, b:b + 1], None, ALU.mult)
                    ins.then_inc(vmask_ready, 1)
                    wait_apart(e, P, att_sum, i + 1)
                    v.copy_predicated(att[:, 0:NPT], mask_p[:].bitcast(I32).rearrange("p (a n) -> p a n", a=1)
                                      .broadcast_to([128, NPT, 128]), ps_att[:, 0:NPT])
                    v.copy_predicated(att[:, NPT], mask_s[:].bitcast(I32), ps_att[:, NPT]).then_inc(att_ready, 1)
                    e.wait_ge(kdec_t, i + 1)
                    v.tensor_copy(kdtok[:], ps_kd).then_inc(kdec_tok, 1)
                    e.wait_ge(exp_a, i * 2 + 2)
                    link(v.tensor_tensor(cum[:], r[:], r[:], ALU.mult))
                    v.scalar_tensor_tensor(out=sf[:], in0=cum[:], scalar=1.0, in1=sf[:],
                                           op0=ALU.add, op1=ALU.mult).then_inc(va_ready, 1)
                    e.wait_ge(sig_i, i + 1)
                    link(v.tensor_tensor(ig[:], ig[:], xc[:], ALU.mult))
                    e.wait_ge(stored, (i + 1) * NSTORE * 16)
                    for c in range(NCH):
                        at = (c + 1) * CH - 1
                        if c % (NCH // 2) == 0:
                            e.wait_ge(ds_ready, i * 2 + c // (NCH // 2) + 1)
                        ins = v.scalar_tensor_tensor(out=states[:, c + 1], in0=states[:, c], scalar=e1[:, at:at + 1],
                                                     in1=ds_of(c), op0=ALU.mult, op1=ALU.add)
                        if c < NCH - 1:
                            link(ins)
                        else:
                            ins.then_inc(st_ready, 1)
                    e.wait_ge(dss_ready, i + 1)
                    e.wait_ge(in_s, (i + 1) * 16)
                    for b in range(DB):
                        at = SEQ + (b + 1) * DS - 1
                        ins = v.scalar_tensor_tensor(out=snew[:, b], in0=s0[:, b], scalar=e1[:, at:at + 1],
                                                     in1=ps_dss[:, b], op0=ALU.mult, op1=ALU.add)
                    ins.then_inc(sn_ready, 1)
                    e.wait_ge(sqrt_b, i + 1)
                    link(v.tensor_tensor(ig[:], ig[:], sf[:], ALU.mult))
                    first_a, first_b = by(r[:, SAMPLE], DS)[:, :, 0], by(ig[:, SAMPLE], DS)[:, :, 0]
                    link(v.tensor_tensor(e3[:, 0:DB], first_a, ps_state[:, 24:32], ALU.mult))
                    link(v.tensor_tensor(first_b, first_b, e3[:, 0:DB], ALU.add))
                    link(v.memset(first_a, 0.0))
                    link(v.tensor_tensor_scan(xc[:], r[:], ig[:], 0.0, ALU.mult, ALU.add))
                    o.did(v.tensor_copy(cols_out[:, 0:3], xp[:, SEQ:SEQ + 3]))
                    o.did(v.tensor_copy(cols_out[:, 3:27].rearrange("p (b j) -> p b j", j=3), xs[:, :, DS:DS + 3]))
                    o.did(v.tensor_copy(cols_out[:, 27:28], xc[:, SEQ - 1:SEQ]))
                    v.tensor_copy(cols_out[:, 28:36], by(xc[:, SAMPLE], DS)[:, :, DS - 1]).then_inc(oc_ready, 1)
                    e.wait_ge(o_sq, i + 1)
                    link(v.tensor_reduce(rs[:], cum[:].rearrange("p (t c) -> p t c", c=128), AX.X, ALU.add))
                    v.tensor_scalar(rs[:], rs[:], 1.0 / 128, EPS, ALU.mult, ALU.add).then_inc(ms_ready, 1)
                    e.wait_ge(rms_root, i + 1)
                    link(v.reciprocal(rs[:], rs[:]))
                    v.tensor_tensor(on[:], ps_o, rs[:].rearrange("p (t a) -> p t a", a=1).broadcast_to([128, NT, 128]),
                                    ALU.mult).then_inc(on_ready, 1)
                    e.wait_ge(gelu_y, i + 1)
                    link(v.tensor_tensor(cat[:, bass.ds(i + 4, 1)].rearrange("p a t -> p (a t)"), xc[:], sq[:],
                                         ALU.mult))
                    e.wait_ge(oc_t, i + 1)
                    v.tensor_copy(rows_out[:], ps_rows[0:36]).then_inc(rows_ready, 1)
                    e.wait_ge(on_t, i + 1)
                    e.wait_ge(stored, (i + 1) * NSTORE * 16)
                    v.scalar_tensor_tensor(out=cat[:, bass.ds(i, 1)].rearrange("p a t -> p (a t)"),
                                           in0=flat[:, 0:T], scalar=cur[:, GN:GN + 1], in1=gs[:],
                                           op0=ALU.mult, op1=ALU.mult).then_inc(all_used, 1)
                    o.close()

            @block.tensor
            def _(e):
                mm, tr = nc.tensor.matmul, nc.tensor.transpose
                with e.Fori(0, 4) as i:
                    e.wait_ge(all_used, i + 1)
                    e.wait_ge(in_rows, (i + 1) * 32)
                    tr(ps_state, rows_in[:], P.ident[:]).then_inc(state_t, 1)
                    e.wait_ge(in_v, (i + 1) * 16)
                    for t in range(NT):
                        last = tr(ps_v[:, t], zv[:, t * 128:(t + 1) * 128], P.ident[:])
                    last.then_inc(v_t, 1)
                    e.wait_ge(in_wg, (i + 1) * 64)
                    e.wait_ge(xc_ready, i + 1)
                    e.wait_ge(v_tok, i + 1)
                    for n in range(NN):
                        for w in range(2):
                            last = mm(gps[:, 3 * w + n, 0:NW], wg[:, w], xc[:, n * NW:(n + 1) * NW],
                                      start=True, stop=True)
                    last.then_inc(gates, 1)
                    e.wait_ge(qk_ready, i + 1)
                    e.wait_ge(sig_r, i + 1)
                    for t in range(NT):
                        cols = slice(t * 128, (t + 1) * 128)
                        last = mm(ps_att[:, t], e2[:, cols], zq[:, cols], start=True, stop=True)
                    last.then_inc(att_sum, 1)
                    e.wait_ge(sig_i, i + 1)
                    e.wait_ge(kdec_ready, i + 1)
                    for t in range(NT):
                        last = tr(ps_kd[:, t], e3[:, t * 128:(t + 1) * 128], P.ident[:])
                    last.then_inc(kdec_t, 1)
                    e.wait_ge(att_ready, i + 1)
                    e.wait_ge(kdec_tok, i + 1)
                    for c in range(NCH):
                        t, half = c // 2, slice(CH * (c % 2), CH * (c % 2) + CH)
                        last = mm(ds_of(c), kdtok[half, t], vtok[half, t], start=True, stop=True)
                        if c % (NCH // 2) == NCH // 2 - 1:
                            last.then_inc(ds_ready, 1)
                    e.wait_ge(vmask_ready, i + 1)
                    for q in range(2):
                        last = mm(ps_dss[:, 4 * q:4 * q + 4].rearrange("p b n -> p (b n)"), kdtok[:, NPT],
                                  vmask[:, 4 * q:4 * q + 4].rearrange("p b n -> p (b n)"), start=True, stop=True)
                    last.then_inc(dss_ready, 1)
                    e.wait_ge(st_ready, i + 1)
                    e.wait_ge(qdz_ready, i + 1)
                    for t in range(NPT):
                        if t == 4:
                            e.wait_ge(sn_ready, i + 1)
                        mm(ps_o[:, t], att[:, t], vtok[:, t], start=True, stop=False, skip_group_check=True)
                        for q in range(2):
                            half = slice(CH * q, CH * q + CH)
                            mm(ps_o[half, t], zq[:, t * 128 + CH * q:t * 128 + CH * q + CH], states[:, 2 * t + q],
                               start=False, stop=True, skip_group_check=True)
                    mm(ps_o[:, NPT], att[:, NPT], vtok[:, NPT], start=True, stop=False, skip_group_check=True)
                    for b in range(DB):
                        last = mm(ps_o[:, NPT], qdz[:, b * 128:(b + 1) * 128], s0[:, b], start=False,
                                  stop=b == DB - 1, skip_group_check=True)
                    last.then_inc(o_sum, 1)
                    e.wait_ge(oc_ready, i + 1)
                    tr(ps_rows, cols_out[:], P.ident[:]).then_inc(oc_t, 1)
                    e.wait_ge(on_ready, i + 1)
                    for t in range(NT):
                        last = tr(ps_ont[:, t], on[:, t], P.ident[:])
                    last.then_inc(on_t, 1)
        nc.clear_and_free_semaphores(used)
        nc.all_engine_barrier()


def output_projection(P, cat):
    nc = P.nc
    w_v = P.a["w_out"][0].rearrange("(k p) c -> p k c", p=128)
    with ExitStack() as ctx:
        def sb(n, shape, d=F32):
            return ctx.enter_context(nc.sbuf_tensor(f"op_{n}", shape, d))
        s = lambda n: ctx.enter_context(nc.semaphore(f"op_{n}"))
        raw = sb("raw", [128, 2, D])
        whi, wlo = sb("whi", [128, KC, D], F32R), sb("wlo", [128, KC, D], F32R)
        chi, clo = sb("chi", [128, 3, KC, 128], F32R), sb("clo", [128, 3, KC, 128], F32R)
        po = ctx.enter_context(nc.psum_tensor("op_ps", [128, 3, D], F32))
        w_in = [s(f"w_in{u}") for u in range(2)]
        whi_done, wlo_done, chi_done, clo_done, summed, added = map(
            s, ("whi", "wlo", "chi", "clo", "summed", "added"))
        with nc.Block() as block:
            @block.sync
            def _(e):
                for k in range(KC):
                    if k >= 2:
                        e.wait_ge(wlo_done, k - 1)
                    e.dma_start(raw[:, k % 2], w_v[:, k]).then_inc(w_in[k % 2], 16)

            @block.scalar
            def _(e):
                def c_hi(t):
                    nc.scalar.activation(chi[:, t % 3], cat[:, :, t * 128:(t + 1) * 128],
                                         ACT.Copy).then_inc(chi_done, 1)

                for k in range(KC):
                    if k < 3:
                        c_hi(k)
                    e.wait_ge(w_in[k % 2], (k // 2 + 1) * 16)
                    nc.scalar.activation(whi[:, k], raw[:, k % 2], ACT.Copy).then_inc(whi_done, 1)
                for t in range(3, NT):
                    e.wait_ge(summed, t - 2)
                    c_hi(t)

            @block.vector
            def _(e):
                def c_lo(t):
                    e.wait_ge(chi_done, t + 1)
                    nc.vector.tensor_tensor(clo[:, t % 3], cat[:, :, t * 128:(t + 1) * 128],
                                            chi[:, t % 3].bitcast(F32), ALU.subtract).then_inc(clo_done, 1)

                for k in range(KC):
                    if k < 3:
                        c_lo(k)
                    e.wait_ge(whi_done, k + 1)
                    nc.vector.tensor_tensor(wlo[:, k], raw[:, k % 2], whi[:, k].bitcast(F32),
                                            ALU.subtract).then_inc(wlo_done, 1)
                for t in range(NT):
                    e.wait_ge(summed, t + 1)
                    nc.vector.tensor_tensor(P.h[:, t], po[:, t % 3], P.h[:, t], ALU.add).then_inc(added, 1)
                    if t + 3 < NT:
                        c_lo(t + 3)

            @block.tensor
            def _(e):
                def product(t, k):
                    for q in range(2):
                        cols = slice(512 * q, 512 * q + 512)
                        last = three_passes(nc, po[:, t % 3, cols], (chi[:, t % 3, k], clo[:, t % 3, k]),
                                            (whi[:, k, cols], wlo[:, k, cols]), k == 0, k == KC - 1)
                    return last

                for k in range(KC):
                    e.wait_ge(wlo_done, k + 1)
                    for t in range(3):
                        if k == 0:
                            e.wait_ge(clo_done, t + 1)
                        last = product(t, k)
                        if k == KC - 1:
                            last.then_inc(summed, 1)
                for t in range(3, NT):
                    e.wait_ge(clo_done, t + 1)
                    e.wait_ge(added, t - 2)
                    for k in range(KC):
                        last = product(t, k)
                    last.then_inc(summed, 1)


class RouteLoads:

    def __init__(self, P, ctx):
        nc = P.nc
        self.ctx = ctx.enter_context(ExitStack())
        sb = lambda n, shape: self.ctx.enter_context(nc.sbuf_tensor(f"rs_{n}", shape, F32))
        self.w_v = P.a["w_peer_q"][0].rearrange("(r c d) n -> r d c n", r=QR, c=QC)
        self.keys = P.a["peer_keys"][0].rearrange("h p n c -> (h p) n c")
        self.raw, self.kraw = sb("raw", [128, 2, KC, 128]), sb("kraw", [128, 2, 128])
        self.w_in = [self.ctx.enter_context(nc.semaphore(f"rs_w_in{u}")) for u in range(2)]

    def load(self, e, n, u):
        for r in range(QR):
            e.dma_start(self.raw[32 * r:32 * r + 32, u], self.w_v[r, :, :, bass.ds(n * 128, 128)]
                        ).then_inc(self.w_in[u], 16)
        e.dma_start(self.kraw[:, u], self.keys[bass.ds(n, 1)].rearrange("a n c -> n (a c)")
                    ).then_inc(self.w_in[u], 16)

    def first(self, e):
        self.load(e, 0, 0)
        self.load(e, 1, 1)

    def free(self):
        self.ctx.close()


def route_scores(P, xhi, xlo, sv, si, loads):
    nc = P.nc
    raw, kraw, w_in = loads.raw, loads.kraw, loads.w_in
    with ExitStack() as ctx:
        def sb(n, shape, d=F32):
            return ctx.enter_context(nc.sbuf_tensor(f"rs_{n}", shape, d))
        s = lambda n: ctx.enter_context(nc.semaphore(f"rs_{n}"))
        whi, wlo = sb("whi", [128, 2, KC, 128], F32R), sb("wlo", [128, 2, KC, 128], F32R)
        kt = sb("kt", [128, 2, 128])
        q = sb("q", [128, T])
        rest = sb("rest", [128, NT, 128])
        val16, ind16 = sb("val16", [128, NT, K]), sb("ind16", [128, NT, K], U32)
        pq = ctx.enter_context(nc.psum_tensor("rs_pq", [128, 2, 512], F32))
        pk = ctx.enter_context(nc.psum_tensor("rs_pk", [128, 512], F32))
        psc = ctx.enter_context(nc.psum_tensor("rs_sc", [128, 3, 4, 128], F32))
        scores = [psc[:, t // 4, t % 4] for t in range(NT)]
        hi_done, lo_done, q_sum, q_ready, k_t, kt_ready, scored, ranked, self_ok = map(
            s, ("hi", "lo", "q_sum", "q_ready", "k_t", "kt", "scored", "ranked", "self"))
        LAST = HP // 2 - 1
        with nc.Block() as block:
            @block.sync
            def _(e):
                with e.Fori(0, HP // 2 - 1) as i:
                    for u in range(2):
                        n = i * 2 + (2 + u)
                        e.wait_ge(lo_done, n + 1)
                        e.wait_ge(k_t, n + 1)
                        loads.load(e, n, u)

            @block.scalar
            def _(e):
                nc.scalar.sem_inc(q_ready, 2)
                nc.scalar.sem_inc(kt_ready, 2)

                def hi(i, u):
                    n = i * 2 + u
                    e.wait_ge(w_in[u], (i + 1) * 16 * (QR + 1))
                    e.wait_ge(q_sum, (n + 1) * NN)
                    nc.scalar.activation(whi[:, u], raw[:, u], ACT.Copy).then_inc(hi_done, 1)

                def step(i, u):
                    n = i * 2 + u
                    e.wait_ge(k_t, n + 3)
                    e.wait_ge(scored, n + 1)
                    nc.scalar.activation(kt[:, u], pk[:, u * 128:(u + 1) * 128], ACT.Copy).then_inc(kt_ready, 1)
                    for m in range(NN):
                        e.wait_ge(q_sum, (n + 2) * NN + m + 1)
                        nc.scalar.activation(q[:, m * NW:(m + 1) * NW], pq[:, (m + u) % 2, 0:NW],
                                             ACT.Copy).then_inc(q_ready, 1)

                hi(0, 0)
                with e.Fori(0, LAST) as i:
                    hi(i, 1)
                    step(i, 0)
                    hi(i + 1, 0)
                    step(i, 1)
                hi(LAST, 1)
                step(LAST, 0)
                step(LAST, 1)

            @block.vector
            def _(e):
                v = nc.vector
                nc.vector.sem_inc(lo_done, 2)
                nc.vector.sem_inc(ranked, 1)

                def lo(i, u):
                    e.wait_ge(hi_done, i * 2 + u + 1)
                    v.tensor_tensor(wlo[:, u], raw[:, u], whi[:, u].bitcast(F32), ALU.subtract).then_inc(lo_done, 1)

                def rank(i, u):
                    n = i * 2 + u
                    o = Order(e, self_ok, 5 * NT + 1, n)
                    val = [val16[:, t] for t in range(NT)]
                    ind = [ind16[:, t] for t in range(NT)]
                    wait_apart(e, P, scored, n + 2)
                    for t in range(NT):
                        o.did(v.max(val[t][:, 0:8], scores[t]))
                    wait_apart(e, P, o.sem, o.value())
                    for t in range(NT):
                        o.did(v.max_index(ind[t][:, 0:8], val[t][:, 0:8], scores[t]))
                        o.did(v.match_replace(rest[:, t], val[t][:, 0:8], scores[t], LOWEST))
                    wait_apart(e, P, o.sem, o.value())
                    for t in range(NT):
                        o.did(v.max(val[t][:, 8:16], rest[:, t]))
                    wait_apart(e, P, o.sem, o.value())
                    for t in range(NT):
                        o.did(v.max_index(ind[t][:, 8:16], val[t][:, 8:16], rest[:, t]))
                    o.settle()
                    o.did(v.tensor_copy(sv[:, :, bass.ds(n, 1), :].rearrange("p t a n -> p t (a n)"), val16[:]))
                    o.settle()
                    v.tensor_copy(si[:, :, bass.ds(n, 1), :].rearrange("p t a n -> p t (a n)"), ind16[:]
                                  ).then_inc(ranked, 1)
                    o.close()

                lo(0, 0)
                with e.Fori(0, LAST) as i:
                    lo(i, 1)
                    rank(i, 0)
                    lo(i + 1, 0)
                    rank(i, 1)
                lo(LAST, 1)
                rank(LAST, 0)
                rank(LAST, 1)

            @block.tensor
            def _(e):
                nc.tensor.sem_inc(q_sum, 2 * NN)
                nc.tensor.sem_inc(k_t, 2)
                nc.tensor.sem_inc(scored, 1)
                with e.Fori(0, HP // 2) as i:
                    for u in range(2):
                        n = i * 2 + u
                        e.wait_ge(w_in[u], (i + 1) * 16 * (QR + 1))
                        e.wait_ge(kt_ready, n + 1)
                        nc.tensor.transpose(pk[:, u * 128:(u + 1) * 128], kraw[:, u], P.ident[:]).then_inc(k_t, 1)
                        e.wait_ge(lo_done, n + 3)
                        for m in range(NN):
                            e.wait_ge(q_ready, n * NN + m + 1)
                            cols = slice(m * NW, (m + 1) * NW)
                            for k in range(KC):
                                last = three_passes(nc, pq[:, (m + u) % 2, 0:NW], (whi[:, u, k], wlo[:, u, k]),
                                                    (xhi[:, k, cols], xlo[:, k, cols]), k == 0, k == KC - 1)
                            last.then_inc(q_sum, 1)
                        e.wait_ge(kt_ready, n + 3)
                        e.wait_ge(q_ready, (n + 1) * NN + 2)
                        e.wait_ge(ranked, n + 1)
                        for t in range(NT):
                            last = nc.tensor.matmul(scores[t], q[:, t * 128:(t + 1) * 128], kt[:, u],
                                                    start=True, stop=True)
                        last.then_inc(scored, 1)


SUB = 32
NSUB = T // SUB
QUAD = 4
NQ = SUB // QUAD
G_SCALE = float(2 ** 15)


GRP = 4


class OutputLoads:

    def __init__(self, P, ctx, region, w_dram, act_dram):
        nc, self.w_dram, self.act_dram = P.nc, w_dram, act_dram
        words = GRP * T
        self.wt = [region[:, 0:words].rearrange("p (s j t) -> p s j t", j=GRP, t=SUB)]
        self.at = [region[:, words:2 * words].rearrange("p (j t) -> p j t", j=GRP)]
        self.raw = region[:, 2 * words:2 * words + 2 * D].rearrange("p (u d) -> p u d", u=2)
        self.v_v = P.a["peer_v"][0].rearrange("(i j) d -> i j d", j=NK)
        sem = lambda n: ctx.enter_context(nc.semaphore(f"eo_{n}"))
        self.wa_in = [sem(f"wa_in{u}") for u in range(2)]
        self.v_in = [sem(f"v_in{u}") for u in range(2)]

    def rows(self, e, g, jj):
        e.dma_start(self.raw[:, jj % 2], self.v_v[:, bass.ds(g * GRP + jj, 1)].rearrange("p a d -> p (a d)")
                    ).then_inc(self.v_in[jj % 2], 16)

    def weights(self, e, g, u):
        e.dma_start(self.wt[u].rearrange("p s j t -> p s (j t)"),
                    self.w_dram[:, :, bass.ds(g * GRP, GRP), :].rearrange("p s j t -> p s (j t)")
                    ).then_inc(self.wa_in[u], 16)
        e.dma_start(self.at[u].rearrange("p j t -> p (j t)"),
                    self.act_dram[:, bass.ds(g * GRP, GRP), :].rearrange("p j t -> p (j t)")
                    ).then_inc(self.wa_in[u], 16)

    def first(self, e):
        self.rows(e, 0, 0)
        self.rows(e, 0, 1)
        self.weights(e, 0, 0)


def experts(P, xhi, xlo, sv, si_of, region, act_dram, w_dram, after):
    nc = P.nc
    u_v = P.a["peer_u"][0].rearrange("(e x j) d -> x e j d", e=4, j=NK)
    with ExitStack() as ctx:
        def sb(n, shape, d=F32):
            return ctx.enter_context(nc.sbuf_tensor(f"ea_{n}", shape, d))
        s = lambda n: ctx.enter_context(nc.semaphore(f"ea_{n}"))
        raw = sb("raw", [128, 2, 4, D // QR])
        ut = sb("ut", [128, 4, QC, 32])
        uhi, ulo = sb("uhi", [128, 2, KC, 128], F32R), sb("ulo", [128, 2, KC, 128], F32R)
        stage = sb("stage", [128, 2, T])
        best, at = sb("best", [128, PH, K]), sb("at", [128, PH, K], U32)
        ab = sb("ab", [128, 2, PH * K], U32)
        sif = sb("sif", [128, HP, K])
        rows = sb("rows", [128, 3, PH * K])
        total = sb("total", [128, PH])
        iota = sb("iota", [128, NK], F16)
        iota_u = rows[:, 0].bitcast(I32)
        cand = region[:, 4608:6656].rearrange("p (h a b) -> p h a b", a=K, b=K)
        eq = region[:, 6656:8704].rearrange("p (n a) -> p n a", a=K)
        si = si_of(region)
        picks = sb("picks", [128, 4, T], F16)
        cur = sb("cur", [128, 2, 4, SUB], F16)
        wt = region[:, 0:2 * NK * SUB].rearrange("p (u j t) -> p u j t", u=2, t=SUB)
        RING = 4
        hot = region[:, 8192:8192 + 3072].bitcast(F16).rearrange("p (x r q n) -> p x r q n", x=3, r=RING, q=QUAD)
        pa = ctx.enter_context(nc.psum_tensor("ea_pa", [128, NN, 512], F32))
        pr = ctx.enter_context(nc.psum_tensor("ea_pr", [128, 4, 128], F32))
        pw = ctx.enter_context(nc.psum_tensor("ea_pw", [128, 2, QUAD, NK], F32))
        u_in = [s(f"u_in{u}") for u in range(2)]
        stored = [s(f"stored{u}") for u in range(2)]
        w_out = [s(f"w_out{u}") for u in range(2)]
        u_t, hi_done, lo_done, summed, gelued = map(s, ("u_t", "hi", "lo", "summed", "gelued"))
        made, self_ok, shifted, exped, rows_ready, rows_t, picks_hi, picks_done = map(
            s, ("made", "self", "shifted", "exped", "rows", "rows_t", "picks_hi", "picks_done"))
        cur_ready, onehot_i, onehot_j, w_summed, w_ready = map(s, ("cur", "onehot_i", "onehot_j", "w_summed", "w"))
        A_STEPS = 4
        B0 = NT * A_STEPS // 2
        C0 = B0 + NSUB
        LAST = NK // 2 - 1

        def chunks(x):
            return x.rearrange("p c (e x) -> p e c x", x=32)

        def nxt(p, u):
            return (p, 1) if u == 0 else (p + 1, 0)

        with nc.Block() as block:
            @block.gpsimd
            def _(e):
                nc.gpsimd.iota(iota_u, [[1, NK]], base=0, channel_multiplier=0).then_inc(made, 1)
                e.wait_ge(made, 1)
                nc.gpsimd.tensor_copy(iota[:], iota_u).then_inc(made, 1)
                e.wait_ge(made, 2)
                with e.Fori(0, NSUB // 2) as i:
                    for v in range(2):
                        for q in range(NQ):
                            m = (i * 2 + v) * NQ + q
                            e.wait_ge(cur_ready, i * 2 + v + 1)
                            wait_apart(e, P, w_summed, m + 1)
                            for t in range(QUAD):
                                c = q * QUAD + t
                                last = nc.gpsimd.tensor_scalar(hot[:, 0, q % RING, t], iota[:],
                                                               cur[:, v, 0, c:c + 1], None, ALU.is_equal)
                            last.then_inc(onehot_i, 1)

            @block.sync
            def _(e):
                for u in range(2):
                    nc.sync.sem_inc(stored[u], 16)
                    nc.sync.sem_inc(w_out[u], 16)

                def load(p, u):
                    e.wait_ge(u_t, p * 2 + u + 1)
                    for r in range(QR):
                        src = u_v[:, :, bass.ds(p * 2 + u, 1), r * (D // QR):(r + 1) * (D // QR)]
                        e.dma_start(raw[32 * r:32 * r + 32, u], src.rearrange("x e a d -> x e (a d)")
                                    ).then_inc(u_in[u], 16)

                def store(p, u):
                    e.wait_ge(gelued, (p * 2 + u + 1) * NN + NN)
                    e.dma_start(act_dram[:, bass.ds(p * 2 + u, 1)].rearrange("p a t -> p (a t)"),
                                stage[:, u]).then_inc(stored[u], 16)

                def pair(p, last=False):
                    for u in range(2):
                        now = nxt(p, u)
                        if not (last and u == 1):
                            load(*nxt(*nxt(*now)))
                        store(*now)

                def store_weights(n, v):
                    e.wait_ge(w_ready, (n + 1) * NQ + 2)
                    e.dma_start(w_dram[:, bass.ds(n, 1)].rearrange("p a j t -> p (a j t)"),
                                wt[:, v].rearrange("p j t -> p (j t)")).then_inc(w_out[v], 16)

                load(0, 0)
                load(0, 1)
                load(1, 0)
                store(0, 0)
                with e.Fori(0, B0) as i:
                    pair(i)
                with e.Fori(0, NSUB // 2) as i:
                    for v in range(2):
                        pair(i * 2 + (B0 + v))
                        store_weights(i * 2 + v, v)
                with e.Fori(0, LAST - 1 - C0) as i:
                    pair(i + C0)
                for u in range(2):
                    e.wait_ge(w_out[u], (NSUB // 2 + 1) * 16)
                    e.wait_ge(stored[u], LAST * 16)
                after.first(e)
                pair(LAST - 1, last=True)
                store(LAST, 1)
                for u in range(2):
                    e.wait_ge(stored[u], (NK // 2 + 1) * 16)

            @block.scalar
            def _(e):
                nc.scalar.sem_inc(gelued, NN)
                nc.scalar.sem_inc(w_ready, 2)

                def hi(p, u):
                    e.wait_ge(u_t, p * 2 + u + 3)
                    e.wait_ge(summed, (p * 2 + u + 1) * NN)
                    nc.scalar.activation(chunks(uhi[:, u]), ut[:], ACT.Copy).then_inc(hi_done, 1)

                def gelu(p, u, n):
                    e.wait_ge(stored[u], (p + 1) * 16)
                    e.wait_ge(summed, (p * 2 + u + 2) * NN + n + 1)
                    nc.scalar.activation(stage[:, u, n * NW:(n + 1) * NW], pa[:, n, 0:NW],
                                         ACT.Gelu_apprx_tanh).then_inc(gelued, 1)

                def weights(i, v, q):
                    e.wait_ge(w_out[v], (i + 1) * 16)
                    e.wait_ge(w_summed, (i * 2 + v) * NQ + q + 1 + RING)
                    dst = wt[:, v, :, q * QUAD:(q + 1) * QUAD].rearrange("p j t -> p t j")
                    nc.scalar.activation(dst, pw[:, q % 2], ACT.Copy, scale=1.0 / G_SCALE).then_inc(w_ready, 1)

                hi(0, 0)
                hi(0, 1)
                for n in range(NN):
                    gelu(0, 0, n)
                with e.Fori(0, NT) as i:
                    for st in range(A_STEPS):
                        p, u = nxt(i * 2 + st // 2, st % 2)
                        hi(*nxt(p, u))
                        if st == 2:
                            e.wait_ge(shifted, i + 1)
                            nc.scalar.activation(rows[:, 2], rows[:, 2], ACT.Exp).then_inc(exped, 1)
                        for n in range(NN):
                            gelu(p, u, n)
                    e.wait_ge(rows_t, i + 1)
                    cols = bass.ds(i * 128, 128)
                    for x, scale in ((0, 1.0), (1, 1.0), (2, G_SCALE)):
                        nc.scalar.activation(picks[:, x, cols], pr[:, x], ACT.Copy, scale=scale).then_inc(picks_hi, 1)
                with e.Fori(0, NSUB // 2) as i:
                    for v in range(2):
                        for u in range(2):
                            now = nxt(i * 2 + (B0 + v), u)
                            hi(*nxt(*now))
                            for n in range(NN):
                                gelu(*now, n)
                                weights(i, v, 4 * u + n)
                            weights(i, v, 4 * u + NN)
                with e.Fori(0, LAST - C0) as i:
                    for u in range(2):
                        now = nxt(i + C0, u)
                        hi(*nxt(*now))
                        for n in range(NN):
                            gelu(*now, n)
                for n in range(NN):
                    gelu(LAST, 1, n)

            @block.vector
            def _(e):
                v_ = nc.vector
                nc.vector.sem_inc(lo_done, 1)
                nc.vector.sem_inc(u_t, 2)

                def turn(p, u):
                    e.wait_ge(u_in[u], (p + 1) * 16 * QR)
                    e.wait_ge(lo_done, p * 2 + u + 1)
                    nc.vector.transpose(ut[:].rearrange("p e c x -> p (e c x)"),
                                        raw[:, u].rearrange("p e d -> p (e d)")).then_inc(u_t, 1)

                def lo(p, u):
                    e.wait_ge(hi_done, p * 2 + u + 1)
                    nc.vector.tensor_tensor(chunks(ulo[:, u]), ut[:], chunks(uhi[:, u]).bitcast(F32),
                                            ALU.subtract).then_inc(lo_done, 1)

                def turn_lo(p, u):
                    turn(p, u)
                    lo(p, u)

                PER = 6 * PH + 4
                flat = [cand[:, h].rearrange("p a b -> p (a b)") for h in range(PH)]
                shape = [128, PH, K, K]
                g = rows[:, 2].rearrange("p (h k) -> p h k", k=K)
                sif4 = sif[:].rearrange("p (h x) k -> p h x k", x=2)

                def over_k(x):
                    return x.rearrange("p h (k a) -> p h k a", a=1).broadcast_to(shape)

                def over_a(x):
                    return x.rearrange("p h (a k) -> p h a k", a=1).broadcast_to(shape)

                def best_sums(o, i):
                    one = lambda x: x[:, bass.ds(i, 1)].rearrange("p a n k -> p (a n) k")
                    sv4 = one(sv).rearrange("p (h x) k -> p h x k", x=2)
                    o.did(v_.tensor_tensor(cand, over_k(sv4[:, :, 0, :]), over_a(sv4[:, :, 1, :]), ALU.add))
                    o.did(v_.tensor_copy(sif[:], one(si)))
                    wait_apart(e, P, o.sem, o.value())
                    for h in range(PH):
                        o.did(v_.max(best[:, h, 0:8], flat[h]))
                    wait_apart(e, P, o.sem, o.value())
                    for h in range(PH):
                        o.did(v_.max_index(at[:, h, 0:8], best[:, h, 0:8], flat[h]))
                    wait_apart(e, P, o.sem, o.value())
                    for h in range(PH):
                        o.did(v_.match_replace(flat[h], best[:, h, 0:8], flat[h], LOWEST))

                def next_sums(o, i):
                    wait_apart(e, P, o.sem, o.value())
                    for h in range(PH):
                        o.did(v_.max(best[:, h, 8:16], flat[h]))
                    wait_apart(e, P, o.sem, o.value())
                    for h in range(PH):
                        o.did(v_.max_index(at[:, h, 8:16], best[:, h, 8:16], flat[h]))
                    e.wait_ge(picks_done, i + 1)
                    v_.tensor_tensor(g, best[:], best[:, :, 0:1].broadcast_to([128, PH, K]),
                                     ALU.subtract).then_inc(shifted, 1)
                    o.settle()
                    places = at[:].rearrange("p h k -> p (h k)")
                    o.did(v_.tensor_single_scalar(ab[:, 0], places, 4, ALU.logical_shift_right))
                    o.did(v_.tensor_single_scalar(ab[:, 1], places, K - 1, ALU.bitwise_and))

                def subkey(o, x):
                    o.settle()
                    o.did(v_.tensor_tensor(
                        eq, ab[:, x].rearrange("p (n a) -> p n a", a=1).broadcast_to([128, PH * K, K]),
                        iota[:, 0:K].rearrange("p (a k) -> p a k", a=1).broadcast_to([128, PH * K, K]),
                        ALU.is_equal))
                    o.settle()
                    q4 = eq.rearrange("p (h k) a -> p h k a", k=K)
                    o.did(v_.tensor_tensor(q4, q4, over_a(sif4[:, :, x, :]), ALU.mult))
                    o.settle()
                    o.did(v_.tensor_reduce(rows[:, x], eq, AX.X, ALU.add))

                def softmax(o, i):
                    e.wait_ge(exped, i + 1)
                    o.did(v_.tensor_reduce(total[:], g, AX.X, ALU.add))
                    o.settle()
                    o.did(v_.reciprocal(total[:], total[:]))
                    o.settle()
                    v_.tensor_tensor(g, g, total[:].rearrange("p (h a) -> p h a", a=1).broadcast_to([128, PH, K]),
                                     ALU.mult).then_inc(rows_ready, 1)

                def rest_of_g(i):
                    e.wait_ge(picks_hi, i * 3 + 3)
                    cols = bass.ds(i * 128, 128)
                    v_.scalar_tensor_tensor(out=picks[:, 3, cols], in0=pr[:, 2], scalar=G_SCALE,
                                            in1=picks[:, 2, cols], op0=ALU.mult,
                                            op1=ALU.subtract).then_inc(picks_done, 1)

                def one_hots(n, v, q):
                    e.wait_ge(w_summed, n * NQ + q + 1)
                    r = q % RING
                    for t in range(QUAD):
                        j_, gh, gl = (cur[:, v, x, q * QUAD + t:q * QUAD + t + 1] for x in range(1, 4))
                        v_.tensor_scalar(hot[:, 1, r, t], iota[:], j_, gh, ALU.is_equal, ALU.mult)
                        last = v_.tensor_scalar(hot[:, 2, r, t], iota[:], j_, gl, ALU.is_equal, ALU.mult)
                    last.then_inc(onehot_j, 1)

                turn_lo(0, 0)
                turn_lo(0, 1)
                e.wait_ge(made, 2)
                v_.sem_inc(picks_done, 1)

                def picks_of(o, i):
                    turn_lo(i * 2 + 1, 0)
                    next_sums(o, i)
                    turn_lo(i * 2 + 1, 1)
                    subkey(o, 0)
                    turn_lo(i * 2 + 2, 0)
                    subkey(o, 1)
                    softmax(o, i)
                    turn_lo(i * 2 + 2, 1)

                first = Order(e, self_ok)
                best_sums(first, 0)
                with e.Fori(0, NT - 1) as i:
                    o = Order(e, self_ok, PER, i, first.n)
                    picks_of(o, i)
                    best_sums(o, i + 1)
                    rest_of_g(i)
                    o.close()
                picks_of(Order(e, self_ok, PER, NT - 1, first.n), NT - 1)
                rest_of_g(NT - 1)
                e.wait_ge(picks_done, NT + 1)
                with e.Fori(0, NSUB // 2) as i:
                    for v in range(2):
                        n = i * 2 + v
                        v_.tensor_copy(cur[:, v], picks[:, :, bass.ds(n * SUB, SUB)]).then_inc(cur_ready, 1)
                        e.wait_ge(cur_ready, n + 1)
                        for u in range(2):
                            after = nxt(*nxt(i * 2 + (B0 + v), u))
                            turn(*after)
                            one_hots(n, v, 4 * u)
                            lo(*after)
                            for q in range(4 * u + 1, 4 * u + 4):
                                one_hots(n, v, q)
                with e.Fori(0, LAST - C0) as i:
                    for u in range(2):
                        turn_lo(*nxt(*nxt(i + C0, u)))

            @block.tensor
            def _(e):
                nc.tensor.sem_inc(summed, 2 * NN)
                nc.tensor.sem_inc(w_summed, RING)

                def product(p, u, n):
                    e.wait_ge(lo_done, p * 2 + u + 2)
                    e.wait_ge(gelued, (p * 2 + u) * NN + n + 1)
                    cols = slice(n * NW, (n + 1) * NW)
                    for k in range(KC):
                        last = three_passes(nc, pa[:, n, 0:NW], (uhi[:, u, k], ulo[:, u, k]),
                                            (xhi[:, k, cols], xlo[:, k, cols]), k == 0, k == KC - 1)
                    last.then_inc(summed, 1)

                def weights(n, q):
                    e.wait_ge(onehot_i, n * NQ + q + 1)
                    e.wait_ge(onehot_j, n * NQ + q + 1)
                    e.wait_ge(w_ready, n * NQ + q + 1)
                    r = q % RING
                    for t in range(QUAD):
                        nc.tensor.matmul(pw[:, q % 2, t], hot[:, 0, r, t], hot[:, 1, r, t], start=True, stop=False)
                        last = nc.tensor.matmul(pw[:, q % 2, t], hot[:, 0, r, t], hot[:, 2, r, t],
                                                start=False, stop=True)
                    last.then_inc(w_summed, 1)

                for n in range(NN):
                    product(0, 0, n)
                with e.Fori(0, NT) as i:
                    for st in range(A_STEPS):
                        for n in range(NN):
                            product(*nxt(i * 2 + st // 2, st % 2), n)
                    e.wait_ge(rows_ready, i + 1)
                    for n in range(3):
                        last = nc.tensor.transpose(pr[:, n], rows[:, n], P.ident[:])
                    last.then_inc(rows_t, 1)
                with e.Fori(0, NSUB // 2) as i:
                    for v in range(2):
                        for u in range(2):
                            for n in range(NN):
                                product(*nxt(i * 2 + (B0 + v), u), n)
                                weights(i * 2 + v, 4 * u + n)
                            weights(i * 2 + v, 4 * u + NN)
                with e.Fori(0, LAST - C0) as i:
                    for u in range(2):
                        for n in range(NN):
                            product(*nxt(i + C0, u), n)
                for n in range(NN):
                    product(LAST, 1, n)


def expert_outputs(P, loads):
    nc = P.nc
    NG = NK // GRP
    raw, wa_in, v_in = loads.raw, loads.wa_in, loads.v_in
    with ExitStack() as ctx:
        def sb(n, shape, d=F32):
            return ctx.enter_context(nc.sbuf_tensor(f"eo_{n}", shape, d))
        s = lambda n: ctx.enter_context(nc.semaphore(f"eo_{n}"))
        loads.wt.append(sb("wt", [128, NSUB, GRP, SUB]))
        loads.at.append(sb("at", [128, GRP, T]))
        wt, at = loads.wt, loads.at
        vhi, vlo = sb("vhi", [128, 2, GRP, D], F32R), sb("vlo", [128, 2, GRP, D], F32R)
        prod = sb("prod", [128, 3, GRP, 128])
        phi, plo = sb("phi", [128, 3, GRP, 128], F32R), sb("plo", [128, 3, GRP, 128], F32R)
        po = ctx.enter_context(nc.psum_tensor("eo_ps", [128, 3, D], F32))
        vhi_done, vlo_done, prod_done, phi_done, plo_done, summed, added = map(
            s, ("vhi", "vlo", "prod", "phi", "plo", "summed", "added"))
        PAIRS = NG // 2

        def in_pairs(e, first, body):
            first()
            with e.Fori(0, PAIRS - 1) as i:
                body(i * 2, 0, False)
                body(i * 2 + 1, 1, False)
            body(NG - 2, 0, False)
            body(NG - 1, 1, True)

        V_TILES = {1: 0, 3: 1, 5: 2, 7: 3}

        with nc.Block() as block:
            @block.sync
            def _(e):
                def rows(g, jj):
                    e.wait_ge(vlo_done, g * GRP + jj + 1)
                    loads.rows(e, g, jj)

                def first():
                    rows(0, 2)
                    rows(0, 3)

                def body(g, u, last):
                    if not last:
                        e.wait_ge(prod_done, (g + 1) * NT + NT)
                        loads.weights(e, g + 1, 1 - u)
                        for jj in range(GRP):
                            rows(g + 1, jj)

                in_pairs(e, first, body)

            @block.scalar
            def _(e):
                def v_hi(g, u, jj):
                    e.wait_ge(v_in[jj % 2], (g * 2 + jj // 2 + 1) * 16)
                    e.wait_ge(summed, g * NT + NT)
                    nc.scalar.activation(vhi[:, u, jj], raw[:, jj % 2], ACT.Copy).then_inc(vhi_done, 1)

                def p_hi(g, t):
                    e.wait_ge(prod_done, g * NT + t + 1 + 2 * NT)
                    e.wait_ge(summed, g * NT + t + 2 * NT - 2)
                    nc.scalar.activation(phi[:, t % 3], prod[:, t % 3], ACT.Copy).then_inc(phi_done, 1)

                def first():
                    v_hi(0, 0, 0)
                    v_hi(0, 0, 1)
                    p_hi(0, 0)
                    p_hi(0, 1)
                    v_hi(0, 0, 2)
                    v_hi(0, 0, 3)

                def body(g, u, last):
                    for t in range(NT):
                        if t + 2 < NT or not last:
                            p_hi(g + (t + 2) // NT, (t + 2) % NT)
                        if t in V_TILES and not last:
                            v_hi(g + 1, 1 - u, V_TILES[t])

                in_pairs(e, first, body)

            @block.vector
            def _(e):
                v = nc.vector
                v.sem_inc(vlo_done, 2)
                v.sem_inc(prod_done, 2 * NT)
                v.sem_inc(added, 3)

                def v_lo(g, u, jj):
                    e.wait_ge(vhi_done, g * GRP + jj + 1)
                    v.tensor_tensor(vlo[:, u, jj], raw[:, jj % 2], vhi[:, u, jj].bitcast(F32),
                                    ALU.subtract).then_inc(vlo_done, 1)

                def product(g, u, t):
                    e.wait_ge(wa_in[u], (g // 2) * 32 + 32)
                    e.wait_ge(summed, g * NT + t + 2 * NT - 2)
                    w = wt[u][:, 4 * t:4 * t + 4].rearrange("p s j t -> p j s t")
                    x = at[u][:, :, t * 128:(t + 1) * 128].rearrange("p j (s t) -> p j s t", t=SUB)
                    v.tensor_tensor(prod[:, t % 3].rearrange("p j (s t) -> p j s t", t=SUB), w, x,
                                    ALU.mult).then_inc(prod_done, 1)

                def p_lo(g, t):
                    e.wait_ge(phi_done, g * NT + t + 1)
                    v.tensor_tensor(plo[:, t % 3], prod[:, t % 3], phi[:, t % 3].bitcast(F32),
                                    ALU.subtract).then_inc(plo_done, 1)

                def add(g, t):
                    e.wait_ge(summed, g * NT + t + 1 + 2 * NT)
                    e.wait_ge(added, g * NT + t + 1)
                    v.tensor_tensor(P.h[:, t], po[:, t % 3], P.h[:, t], ALU.add).then_inc(added, 1)

                def first():
                    v_lo(0, 0, 0)
                    v_lo(0, 0, 1)
                    product(0, 0, 0)
                    product(0, 0, 1)
                    p_lo(0, 0)
                    p_lo(0, 1)
                    v_lo(0, 0, 2)
                    v_lo(0, 0, 3)

                def body(g, u, last):
                    for t in range(NT):
                        more = t + 2 < NT or not last
                        ng, nt = g + (t + 2) // NT, (t + 2) % NT
                        nu = u if t + 2 < NT else 1 - u
                        if more:
                            product(ng, nu, nt)
                        if t in V_TILES and not last:
                            v_lo(g + 1, 1 - u, V_TILES[t])
                        if more:
                            p_lo(ng, nt)
                        add(g, t)

                in_pairs(e, first, body)

            @block.tensor
            def _(e):
                nc.tensor.sem_inc(summed, 2 * NT)

                def body(g, u, last):
                    e.wait_ge(vlo_done, g * GRP + GRP + 2)
                    for t in range(NT):
                        e.wait_ge(plo_done, g * NT + t + 1)
                        e.wait_ge(added, g * NT + t + 1)
                        for q in range(2):
                            cols = slice(512 * q, 512 * q + 512)
                            for jj in range(GRP):
                                mm = three_passes(nc, po[:, t % 3, cols], (phi[:, t % 3, jj], plo[:, t % 3, jj]),
                                                  (vhi[:, u, jj, cols], vlo[:, u, jj, cols]),
                                                  jj == 0, jj == GRP - 1)
                        mm.then_inc(summed, 1)

                in_pairs(e, lambda: None, body)


class EmbeddingLoads:
    QW = D // 4

    def __init__(self, P, ctx):
        nc, self.a = P.nc, P.a
        self.PK = self.a["w_ple"].shape[1] // 128
        self.NB = KC + self.PK
        sb = lambda n, shape: ctx.enter_context(nc.sbuf_tensor(f"ie_{n}", shape, F32))
        self.raw = sb("raw", [128, 2, self.NB, self.QW])
        self.ptok = sb("ptok", [128, NT, self.PK * 128])
        self.p_in = ctx.enter_context(nc.semaphore("ie_p_in"))
        self.w_in = [ctx.enter_context(nc.semaphore(f"ie_w_in{u}")) for u in range(2)]

    def p(self, e):
        p_rows, s_rows = token_rows(self.a["p_prompt"][0], self.a["p_sample"][0])
        e.dma_start(self.ptok[:, 0:NPT], p_rows).then_inc(self.p_in, 16)
        e.dma_start(self.ptok[:, NPT], s_rows).then_inc(self.p_in, 16)

    def weights(self, e, q):
        cols = slice(self.QW * q, self.QW * (q + 1))
        for name, of in (("w_ple_gate", slice(0, KC)), ("w_ple", slice(KC, self.NB))):
            w_v = self.a[name][0].rearrange("(k p) c -> p k c", p=128)
            e.dma_start(self.raw[:, q % 2, of], w_v[:, :, cols]).then_inc(self.w_in[q % 2], 16)

    def first(self, e):
        self.p(e)
        self.weights(e, 0)
        self.weights(e, 1)


def input_embedding(P, xhi, xlo, loads):
    nc, a = P.nc, P.a
    PK, NB, QW, raw, ptok, p_in, w_in = (loads.PK, loads.NB, loads.QW, loads.raw, loads.ptok, loads.p_in,
                                         loads.w_in)
    NQT, PER = D // QW, 2
    SPLITS = NB // PER
    ends = {end - 1: (first, i) for i, (first, end) in enumerate(NORM_GROUPS)}
    with ExitStack() as ctx:
        def sb(n, shape, d=F32):
            return ctx.enter_context(nc.sbuf_tensor(f"ie_{n}", shape, d))
        s = lambda n: ctx.enter_context(nc.semaphore(f"ie_{n}"))
        whi, wlo = sb("whi", [128, 2, NB, QW], F32R), sb("wlo", [128, 2, NB, QW], F32R)
        phi, plo = sb("phi", [128, PK, T], F32R), sb("plo", [128, PK, T], F32R)
        gate = sb("gate", [128, 3, QW])
        junk = sb("squares", [128, D])
        stat, rstd = sb("stat", [128, NT]), sb("rstd", [128, NT])
        gbc = sb("gbc", [128, D])
        pt = ctx.enter_context(nc.psum_tensor("ie_pt", [128, 2, 512], F32))
        pg = ctx.enter_context(nc.psum_tensor("ie_pg", [128, 3, 512], F32))
        pp = ctx.enter_context(nc.psum_tensor("ie_pp", [128, 3, 512], F32))
        (gain_in, p_t, phi_done, plo_done, whi_done, wlo_done, summed, gated, mixed, added, squared, meaned, rooted,
         rstd_ready, out_ready, stored) = map(s, (
             "gain_in", "p_t", "phi", "plo", "whi", "wlo", "summed", "gated", "mixed", "added", "squared", "meaned",
             "rooted", "rstd", "out", "stored"))
        with nc.Block() as block:
            @block.sync
            def _(e):
                e.dma_start(gbc[:], a["g_final"].rearrange("(a n) -> a n", a=1).broadcast_to([128, D])
                            ).then_inc(gain_in, 16)
                for q in range(2, NQT):
                    e.wait_ge(wlo_done, (q - 1) * SPLITS)
                    loads.weights(e, q)
                yp, ys = token_rows(P.out["y_p"], P.out["y_s"])
                for t in range(NT):
                    e.wait_ge(out_ready, t + 1)
                    e.dma_start(yp[:, t] if t < NPT else ys, P.h[:, t]).then_inc(stored, 16)
                e.wait_ge(stored, NT * 16)

            @block.scalar
            def _(e):
                def w_hi(q, b):
                    e.wait_ge(w_in[q % 2], (q // 2 + 1) * 32)
                    if q >= 2:
                        e.wait_ge(summed, (q - 1) * NT)
                    of = slice(b * PER, b * PER + PER)
                    nc.scalar.activation(whi[:, q % 2, of], raw[:, q % 2, of], ACT.Copy).then_inc(whi_done, 1)

                for t in range(NT):
                    e.wait_ge(p_t, t + 1)
                    nc.scalar.activation(phi[:, :, t * 128:(t + 1) * 128],
                                         pt[:, t % 2, 0:PK * 128].rearrange("p (k n) -> p k n", k=PK),
                                         ACT.Copy).then_inc(phi_done, 1)
                    if t < SPLITS:
                        w_hi(0, t)
                for q in range(NQT):
                    for t in range(NT):
                        n = q * NT + t
                        if t < SPLITS and q + 1 < NQT:
                            w_hi(q + 1, t)
                        e.wait_ge(summed, n + 1)
                        if n >= 3:
                            e.wait_ge(added, n - 2)
                        nc.scalar.activation(gate[:, n % 3], pg[:, n % 3, 0:QW], ACT.Sigmoid).then_inc(gated, 1)
                        if q == NQT - 1 and t in ends:
                            first, i = ends[t]
                            for x in range(first, t + 1):
                                e.wait_ge(added, (NQT - 1) * NT + x + 1)
                                if x >= 1:
                                    e.wait_ge(squared, x)
                                nc.scalar.activation(junk[:], P.h[:, x], ACT.Square,
                                                     accum_out=stat[:, x:x + 1]).then_inc(squared, 1)
                            e.wait_ge(meaned, i + 1)
                            nc.scalar.activation(rstd[:, first:t + 1], stat[:, first:t + 1],
                                                 ACT.Sqrt).then_inc(rooted, 1)

            @block.vector
            def _(e):
                v = nc.vector

                def w_lo(q, b):
                    e.wait_ge(whi_done, q * SPLITS + b + 1)
                    of = slice(b * PER, b * PER + PER)
                    v.tensor_tensor(wlo[:, q % 2, of], raw[:, q % 2, of], whi[:, q % 2, of].bitcast(F32),
                                    ALU.subtract).then_inc(wlo_done, 1)

                for t in range(NT):
                    e.wait_ge(phi_done, t + 1)
                    cols = slice(t * 128, (t + 1) * 128)
                    v.tensor_tensor(plo[:, :, cols], pt[:, t % 2, 0:PK * 128].rearrange("p (k n) -> p k n", k=PK),
                                    phi[:, :, cols].bitcast(F32), ALU.subtract).then_inc(plo_done, 1)
                    if t < SPLITS:
                        w_lo(0, t)
                for q in range(NQT):
                    cols = slice(QW * q, QW * q + QW)
                    for t in range(NT):
                        n = q * NT + t
                        if t < SPLITS and q + 1 < NQT:
                            w_lo(q + 1, t)
                        e.wait_ge(gated, n + 1)
                        v.tensor_tensor(gate[:, n % 3], pp[:, n % 3, 0:QW], gate[:, n % 3], ALU.mult
                                        ).then_inc(mixed, 1)
                        e.wait_ge(mixed, n + 1)
                        v.tensor_tensor(P.h[:, t, cols], P.h[:, t, cols], gate[:, n % 3], ALU.add).then_inc(added, 1)
                        if q == NQT - 1 and t in ends:
                            first, i = ends[t]
                            of = slice(first, t + 1)
                            e.wait_ge(squared, t + 1)
                            v.tensor_scalar(stat[:, of], stat[:, of], 1.0 / D, EPS, ALU.mult, ALU.add
                                            ).then_inc(meaned, 1)
                            e.wait_ge(rooted, i + 1)
                            v.reciprocal(rstd[:, of], rstd[:, of]).then_inc(rstd_ready, 1)
                            e.wait_ge(rstd_ready, i + 1)
                            e.wait_ge(gain_in, 16)
                            for x in range(first, t + 1):
                                v.scalar_tensor_tensor(out=P.h[:, x], in0=P.h[:, x], scalar=rstd[:, x:x + 1],
                                                       in1=gbc[:], op0=ALU.mult, op1=ALU.mult
                                                       ).then_inc(out_ready, 1)

            @block.tensor
            def _(e):
                e.wait_ge(p_in, 32)
                for t in range(NT):
                    if t >= 2:
                        e.wait_ge(plo_done, t - 1)
                    for k in range(PK):
                        last = nc.tensor.transpose(pt[:, t % 2, k * 128:(k + 1) * 128],
                                                   ptok[:, t, k * 128:(k + 1) * 128], P.ident[:])
                    last.then_inc(p_t, 1)
                e.wait_ge(plo_done, NT)
                for q in range(NQT):
                    e.wait_ge(wlo_done, (q + 1) * SPLITS)
                    for t in range(NT):
                        n = q * NT + t
                        if n >= 3:
                            e.wait_ge(mixed, n - 2)
                        cols = slice(t * 128, (t + 1) * 128)
                        for k in range(KC):
                            three_passes(nc, pg[:, n % 3, 0:QW], (xhi[:, k, cols], xlo[:, k, cols]),
                                         (whi[:, q % 2, k], wlo[:, q % 2, k]), k == 0, k == KC - 1)
                        for k in range(PK):
                            last = three_passes(nc, pp[:, n % 3, 0:QW], (phi[:, k, cols], plo[:, k, cols]),
                                                (whi[:, q % 2, KC + k], wlo[:, q % 2, KC + k]), k == 0, k == PK - 1)
                        last.then_inc(summed, 1)


def build(nc, a, out):
    with ExitStack() as ctx:
        P = Program(nc, a, out, ctx)
        scratch = lambda n, shape: nc.dram_tensor(n, shape, F32, kind="Internal").ap()
        z_dram = scratch("z_scratch", (a["w_in"].shape[2] // 128, 128, T))
        w_dram = scratch("w_scratch", (128, NSUB, NK, SUB))
        act_dram = scratch("act_scratch", (128, NK, T))
        P.channels = ChannelParameters(P)
        load_and_constants(P)

        def split_x(name):
            c = ExitStack()
            return c, *(c.enter_context(nc.sbuf_tensor(f"x{part}_{name}", [128, KC, T], F32R))
                        for part in ("hi", "lo"))

        c, xhi, xlo = split_x("mix")
        with c:
            weights = InputWeights(P, c)
            norm_transpose(P, "mix", a["g_mix"][0], xhi, xlo, beside=weights.first, loading=True)
            project_inputs(P, xhi, xlo, z_dram, weights)
        with nc.sbuf_tensor("cat", [128, KC, T], F32) as cat:
            mixers(P, z_dram, cat)
            output_projection(P, cat)
        with nc.sbuf_tensor("region", [128, 2 * GRP * T + 2 * D], F32) as region:
            loads = OutputLoads(P, ctx, region, w_dram, act_dram)
            c, xhi, xlo = split_x("ffn")
            with c:
                words = NT * HP * K
                sv = region[:, 0:words].rearrange("p (t n k) -> p t n k", n=HP, k=K)

                def si_of(r):
                    return r[:, words:2 * words].bitcast(U32).rearrange("p (t n k) -> p t n k", n=HP, k=K)

                keys = RouteLoads(P, c)
                norm_transpose(P, "ffn", a["g_ffn"][0], xhi, xlo, blocks=True, beside=keys.first)
                route_scores(P, xhi, xlo, sv, si_of(region), keys)
                keys.free()
                experts(P, xhi, xlo, sv, si_of, region, act_dram, w_dram, loads)
            expert_outputs(P, loads)
        c, xhi, xlo = split_x("ple")
        with c:
            loads = EmbeddingLoads(P, c)
            norm_transpose(P, "ple", a["g_ple"][0], xhi, xlo, beside=loads.first)
            input_embedding(P, xhi, xlo, loads)


_INS = ("x_prompt", "x_sample", "state_hgrn", "state_rglru", "state_conv", "p_prompt", "p_sample", "g_mix", "w_in",
        "lower_bounds", "g_hgrn_norm", "conv_w", "conv_b", "w_rg_a", "b_rg_a", "w_rg_x", "b_rg_x", "lambda_rg",
        "w_out", "g_ffn", "w_peer_q", "peer_keys", "peer_u", "peer_v", "g_ple", "w_ple_gate", "w_ple", "g_final")
_OUTS = (("y_p", (1, SEQ, D)), ("y_s", (DB, DS, D)), ("hgrn_p", (1, 1, HA, 128, 128)), ("rglru_p", (1, 1, 512)),
         ("conv_p", (1, 1, 3, 512)), ("hgrn_s", (1, DB, HA, 128, 128)), ("rglru_s", (1, DB, 512)),
         ("conv_s", (1, DB, 3, 512)))


def kernel(**inputs):
    import concourse.bacc as bacc
    from concourse.bass_utils import run_bass_kernel_spmd

    nc = bacc.Bacc("TRN2", target_bir_lowering=False, num_devices=1)
    arrays, a, out = {}, {}, {}
    for name in _INS:
        x = np.ascontiguousarray(inputs[name])
        arrays[f"in_{name}"] = x
        a[name] = nc.dram_tensor(f"in_{name}", x.shape, mybir.dt.from_np(x.dtype), kind="ExternalInput").ap()
    for name, shape in _OUTS:
        out[name] = nc.dram_tensor(f"out_{name}", shape, F32, kind="ExternalOutput").ap()
    build(nc, a, out)
    r = run_bass_kernel_spmd(nc, [arrays], core_ids=[0])
    return tuple(r.results[0][f"out_{name}"] for name, _ in _OUTS)
```
